# Optimizing a Trainium2 kernel written in Bass

```python
import math
import jax, jax.numpy as jnp
from jax import lax
import numpy as np

D_MODEL = 1024
BATCH = 1
SEQ = 256
DEPTH = 2

N_META = 16
N_A_LAYERS = DEPTH // 2
N_B_LAYERS = DEPTH - N_A_LAYERS
POOL_WINDOWS = (2, 4, 8, 16)
N_POOL_GROUPS = len(POOL_WINDOWS)
POOL_GROUP_DIM = D_MODEL // N_POOL_GROUPS
HEAD_DIM = 64
N_Q_HEADS = D_MODEL // HEAD_DIM
N_KV_HEADS = max(1, N_Q_HEADS // 8)
GROUP = N_Q_HEADS // N_KV_HEADS
ATTN_DIM = N_Q_HEADS * HEAD_DIM
KV_DIM = N_KV_HEADS * HEAD_DIM
WINDOW = 128
BLOCK = 128
N_BUCKETS = 32
MAX_DISTANCE = 128
D_FF = (((8 * D_MODEL + 2) // 3 + 255) // 256) * 256
EPS = 1e-6
PAD_FRONT = (-N_META) % BLOCK


def rms_norm(x, g):
    xf = x.astype(jnp.float32)
    y = xf * lax.rsqrt(jnp.mean(xf * xf, axis=-1, keepdims=True) + EPS)
    return (y * g.astype(jnp.float32)).astype(x.dtype)

def swiglu(h, w_gate_up, w_down):
    gu = h @ w_gate_up
    gate, up = jnp.split(gu, 2, axis=-1)
    return (jax.nn.silu(gate) * up) @ w_down

def pool_mixer(h, w_groups, scale):
    B, L, _ = h.shape
    hg = h.astype(jnp.float32).reshape(B, L, N_POOL_GROUPS, POOL_GROUP_DIM)
    cs = jnp.cumsum(hg, axis=1)
    pos = jnp.arange(1, L + 1, dtype=jnp.float32)
    outs = []
    for gi, w in enumerate(POOL_WINDOWS):
        c = cs[:, :, gi]
        lag = jnp.pad(c, ((0, 0), (w, 0), (0, 0)))[:, :L]
        cnt = jnp.minimum(pos, float(w))[None, :, None]
        outs.append((c - lag) / cnt - hg[:, :, gi])
    p = jnp.stack(outs, axis=2).astype(h.dtype)
    y = jnp.einsum('blgc,gcd->blgd', p, w_groups).reshape(B, L, D_MODEL)
    return y * scale

def t5_bucket(d):
    max_exact = N_BUCKETS // 2
    df = jnp.maximum(d, 1).astype(jnp.float32)
    large = max_exact + (jnp.log(df / max_exact) / math.log(MAX_DISTANCE / max_exact)
                         * (N_BUCKETS - max_exact)).astype(jnp.int32)
    large = jnp.minimum(large, N_BUCKETS - 1)
    return jnp.where(d < max_exact, d, large)

def band_bias_and_mask(rel_bias, n_blocks):
    q = jnp.arange(BLOCK)[:, None]
    s = jnp.arange(2 * BLOCK)[None, :]
    d = q + BLOCK - s
    in_window = (d >= 0) & (d < WINDOW)
    bias = rel_bias[t5_bucket(jnp.maximum(d, 0))]
    bias = jnp.transpose(bias, (2, 0, 1)).astype(jnp.float32)
    key_pos = jnp.arange(n_blocks)[:, None] * BLOCK + s - BLOCK
    valid = in_window[None] & (key_pos >= PAD_FRONT)[:, None, :]
    return bias, valid

def to_blocks_with_prev(t):
    B, L = t.shape[:2]
    nb = (L + PAD_FRONT) // BLOCK
    t = jnp.pad(t, ((0, 0), (PAD_FRONT + BLOCK, 0), (0, 0), (0, 0)))
    t = t.reshape(B, nb + 1, BLOCK, t.shape[2], t.shape[3])
    return jnp.concatenate([t[:, :-1], t[:, 1:]], axis=2)

def sliding_window_attention(h, k_blk, v_blk, w_q, b_q, w_o, b_o, sinks, bias, valid):
    B, L, _ = h.shape
    q = (h @ w_q + b_q).reshape(B, L, N_KV_HEADS, GROUP, HEAD_DIM)
    q = jnp.pad(q, ((0, 0), (PAD_FRONT, 0), (0, 0), (0, 0), (0, 0)))
    nb = q.shape[1] // BLOCK
    q = q.reshape(B, nb, BLOCK, N_KV_HEADS, GROUP, HEAD_DIM)
    logits = jnp.einsum('bnqhgd,bnshd->bhgnqs', q, k_blk,
                        preferred_element_type=jnp.float32) * (HEAD_DIM ** -0.5)
    logits = logits + bias.reshape(N_KV_HEADS, GROUP, 1, BLOCK, 2 * BLOCK)
    logits = jnp.where(valid, logits, -jnp.inf)
    sink = sinks.astype(jnp.float32).reshape(N_KV_HEADS, GROUP, 1, 1, 1)
    m = jnp.maximum(logits.max(axis=-1, keepdims=True), sink)
    p = jnp.exp(logits - m)
    denom = p.sum(axis=-1, keepdims=True) + jnp.exp(sink - m)
    probs = (p / denom).astype(v_blk.dtype)
    o = jnp.einsum('bhgnqs,bnshd->bnqhgd', probs, v_blk)
    o = o.reshape(B, nb * BLOCK, ATTN_DIM)[:, PAD_FRONT:]
    return o @ w_o + b_o

def first_inputs(seed: int = 0) -> dict:
    key = jax.random.key(seed)
    ks = jax.random.split(key, 24)
    f32 = jnp.float32

    def nrm(k, shape, scale):
        return jax.random.normal(k, shape, f32) * scale

    def gain(k, shape):
        return jnp.ones(shape, f32) + 0.05 * jax.random.normal(k, shape, f32)

    return {
        "x": nrm(ks[0], (BATCH, SEQ, D_MODEL), 1.0),
        "meta_tokens": nrm(ks[1], (N_META, D_MODEL), 1.0),
        "norm_mix_pre": gain(ks[2], (DEPTH, D_MODEL)),
        "norm_mix_post": gain(ks[3], (DEPTH, D_MODEL)),
        "norm_ffn_pre": gain(ks[4], (DEPTH, D_MODEL)),
        "norm_ffn_post": gain(ks[5], (DEPTH, D_MODEL)),
        "pool_w": nrm(ks[6], (N_A_LAYERS, N_POOL_GROUPS, POOL_GROUP_DIM, POOL_GROUP_DIM), POOL_GROUP_DIM ** -0.5),
        "pool_scale": gain(ks[7], (N_A_LAYERS, D_MODEL)) + 0.05 * jax.random.normal(ks[8], (N_A_LAYERS, D_MODEL), f32),
        "kv_norm": gain(ks[9], (D_MODEL,)),
        "w_k": nrm(ks[10], (D_MODEL, KV_DIM), D_MODEL ** -0.5),
        "b_k": nrm(ks[11], (KV_DIM,), 0.02),
        "w_v": nrm(ks[12], (D_MODEL, KV_DIM), D_MODEL ** -0.5),
        "b_v": nrm(ks[13], (KV_DIM,), 0.02),
        "w_q": nrm(ks[14], (N_B_LAYERS, D_MODEL, ATTN_DIM), D_MODEL ** -0.5),
        "b_q": nrm(ks[15], (N_B_LAYERS, ATTN_DIM), 0.02),
        "w_o": nrm(ks[16], (N_B_LAYERS, ATTN_DIM, D_MODEL), ATTN_DIM ** -0.5),
        "b_o": nrm(ks[17], (N_B_LAYERS, D_MODEL), 0.02),
        "sinks": nrm(ks[18], (N_B_LAYERS, N_Q_HEADS), 0.5),
        "rel_bias": nrm(ks[19], (N_BUCKETS, N_Q_HEADS), 0.3),
        "w_gate_up": nrm(ks[20], (DEPTH, D_MODEL, 2 * D_FF), D_MODEL ** -0.5),
        "w_down": nrm(ks[21], (DEPTH, D_FF, D_MODEL), D_FF ** -0.5),
    }

def first_block(x, meta_tokens, norm_mix_pre, norm_mix_post, norm_ffn_pre, norm_ffn_post,
              pool_w, pool_scale, kv_norm, w_k, b_k, w_v, b_v, w_q, b_q, w_o, b_o,
              sinks, rel_bias, w_gate_up, w_down):
    B = x.shape[0]
    meta = jnp.broadcast_to(meta_tokens[None].astype(x.dtype), (B, N_META, D_MODEL))
    hs = jnp.concatenate([meta, x], axis=1)
    L = hs.shape[1]
    n_blocks = (L + PAD_FRONT) // BLOCK
    bias, valid = band_bias_and_mask(rel_bias, n_blocks)
    k_blk = None
    v_blk = None
    for layer in range(DEPTH):
        h = rms_norm(hs, norm_mix_pre[layer])
        if layer < N_A_LAYERS:
            mix = pool_mixer(h, pool_w[layer], pool_scale[layer])
        else:
            j = layer - N_A_LAYERS
            mix = sliding_window_attention(h, k_blk, v_blk, w_q[j], b_q[j], w_o[j], b_o[j],
                                           sinks[j], bias, valid)
        hs = hs + rms_norm(mix, norm_mix_post[layer])
        h = rms_norm(hs, norm_ffn_pre[layer])
        hs = hs + rms_norm(swiglu(h, w_gate_up[layer], w_down[layer]), norm_ffn_post[layer])
        if layer == N_A_LAYERS - 1:
            kv_in = rms_norm(hs, kv_norm)
            k = (kv_in @ w_k + b_k).reshape(B, L, N_KV_HEADS, HEAD_DIM)
            v = (kv_in @ w_v + b_v).reshape(B, L, N_KV_HEADS, HEAD_DIM)
            k_blk = to_blocks_with_prev(k)
            v_blk = to_blocks_with_prev(v)
    return hs[:, N_META:]


DEPTH_2 = 1

CHUNK = 64
P_DIM = 256
SB_HEAD_DIM = 64
SB_WIDTH = 3 * D_MODEL // 8
SB_HEADS = SB_WIDTH // SB_HEAD_DIM
SB_QBLOCK = 128
ML_HEADS = 4
ML_WIDTH = 3 * D_MODEL // 8
ML_HEAD_DIM = ML_WIDTH // ML_HEADS
CONV_K = 4
SGU_WIDTH = D_MODEL - SB_WIDTH - ML_WIDTH
SGU_GROUPS = 4
SGU_GROUP_DIM = SGU_WIDTH // SGU_GROUPS
SGU_BLOCK = 128
IN_SPLITS = (SB_WIDTH, SB_WIDTH, SB_WIDTH, ML_WIDTH, ML_WIDTH, ML_WIDTH, ML_WIDTH, ML_HEADS, ML_HEADS, SGU_WIDTH, SGU_WIDTH)
N_IN = 3 * SB_WIDTH + 4 * ML_WIDTH + 2 * ML_HEADS + 2 * SGU_WIDTH
N_GROUPS = 4
EXPERTS_PER_GROUP = 8
N_EXPERTS = N_GROUPS * EXPERTS_PER_GROUP
TOP_K = 2
D_EXPERT = D_MODEL // 4
MOE_BLOCK = 512


F32 = jnp.float32

def rms_norm_2(x, g):
    x32 = x.astype(F32)
    return x32 * lax.rsqrt(jnp.mean(x32 * x32, axis=-1, keepdims=True) + EPS) * g.astype(F32)

def split_cols(z, sizes):
    idx = np.cumsum(sizes)[:-1].tolist()
    return jnp.split(z, idx, axis=-1)

def causal_depthwise_conv(x, w, b):
    y = lax.conv_general_dilated(x.astype(F32), w.astype(F32)[:, None, :], window_strides=(1,),
                                 padding=[(CONV_K - 1, 0)], dimension_numbers=('NWC', 'WIO', 'NWC'),
                                 feature_group_count=x.shape[-1])
    return y + b.astype(F32)

def stick_breaking_attention(q, k, v):
    S = q.shape[1]
    scale = q.shape[-1] ** -0.5
    outs = []
    for n in range(S // SB_QBLOCK):
        t0 = n * SB_QBLOCK
        kend = t0 + SB_QBLOCK
        z = jnp.einsum('bthd,bshd->bhts', q[:, t0:kend], k[:, :kend]) * scale
        tpos = t0 + jnp.arange(SB_QBLOCK)
        spos = jnp.arange(kend)
        mask = spos[None, :] < tpos[:, None]
        log_1m = jnp.where(mask, -jax.nn.softplus(z), 0.0)
        after = lax.cumsum(log_1m, axis=3, reverse=True) - log_1m
        a = jnp.where(mask, jnp.exp(jax.nn.log_sigmoid(z) + after), 0.0)
        outs.append(jnp.einsum('bhts,bshd->bthd', a, v[:, :kend]))
    return jnp.concatenate(outs, axis=1)

def mlstm_chunkwise(q, k, v, i_pre, f_pre):
    Bn, S, H, d = q.shape
    N, L = S // CHUNK, CHUNK
    q = q.reshape(Bn, N, L, H, d)
    k = k.reshape(Bn, N, L, H, d) * (d ** -0.5)
    v = v.reshape(Bn, N, L, H, d)
    ig = i_pre.reshape(Bn, N, L, H)
    bcum = jnp.cumsum(jax.nn.log_sigmoid(f_pre.reshape(Bn, N, L, H)), axis=2)
    btot = bcum[:, :, -1]
    a = btot[:, :, None] - bcum + ig

    def step(carry, xs):
        c, nvec, m = carry
        k_c, v_c, a_c, bt_c = xs
        m_new = jnp.maximum(bt_c + m, a_c.max(axis=1))
        decay = jnp.exp(bt_c + m - m_new)
        w = jnp.exp(a_c - m_new[:, None])
        c_new = decay[..., None, None] * c + jnp.einsum('blh,blhd,blhe->bhde', w, k_c, v_c)
        n_new = decay[..., None] * nvec + jnp.einsum('blh,blhd->bhd', w, k_c)
        return (c_new, n_new, m_new), (c, nvec, m)

    init = (jnp.zeros((Bn, H, d, d), F32), jnp.zeros((Bn, H, d), F32), jnp.zeros((Bn, H), F32))
    xs = (jnp.moveaxis(k, 1, 0), jnp.moveaxis(v, 1, 0), jnp.moveaxis(a, 1, 0), jnp.moveaxis(btot, 1, 0))
    _, (c_in, n_in, m_in) = lax.scan(step, init, xs)
    c_in = jnp.moveaxis(c_in, 0, 1)
    n_in = jnp.moveaxis(n_in, 0, 1)
    m_in = jnp.moveaxis(m_in, 0, 1)

    bT = jnp.moveaxis(bcum, 2, -1)
    igT = jnp.moveaxis(ig, 2, -1)
    causal = jnp.tril(jnp.ones((L, L), dtype=bool))
    dmat = jnp.where(causal, bT[..., :, None] - bT[..., None, :] + igT[..., None, :], -jnp.inf)
    m_inter = bT + m_in[..., None]
    m_t = jnp.maximum(m_inter, dmat.max(axis=-1))
    wd = jnp.where(causal, jnp.exp(dmat - m_t[..., None]), 0.0)
    s = jnp.einsum('bnthd,bnshd->bnhts', q, k) * wd
    inter = jnp.exp(m_inter - m_t)
    num = jnp.einsum('bnhts,bnshd->bnthd', s, v) + jnp.einsum('bnhl,bnlhd,bnhde->bnlhe', inter, q, c_in)
    den = s.sum(axis=-1) + inter * jnp.einsum('bnlhd,bnhd->bnhl', q, n_in)
    den = jnp.maximum(jnp.abs(den), jnp.exp(-m_t))
    h = num / jnp.moveaxis(den, 2, -1)[..., None]
    return h.reshape(Bn, S, H, d)

def spatial_gating(u, v, ln_g, ln_b, w_s, b_s):
    Bn, S, _ = u.shape
    v = v.reshape(Bn, S, SGU_GROUPS, SGU_GROUP_DIM)
    mu = v.mean(axis=-1, keepdims=True)
    var = jnp.mean(jnp.square(v - mu), axis=-1, keepdims=True)
    v = (v - mu) * lax.rsqrt(var + EPS) * ln_g.reshape(SGU_GROUPS, SGU_GROUP_DIM) + ln_b.reshape(SGU_GROUPS, SGU_GROUP_DIM)
    v = v.reshape(Bn, S // SGU_BLOCK, SGU_BLOCK, SGU_GROUPS, SGU_GROUP_DIM)
    cpos = jnp.arange(SGU_BLOCK) // CHUNK
    mask = cpos[None, :] <= cpos[:, None]
    w = jnp.where(mask[None], w_s.astype(F32), 0.0)
    mixed = jnp.einsum('gts,bnsgc->bntgc', w, v) + b_s.astype(F32).T[:, :, None]
    return u * mixed.reshape(Bn, S, SGU_WIDTH)

def routed_experts(xt, e_idx, e_w, w_gate, w_up, w_down):
    T, D = xt.shape
    M = T * TOP_K
    flat_e = e_idx.reshape(M)
    order = jnp.argsort(flat_e)
    sorted_e = flat_e[order]
    sorted_tok = order // TOP_K
    sorted_w = e_w.reshape(M)[order]
    sizes = jnp.bincount(flat_e, length=N_EXPERTS)
    padded = (sizes + MOE_BLOCK - 1) // MOE_BLOCK * MOE_BLOCK
    start = jnp.cumsum(sizes) - sizes
    pend = jnp.cumsum(padded)
    pstart = pend - padded
    dest = pstart[sorted_e] + jnp.arange(M) - start[sorted_e]
    n_blocks = -(-(M + N_EXPERTS * (MOE_BLOCK - 1)) // MOE_BLOCK)
    rows = n_blocks * MOE_BLOCK
    row_tok = jnp.zeros((rows,), jnp.int32).at[dest].set(sorted_tok.astype(jnp.int32))
    row_w = jnp.zeros((rows,), F32).at[dest].set(sorted_w)
    block_e = jnp.minimum(jnp.searchsorted(pend, jnp.arange(n_blocks) * MOE_BLOCK, side='right'), N_EXPERTS - 1)

    def block_ffn(args):
        tok, wt, e = args
        xb = xt[tok]
        hb = jax.nn.silu(xb @ w_gate[e]) * (xb @ w_up[e])
        return (hb @ w_down[e]).astype(F32) * wt[:, None]

    yb = lax.map(block_ffn, (row_tok.reshape(n_blocks, MOE_BLOCK), row_w.reshape(n_blocks, MOE_BLOCK), block_e))
    return jnp.zeros((T, D), F32).at[row_tok].add(yb.reshape(rows, D))

def hierarchical_moe(h, rg_w, rg_b, re_w, re_b, w_gate, w_up, w_down):
    Bn, S, D = h.shape
    xt = h.reshape(Bn * S, D)
    g_logits = (xt @ rg_w + rg_b).astype(F32)
    g_prob = jax.nn.softmax(g_logits, axis=-1)
    g_top = jnp.argmax(g_logits, axis=-1)
    g_w = jnp.take_along_axis(g_prob, g_top[:, None], axis=-1)[:, 0]
    e_logits = (xt @ re_w + re_b).astype(F32).reshape(-1, N_GROUPS, EXPERTS_PER_GROUP)
    e_in = jnp.take_along_axis(e_logits, g_top[:, None, None], axis=1)[:, 0]
    e_val, e_loc = lax.top_k(e_in, TOP_K)
    e_w = jax.nn.softmax(e_val, axis=-1) * g_w[:, None]
    e_idx = g_top[:, None].astype(jnp.int32) * EXPERTS_PER_GROUP + e_loc.astype(jnp.int32)
    y = routed_experts(xt, e_idx, e_w, w_gate, w_up, w_down)
    return y.reshape(Bn, S, D)

def second_inputs(seed: int = 0) -> dict:
    key = jax.random.key(seed)
    ks = jax.random.split(key, 32)

    def nrm(k, shape, scale):
        return jax.random.normal(k, shape, F32) * scale

    def gain(k, shape):
        return 1.0 + 0.05 * jax.random.normal(k, shape, F32)

    D = D_MODEL
    return {
        "x": nrm(ks[0], (BATCH, SEQ, D), 1.0),
        "p": nrm(ks[1], (DEPTH_2, BATCH, SEQ, P_DIM), 1.0),
        "norm1_g": gain(ks[2], (DEPTH_2, D)),
        "w_in": nrm(ks[3], (DEPTH_2, D, N_IN), D ** -0.5),
        "conv_w": nrm(ks[4], (DEPTH_2, CONV_K, 2 * ML_WIDTH), CONV_K ** -0.5),
        "conv_b": nrm(ks[5], (DEPTH_2, 2 * ML_WIDTH), 0.01),
        "igate_b": nrm(ks[6], (DEPTH_2, ML_HEADS), 0.1),
        "fgate_b": jnp.linspace(3.0, 6.0, ML_HEADS, dtype=F32)[None, :] + nrm(ks[7], (DEPTH_2, ML_HEADS), 0.1),
        "mnorm_g": gain(ks[8], (DEPTH_2, ML_WIDTH)),
        "sb_out_g": gain(ks[9], (DEPTH_2, SB_WIDTH)),
        "sgu_ln_g": gain(ks[10], (DEPTH_2, SGU_WIDTH)),
        "sgu_ln_b": nrm(ks[11], (DEPTH_2, SGU_WIDTH), 0.01),
        "sgu_w": nrm(ks[12], (DEPTH_2, SGU_GROUPS, SGU_BLOCK, SGU_BLOCK), SGU_BLOCK ** -0.5),
        "sgu_b": gain(ks[13], (DEPTH_2, SGU_GROUPS, SGU_BLOCK)),
        "sgu_out_g": gain(ks[14], (DEPTH_2, SGU_WIDTH)),
        "w_out": nrm(ks[15], (DEPTH_2, D, D), D ** -0.5),
        "norm2_g": gain(ks[16], (DEPTH_2, D)),
        "router_gw": nrm(ks[17], (DEPTH_2, D, N_GROUPS), D ** -0.5),
        "router_gb": nrm(ks[18], (DEPTH_2, N_GROUPS), 0.01),
        "router_ew": nrm(ks[19], (DEPTH_2, D, N_EXPERTS), D ** -0.5),
        "router_eb": nrm(ks[20], (DEPTH_2, N_EXPERTS), 0.01),
        "w_gate": nrm(ks[21], (DEPTH_2, N_EXPERTS, D, D_EXPERT), D ** -0.5),
        "w_up": nrm(ks[22], (DEPTH_2, N_EXPERTS, D, D_EXPERT), D ** -0.5),
        "w_down": nrm(ks[23], (DEPTH_2, N_EXPERTS, D_EXPERT, D), D_EXPERT ** -0.5),
        "ple_norm_g": gain(ks[24], (DEPTH_2, D)),
        "ple_gate_w": nrm(ks[25], (DEPTH_2, D, D), D ** -0.5),
        "ple_proj_w": nrm(ks[26], (DEPTH_2, P_DIM, D), P_DIM ** -0.5),
        "final_g": gain(ks[27], (D,)),
    }

def second_block(x, p, norm1_g, w_in, conv_w, conv_b, igate_b, fgate_b, mnorm_g, sb_out_g,
              sgu_ln_g, sgu_ln_b, sgu_w, sgu_b, sgu_out_g, w_out, norm2_g,
              router_gw, router_gb, router_ew, router_eb, w_gate, w_up, w_down,
              ple_norm_g, ple_gate_w, ple_proj_w, final_g):
    Bn, S, D = x.shape
    h = x.astype(F32)
    for i in range(DEPTH_2):
        hn = rms_norm_2(h, norm1_g[i])
        z = hn @ w_in[i]
        qa, ka, va, qb, kb, vb, ob, ib, fb, uc, vc = split_cols(z, IN_SPLITS)
        ya = stick_breaking_attention(qa.reshape(Bn, S, SB_HEADS, SB_HEAD_DIM),
                                      ka.reshape(Bn, S, SB_HEADS, SB_HEAD_DIM),
                                      va.reshape(Bn, S, SB_HEADS, SB_HEAD_DIM)).reshape(Bn, S, SB_WIDTH)
        ya = rms_norm_2(ya, sb_out_g[i])
        qk = jax.nn.silu(causal_depthwise_conv(jnp.concatenate([qb, kb], axis=-1), conv_w[i], conv_b[i]))
        qb, kb = jnp.split(qk, 2, axis=-1)
        hb = mlstm_chunkwise(qb.reshape(Bn, S, ML_HEADS, ML_HEAD_DIM),
                             kb.reshape(Bn, S, ML_HEADS, ML_HEAD_DIM),
                             vb.astype(F32).reshape(Bn, S, ML_HEADS, ML_HEAD_DIM),
                             ib + igate_b[i], fb + fgate_b[i])
        hb = rms_norm_2(hb, mnorm_g[i].reshape(ML_HEADS, ML_HEAD_DIM)).reshape(Bn, S, ML_WIDTH)
        yb = hb * jax.nn.sigmoid(ob)
        yc = spatial_gating(jax.nn.gelu(uc), jax.nn.gelu(vc), sgu_ln_g[i], sgu_ln_b[i], sgu_w[i], sgu_b[i])
        yc = rms_norm_2(yc, sgu_out_g[i])
        h = h + jnp.concatenate([ya, yb, yc], axis=-1) @ w_out[i]
        h = h + hierarchical_moe(rms_norm_2(h, norm2_g[i]), router_gw[i], router_gb[i], router_ew[i], router_eb[i],
                                 w_gate[i], w_up[i], w_down[i])
        gate = jax.nn.sigmoid(rms_norm_2(h, ple_norm_g[i]) @ ple_gate_w[i])
        h = h + gate * (p[i] @ ple_proj_w[i]).astype(F32)
    return rms_norm_2(h, final_g).astype(x.dtype)


def setup_inputs(seed=0):
    out = dict(first_inputs(seed))
    for name, value in second_inputs(seed + 1).items():
        if name != "x":
            out[name + "_2"] = value
    return out


def reference(
    x, meta_tokens, norm_mix_pre, norm_mix_post, norm_ffn_pre, norm_ffn_post, pool_w,
    pool_scale, kv_norm, w_k, b_k, w_v, b_v, w_q, b_q, w_o, b_o, sinks, rel_bias, w_gate_up,
    w_down, p_2, norm1_g_2, w_in_2, conv_w_2, conv_b_2, igate_b_2, fgate_b_2, mnorm_g_2,
    sb_out_g_2, sgu_ln_g_2, sgu_ln_b_2, sgu_w_2, sgu_b_2, sgu_out_g_2, w_out_2, norm2_g_2,
    router_gw_2, router_gb_2, router_ew_2, router_eb_2, w_gate_2, w_up_2, w_down_2,
    ple_norm_g_2, ple_gate_w_2, ple_proj_w_2, final_g_2,
):
    x = first_block(
        x, meta_tokens, norm_mix_pre, norm_mix_post, norm_ffn_pre, norm_ffn_post, pool_w,
        pool_scale, kv_norm, w_k, b_k, w_v, b_v, w_q, b_q, w_o, b_o, sinks, rel_bias, w_gate_up,
        w_down,
    )
    return second_block(
        x, p_2, norm1_g_2, w_in_2, conv_w_2, conv_b_2, igate_b_2, fgate_b_2, mnorm_g_2,
        sb_out_g_2, sgu_ln_g_2, sgu_ln_b_2, sgu_w_2, sgu_b_2, sgu_out_g_2, w_out_2, norm2_g_2,
        router_gw_2, router_gb_2, router_ew_2, router_eb_2, w_gate_2, w_up_2, w_down_2,
        ple_norm_g_2, ple_gate_w_2, ple_proj_w_2, final_g_2,
    )


_drawn_inputs = setup_inputs


def setup_inputs(seed=0):
    import zlib

    import numpy as np

    out = dict(_drawn_inputs(seed))
    spreads = {}
    factors = {'b_k': 8.0,
     'b_q': 3.921,
     'sinks': 8.0,
     'conv_b_2': 8.0,
     'igate_b_2': 64.0,
     'mnorm_g_2': 5.521,
     'sb_out_g_2': 3.532,
     'sgu_ln_g_2': 4.418,
     'sgu_ln_b_2': 21.963,
     'sgu_b_2': 5.511,
     'sgu_out_g_2': 4.475,
     'norm2_g_2': 2.727,
     'router_gb_2': 5.296,
     'router_eb_2': 8.0,
     'ple_norm_g_2': 64.0}
    for name, (base, spread) in spreads.items():
        noise = np.random.default_rng([zlib.crc32(name.encode()), seed]).standard_normal(out[name].shape)
        drawn = base * np.exp(spread * noise) if base else spread * noise
        out[name] = __import__('jax').numpy.asarray(drawn.astype(out[name].dtype))
    for name, factor in factors.items():
        out[name] = (out[name] * factor).astype(out[name].dtype)
    return out
```

```python
import numpy as np
import concourse.bass as bass
from concourse import mybir
from contextlib import ExitStack

F32 = mybir.dt.float32
F32R = mybir.dt.float32r
I32 = mybir.dt.int32
ACT = mybir.ActivationFunctionType
ALU = mybir.AluOpType
AX = mybir.AxisListType

P = 128
D = 1024
KD = D // P
N_META = 16
SEQ = 256
T = N_META + SEQ
NB = SEQ // P
FF = 2816
NF = FF // P
WINDOWS = (2, 4, 8, 16)
PADT = max(WINDOWS)
NH = 16
HD = 64
HEADS_PER_GROUP = 4
EPS = 1e-6
NEG = -1e30
SB_H = 6
SB_W = SB_H * HD
SB_C = SB_W // P
ML_H = 4
ML_D = 96
SG = 4
SG_D = 64
SG_W = SG * SG_D
NE = 32
NGRP = 4
EPG = NE // NGRP
ROWS = 2 * SEQ
NARROW = 64
WIDE = SEQ
FE = 256

SLOTS = 3
SLOT = 6144
PIECE = 2048
STREAM = [("w_pool", 1, 2048), ("w_gu0", NF // 2, 4096), ("w_dn0", KD, FF), ("w_kv", 1, 3072),
          ("w_q", 2, 4096), ("w_o", 2, 4096), ("w_gu1", NF // 2, 4096), ("w_dn1", KD, FF),
          ("w_z", 7, 4096), ("w_out", 4, 2304), ("w_proj", 1, 2560), ("w_exp", NE, SLOT),
          ("w_ple", 2, 4096)]
UNSPLIT = ("w_pool", "w_kv", "w_proj", "w_exp")
FIRST, FIRST_PIECE = {}, {}
_t = _p = 0
for _name, _n, _ in STREAM:
    FIRST[_name], FIRST_PIECE[_name] = _t, _p
    _t += _n
    _p += 0 if _name in UNSPLIT else 2 * _n

NORMS = [("mixpre0", 8), ("mixpost0", 8), ("ffnpre0", 8), ("ffnpost0", 8), ("pre1", 8),
         ("mixpost1", 8), ("ffnpre1", 8), ("ffnpost1", 8), ("norm1", 8), ("sb_out", SB_C),
         ("norm2", 8), ("ple", 8), ("final", 8)]
NORM, SQ0 = {}, {}
_s = 0
for _i, (_name, _n) in enumerate(NORMS):
    NORM[_name], SQ0[_name] = _i, _s
    _s += _n

VECS = [("mixpre0", 8), ("mixpost0", 8), ("ffnpre0", 8), ("ffnpost0", 8), ("mixpre1", 8),
        ("mixpost1", 8), ("ffnpre1", 8), ("ffnpost1", 8), ("kv_norm", 8), ("pool_scale", 8),
        ("norm1", 8), ("norm2", 8), ("ple", 8), ("final", 8), ("b_q", 8), ("b_o", 8), ("b_k", 2),
        ("sb_out", SB_C), ("conv_w", 32), ("conv_b", 8), ("mnorm", ML_H), ("igate_b", 1),
        ("fgate_b", 1), ("sgu_b", SG)]
VCOL, NV = {}, 0
for _name, _n in VECS:
    VCOL[_name] = NV
    NV += _n
ROWV = [("sinks", NH), ("b_v", 128), ("ln_g", SG_W), ("ln_b", SG_W), ("sgu_out", SG_W),
        ("router_b", NGRP + NE), ("desc", NGRP)]
RCOL, NR = {}, 0
for _name, _n in ROWV:
    RCOL[_name] = NR
    NR += _n
CONST = [("ident", P), ("strict", P), ("negtri", P), ("sgumask", P),
         ("invcnt", len(WINDOWS) * PADT), ("buckets", P)]
CCOL, NC = {}, 0
for _name, _n in CONST:
    CCOL[_name] = NC
    NC += _n

Z_OUT = [[("conv", 0), ("conv", 1)], [("conv", 2), ("conv", 3)], [("conv", 4), ("conv", 5)],
         [("conv", 6), ("conv", 7)], [("ob", 0), ("ob", 1)],
         [("gate", 0), ("ob", 2), ("gate", 1), ("ob", 3)], [("qa", 0), ("qa", 1)],
         [("qa", 2), ("ka", 0)], [("ka", 1), ("ka", 2)], [("va", 0), ("va", 1)],
         [("vab", 0), ("vab", 1)], [("vb", 0), ("vb", 1)], [("uc", 0), ("uc", 1)], [("vc", 0), ("vc", 1)]]
Z_TOKENS = ("va", "vab", "vb", "uc", "vc")
Z_COUNT = sum(len(x) for x in Z_OUT)
GATE_AT = [(0, ML_H + ML_D), (ML_H, ML_D), (ML_H + ML_D, ML_H + ML_D), (2 * ML_H + ML_D, ML_D)]


def bass_two_blocks(nc, a, out):
    bias_rows = nc.dram_tensor("bias_rows", (NH, 3 * P), F32, kind="Internal").ap()

    ctx = ExitStack()
    with ctx:
        def sb(name, shape, dt=F32, within=None):
            return (within or ctx).enter_context(nc.sbuf_tensor(name, shape, dt))

        sems = {}

        def sem(name):
            if name not in sems:
                sems[name] = ctx.enter_context(nc.semaphore(name))
            return sems[name]

        ring = sb("ring", [P, SLOTS, SLOT])
        hs = sb("hs", [P, KD, T])
        mix = sb("mix", [P, KD, T])
        rstd = sb("rstd", [P, 2, T])
        sq = sb("sq", [P, 4, T])
        vec = sb("vec", [P, NV])
        row = sb("row", [P, NR])
        cst = sb("cst", [P, NC])
        rw = sb("rw", [P, KD, NGRP + NE])
        sgw = sb("sgw", [P, SG, P])
        relb = sb("relb", [32, NH])
        ones = sb("ones", [P, P])
        nones = sb("nones", [P, P])
        iota = sb("iota", [P, ROWS])
        small = sb("small", [P, 420])
        route_i = sb("route_i", [P, 2, NE], I32)

        with ExitStack() as turn:
            wh = sb("wh", [P, 2, PIECE], F32R, turn)
            wl = sb("wl", [P, 2, PIECE], F32R, turn)
        with ExitStack() as turn:
            ysT = sb("ysT", [P, KD, ROWS + WIDE], F32, turn)
            ae = sb("ae", [P, 2, WIDE], F32, turn)
            sgate = sb("sgate", [P, 2, WIDE], F32, turn)
        ctx.enter_context(nc.sbuf_tensor("split_room", [P, 4 * PIECE], F32))
        with ExitStack() as turn:
            xh = sb("xh", [P, 9, SEQ], F32R, turn)
            xl = sb("xl", [P, 9, SEQ], F32R, turn)
        with ExitStack() as turn:
            xhT = sb("xhT", [P, KD, T], F32R, turn)
            sb("xgap", [P, 9 * SEQ - KD * T], F32, turn)
            xlT = sb("xlT", [P, KD, T], F32R, turn)
        with ExitStack() as turn:
            xtra = sb("xtra", [P, 2, 9 * SEQ], F32, turn)
        ctx.enter_context(nc.sbuf_tensor("x_room", [P, 18 * SEQ], F32))
        with ExitStack() as turn:
            acth = sb("acth", [P, NF, T], F32R, turn)
            actl = sb("actl", [P, NF, T], F32R, turn)
        work = sb("work", [P, 2 * NF * T])

        ps = ctx.enter_context(nc.psum_tensor("ps", [P, 8, 512], F32))

        def carve():
            at = [0]

            def take(*shape):
                n = 1
                for s in shape:
                    n *= s
                v = work[:, at[0]:at[0] + n]
                at[0] += n
                assert at[0] <= 2 * NF * T
                if len(shape) == 2:
                    v = v.rearrange("p (a b) -> p a b", b=shape[1])
                if len(shape) == 3:
                    v = v.rearrange("p (a b c) -> p a b c", b=shape[1], c=shape[2])
                return v
            return take

        take = carve()
        hp = take(KD, PADT + T)
        win = take(2 * len(WINDOWS), 2, PADT + T)
        pooled = take(KD, T)
        brow = take(3 * P)
        take = carve()
        lg = [take(2 * HEADS_PER_GROUP, SEQ) for _ in range(2)]
        h1 = lg[0]
        qT = take(KD, SEQ)
        kT = take(2, T)
        vtok = take(NB + 1, P)
        brev = take(NH, SEQ)
        pT = [mix[:, 2 * i:2 * i + 2, :].rearrange("p a b -> p (a b)")[:, 0:4 * P] for i in range(2)]
        take = carve()
        qaT = take(SB_C, SEQ)
        kaT = take(SB_C, SEQ)
        va = take(NB, SB_W)
        vb = take(NB, ML_H * ML_D)
        ob = take(ML_H, SEQ)
        uc = take(NB, SG_W)
        vc = take(NB, SG_W)
        cv = take(2 * ML_H, SEQ)
        e1 = take(2, 3 * P)
        sp = take(2, 3 * P)
        aw = take(2, 3 * P)
        yaT = take(SB_C, SEQ)
        yb = take(ML_H, SEQ)
        ycT = take(NB, SEQ)
        zpre = [ring[:, s, 4096:4096 + 4 * (SEQ + 3)].rearrange("p (a b) -> p a b", b=SEQ + 3)
                for s in range(2)]
        gt = ring[:, 2, 4096:4096 + 7 * SEQ].rearrange("p (a b) -> p a b", b=SEQ)
        take = carve()
        xsT = take(KD, ROWS + WIDE)
        ysr = work[:, 0:4 * D].rearrange("p (a b) -> p a b", b=D)
        h2 = take(NB, D)
        combr = take(4, SEQ)
        psel = take(NB, ROWS)
        combt = take(NB, ROWS)
        ppT = work[:, KD * (ROWS + WIDE) + 3 * D:KD * (ROWS + WIDE) + 5 * D].rearrange("p (a b) -> p a b", b=SEQ)
        xe = [mix[:, :, :].rearrange("p a b -> p (a b)")[:, 0:KD * WIDE].rearrange("p (a b) -> p a b", b=WIDE),
              xtra[:, 0, 0:KD * WIDE].rearrange("p (a b) -> p a b", b=WIDE),
              xtra[:, 1, 0:KD * WIDE].rearrange("p (a b) -> p a b", b=WIDE)]

        def V(name, i=0, rows=P):
            return vec[0:rows, VCOL[name] + i:VCOL[name] + i + 1]

        def R(name, n, at=0):
            return row[:, RCOL[name] + at:RCOL[name] + at + n]

        def C(name, n=P, rows=P, at=0):
            return cst[0:rows, CCOL[name] + at:CCOL[name] + at + n]

        ident = C("ident")

        def tile_at(t):
            return t % SLOTS, t // SLOTS

        def ring_steps(eng, name, body, first=0, last=None):
            n = dict((x, y) for x, y, _ in STREAM)[name] if last is None else last
            turns = (n - first) // SLOTS
            if turns >= 2:
                with eng.Fori(0, turns) as k:
                    for j in range(SLOTS):
                        slot, rnd = tile_at(FIRST[name] + first + j)
                        body(slot, k + rnd, k * SLOTS + (first + j))
            else:
                turns = 0
            for i in range(first + turns * SLOTS, n):
                slot, rnd = tile_at(FIRST[name] + i)
                body(slot, rnd, i)

        def owner(t):
            return next((name, t - FIRST[name]) for name, n, _ in STREAM if t - FIRST[name] < n)

        def tile_done(name, i):
            by_product = {"w_pool": ("mix_psum", KD), "w_kv": ("kv_psum", 3), "w_proj": ("pp_psum", KD),
                          "w_exp": ("down_done", i + 1)}
            return by_product.get(name) or ("lo_done", i * 2 + (FIRST_PIECE[name] + 2))

        def piece_done(name, q):
            if name == "w_z":
                return "z_psum", sum(len(x) for x in Z_OUT[:q + 1])
            return {"w_gu0": ("gu_psum", q + 1), "w_dn0": ("dn_psum", q + 1), "w_q": ("q_psum", q * 2 + 2),
                    "w_o": ("wo_psum", q * 2 + 2), "w_gu1": ("gu_psum", q + (NF + 1)),
                    "w_dn1": ("dn_psum", q + (2 * KD + 1)), "w_out": ("wout_psum", q + 1),
                    "w_ple": ("ple_psum", q * 2 + 2)}[name]

        SPLIT = [(name, 2 * n) for name, n, _ in STREAM if name not in UNSPLIT]

        class Chain:

            def __init__(self, eng, name):
                self.eng, self.sem, self.n = eng, sem(name), 0

            def __call__(self, ins):
                self.n += 1
                ins.then_inc(self.sem, 1)
                self.eng.wait_ge(self.sem, self.n)

        block = ctx.enter_context(nc.Block())

        @block.sync
        def _(sp_):
            sp_.dma_start(hs[:, :, :], a["hT"]).then_inc(sem("hs_loaded"), 16)
            sp_.dma_start(vec[:, :], a["vec"]).then_inc(sem("consts_loaded"), 16)
            sp_.dma_start(cst[:, :], a["cst"]).then_inc(sem("consts_loaded"), 16)

            def load(name, size):
                def body(slot, rnd, i):
                    if type(i) is not int or i >= SLOTS:
                        done, count = tile_done(name, i - SLOTS)
                        sp_.wait_ge(sem(done), count)
                    elif FIRST[name] + i >= SLOTS:
                        done, count = tile_done(*owner(FIRST[name] + i - SLOTS))
                        sp_.wait_ge(sem(done), count)
                    src = a[name][bass.ds(i, 1), :, :] if type(i) is not int else a[name][i:i + 1, :, :]
                    sp_.dma_start(ring[:, slot, 0:size], src.rearrange("a p n -> p (a n)"))\
                       .then_inc(sem(f"tile_ready{slot}"), 16)
                return body

            def stream(name):
                size = dict((x, z) for x, _, z in STREAM)[name]
                body = load(name, size)
                n = dict((x, y) for x, y, _ in STREAM)[name]
                for i in range(min(SLOTS, n)):
                    body(*tile_at(FIRST[name] + i), i)
                ring_steps(sp_, name, body, first=min(SLOTS, n))

            stream("w_pool")
            sp_.dma_start(row[:, :], a["row"]).then_inc(sem("tables_loaded"), 16)
            sp_.dma_start(relb[:, :], a["rel_bias"]).then_inc(sem("tables_loaded"), 16)
            sp_.dma_start(rw[:, :, :], a["rw"]).then_inc(sem("tables_loaded"), 16)
            sp_.dma_start(sgw[:, :, :], a["sgw"]).then_inc(sem("tables_loaded"), 16)
            sp_.wait_ge(sem("brow_ready"), 2)
            sp_.dma_start(bias_rows, brow[0:NH, :]).then_inc(sem("bias_out"), 16)
            stream("w_gu0")
            stream("w_dn0")
            stream("w_kv")
            sp_.wait_ge(sem("bias_out"), 16)
            sp_.wait_ge(sem("dn_psum"), 2 * KD)
            skew = bass.AP(bias_rows.tensor, 0, [[1, P], [3 * P, NH], [1, SEQ]])
            sp_.dma_start(brev, skew).then_inc(sem("bias_ready"), 16)
            for name in ("w_q", "w_o", "w_gu1", "w_dn1", "w_z", "w_out", "w_proj", "w_exp", "w_ple"):
                if name == "w_proj":
                    sp_.wait_ge(sem("y_split"), 9)
                stream(name)
            for c in range(KD):
                sp_.wait_ge(sem("out_ready"), c + 1)
                sp_.dma_start(out[:, c, :], mix[:, c, 0:SEQ]).then_inc(sem("out_stored"), 16)
            sp_.wait_ge(sem("out_stored"), 16 * KD)

        def pool_groups(eng, chain, groups, done):
            for g in groups:
                eng.wait_ge(sem("h_ready"), 2 * g + 2)
                eng.wait_ge(sem("hp_padded"), 1)
                if g == groups[0]:
                    eng.wait_ge(sem("consts_loaded"), 32)
                cur, lo, w, k = hp[:, 2 * g:2 * g + 2, :], 0, 1, 0
                while w < WINDOWS[g]:
                    new = win[:, 2 * g + k % 2, :, :]
                    chain(eng.tensor_tensor(new[:, :, lo + w:], cur[:, :, lo + w:], cur[:, :, lo:PADT + T - w], ALU.add))
                    cur, lo, w, k = new, lo + w, 2 * w, k + 1
                h = hp[:, 2 * g:2 * g + 2, PADT:]
                p = pooled[:, 2 * g:2 * g + 2, :]
                inv = C("invcnt", PADT, at=g * PADT).unsqueeze(1).to_broadcast([P, 2, PADT])
                fix = win[:, 2 * g + k % 2, :, 0:PADT]
                chain(eng.tensor_scalar(p[:, :, PADT:], cur[:, :, 2 * PADT:], 1.0 / w, None, ALU.mult))
                chain(eng.tensor_tensor(p[:, :, PADT:], p[:, :, PADT:], h[:, :, PADT:], ALU.subtract))
                chain(eng.tensor_tensor(fix, cur[:, :, PADT:2 * PADT], inv, ALU.mult))
                eng.tensor_tensor(p[:, :, 0:PADT], fix, h[:, :, 0:PADT], ALU.subtract).then_inc(sem(done), 1)

        def residual_add(pool, k, cols):
            n = cols.stop - cols.start
            for c in range(KD):
                pool.wait_ge(sem("delta_ready"), k * KD + c + 1)
                pool.tensor_tensor(hs[:, c, cols], hs[:, c, cols], mix[:, c, 0:n], ALU.add)\
                    .then_inc(sem("hs_ready"), 1)

        def residual_add_gate(pool):
            for c in range(KD):
                pool.wait_ge(sem("delta_ready"), 4 * KD + c + 1)
                pool.tensor_tensor(hs[:, c, N_META:], hs[:, c, N_META:], mix[:, c, 0:SEQ], ALU.add)\
                    .then_inc(sem("hs_ready"), 1)

        def ffn_pool(pool, l, n):
            with pool.Fori(0, NF // 2) as i:
                for j in range(2):
                    f = i * 2 + j
                    pool.wait_ge(sem("silu_ready"), f + (l * NF + 1))
                    pool.wait_ge(sem("up_ready"), f + (l * NF + 1))
                    pool.tensor_tensor(mix[:, 6 + j, 0:n], mix[:, 2 + j, 0:n], mix[:, 4 + j, 0:n], ALU.mult)\
                        .then_inc(sem("act_ready"), 1)
                    pool.wait_ge(sem("act_ready"), f + (l * NF + 1))
                    pool.tensor_copy(acth[:, bass.ds(f, 1), 0:n], mix[:, 6 + j:7 + j, 0:n])\
                        .then_inc(sem("acth_ready"), 1)
                    pool.wait_ge(sem("acth_ready"), f + (l * NF + 1))
                    pool.tensor_tensor(actl[:, bass.ds(f, 1), 0:n], mix[:, 6 + j:7 + j, 0:n],
                                       acth[:, bass.ds(f, 1), 0:n].bitcast(F32), ALU.subtract)\
                        .then_inc(sem("act_split"), 1)

        def conv(eng, chain, j, done):
            eng.wait_ge(sem("z_evac"), j + 1)
            eng.wait_ge(sem("zpre_padded"), 2)
            src, dst = zpre[j // ML_H][0:ML_D, j % ML_H, :], cv[0:ML_D, j, :]
            chain(eng.tensor_scalar(dst, src[:, 0:SEQ], V("conv_w", 4 * j, ML_D), V("conv_b", j, ML_D), ALU.mult, ALU.add))
            for k in range(1, 4):
                ins = eng.scalar_tensor_tensor(dst, src[:, k:k + SEQ], V("conv_w", 4 * j + k, ML_D), dst, ALU.mult, ALU.add)
                if k < 3:
                    chain(ins)
            ins.then_inc(sem(done), 1)

        @block.gpsimd
        def _(pool):
            chain = Chain(pool, "pool_chain")
            pool.memset(ones[:, :], 1.0).then_inc(sem("ones_ready"), 1)
            pool.memset(nones[:, :], -1.0).then_inc(sem("ones_ready"), 1)
            pool.memset(hp[:, :, 0:PADT], 0.0).then_inc(sem("hp_padded"), 1)
            pool.memset(brow[0:NH, :], NEG).then_inc(sem("brow_ready"), 1)
            pool.iota(mix[:, 0:2, 0:SEQ].bitcast(I32), pattern=[[SEQ, 2], [1, SEQ]], base=0, channel_multiplier=0)\
                .then_inc(sem("iota_i"), 1)
            pool.wait_ge(sem("iota_i"), 1)
            pool.tensor_copy(iota[:, :].rearrange("p (a b) -> p a b", a=2), mix[:, 0:2, 0:SEQ].bitcast(I32))\
                .then_inc(sem("iota_ready"), 1)

            pool.wait_ge(sem("consts_loaded"), 32)
            pool.wait_ge(sem("tables_loaded"), 64)
            pool.tensor_tensor(sgw[:, :, :], sgw[:, :, :], C("sgumask").unsqueeze(1).to_broadcast([P, SG, P]), ALU.mult)\
                .then_inc(sem("sgw_masked"), 1)

            pool_groups(pool, chain, (0, 1), "p_pool")
            residual_add(pool, 0, slice(0, T))
            ffn_pool(pool, 0, T)
            residual_add(pool, 1, slice(0, T))
            residual_add(pool, 2, slice(N_META, T))
            ffn_pool(pool, 1, SEQ)
            residual_add(pool, 3, slice(N_META, T))

            for s in range(2):
                pool.memset(zpre[s][0:ML_D, :, 0:3], 0.0).then_inc(sem("zpre_padded"), 1)
            for i in range(SB_H):
                pool.wait_ge(sem("sb_exp"), i + 1)
                v = aw[:, i % 2, :].rearrange("p (a b) -> p a b", a=3)[:, 0:3:2, :]
                pool.affine_select(out=v, in_=v, compare_op=ALU.is_gt, fill=0.0, base=0,
                                   pattern=[[0, 2], [1, P]], channel_multiplier=-1).then_inc(sem("sb_a"), 1)
            for h in range(ML_H):
                pool.wait_ge(sem("ml_exp"), 2 * h + 2)
                v = aw[:, h % 2, :].rearrange("p (a b) -> p a b", a=3)[:, 0:3:2, :]
                pool.affine_select(out=v, in_=v, compare_op=ALU.is_ge, fill=0.0, base=0,
                                   pattern=[[0, 2], [1, P]], channel_multiplier=-1).then_inc(sem("ml_d"), 1)

            pool.wait_ge(sem("hs_ready"), 5 * KD)
            pool.memset(xsT[:, :, ROWS:ROWS + WIDE], 0.0).then_inc(sem("xs_padded"), 1)
            pool.wait_ge(sem("xs_ready"), KD // 2)
            pool.wait_ge(sem("xs_ready_d"), KD // 2)
            pool.wait_ge(sem("xs_padded"), 1)
            pool.wait_ge(sem("route_ready"), 2)

            def window(slot, rnd, e):
                start = pool.value_load(route_i[0:1, 0, bass.ds(e, 1)], min_val=0, max_val=ROWS)
                count = pool.value_load(route_i[0:1, 1, bass.ds(e, 1)], min_val=0, max_val=WIDE)
                buf = xe[slot]

                def buffer_free():
                    if type(e) is not int or e >= SLOTS:
                        pool.wait_ge(sem("gu_done"), e - SLOTS + 1)

                with pool.If(count > NARROW):
                    buffer_free()
                    pool.tensor_copy(buf, xsT[:, :, bass.ds(start, WIDE)]).then_inc(sem("xe_ready"), 1)
                with pool.Else():
                    buffer_free()
                    pool.tensor_copy(buf[:, :, 0:NARROW], xsT[:, :, bass.ds(start, NARROW)])\
                        .then_inc(sem("xe_ready"), 1)

            for e in range(SLOTS):
                slot, rnd = tile_at(FIRST["w_exp"] + e)
                window(slot, rnd, e)
            ring_steps(pool, "w_exp", window, first=SLOTS)
            residual_add_gate(pool)

        def r_of(name):
            return rstd[:, NORM[name] % 2, :]

        def square(act, name, c, src, n, rows=P, **kw):
            k = SQ0[name] + c
            if k >= 4:
                act.wait_ge(sem("sq_used"), k - 3)
            act.activation(sq[0:rows, k % 4, 0:n], src, ACT.Square, **kw).then_inc(sem("sq_ready"), 1)

        def rsqrt(act, chain, name, width, n):
            r = r_of(name)[:, 0:n]
            act.wait_ge(sem("sq_used"), SQ0[name] + dict(NORMS)[name])
            chain(act.activation(r, ps[:, 6, 0:n], ACT.Ln, scale=1.0 / width, bias=EPS))
            act.activation(r, r, ACT.Exp, scale=-0.5).then_inc(sem("r_ready"), 1)

        def split_hi(act, name, slot, rnd, i, j, size):
            if j == 0:
                act.wait_ge(sem(f"tile_ready{slot}"), rnd * 16 + 16)
            if type(i) is not int or i > 0:
                done, count = piece_done(name, i * 2 + (j - 2))
                act.wait_ge(sem(done), count)
            elif FIRST_PIECE[name]:
                before, n = SPLIT[[x for x, _ in SPLIT].index(name) - 1]
                done, count = piece_done(before, n + j - 2)
                act.wait_ge(sem(done), count)
            act.activation(wh[:, j, 0:size], ring[:, slot, j * size:(j + 1) * size], ACT.Copy)\
               .then_inc(sem("hi_done"), 1)

        def split_lo(dve, name, slot, rnd, i, j, size):
            piece = i * 2 + (FIRST_PIECE[name] + j)
            dve.wait_ge(sem("hi_done"), piece + 1)
            dve.tensor_tensor(wl[:, j, 0:size], ring[:, slot, j * size:(j + 1) * size],
                              wh[:, j, 0:size].bitcast(F32), ALU.subtract).then_inc(sem("lo_done"), 1)

        def halves(name, i, size):
            slot, rnd = tile_at(FIRST[name] + i)
            return [(slot, rnd, i, j, size) for j in range(2)]

        def wo_out(act, c):
            act.wait_ge(sem("wo_psum"), c + 1)
            act.activation(mix[:, c, 0:SEQ], ps[:, c % 4, 0:SEQ], ACT.Identity, bias=V("b_o", c))\
               .then_inc(sem("mix_ready"), 1)
            square(act, "mixpost1", c, ps[:, c % 4, 0:SEQ], SEQ, bias=V("b_o", c))

        def ple_gate(act, c):
            act.wait_ge(sem("ple_psum"), c + 1)
            act.activation(mix[:, c, 0:SEQ], ps[:, c % 4, 0:SEQ], ACT.Sigmoid).then_inc(sem("ple_sig"), 1)

        def y_chunks():
            return [(yaT[:, c, :], P) for c in range(SB_C)] + [(yb[0:ML_D, h, :], ML_D) for h in range(ML_H)] \
                + [(ycT[:, c, :], P) for c in range(NB)]

        def z_parts(parts, n):
            bank = ps[:, n % 4, :]
            kind, i = parts
            if kind == "conv":
                return [(zpre[i // ML_H][0:ML_D, i % ML_H, 3:], bank[0:ML_D, 0:SEQ], ACT.Copy, {})]
            if kind == "ob":
                return [(ob[0:ML_D, i, :], bank[0:ML_D, 0:SEQ], ACT.Copy, {})]
            if kind == "gate":
                return [(gt[0:ML_H, i, :], bank[0:ML_H, 0:SEQ], ACT.Identity,
                         {"bias": V("fgate_b" if i else "igate_b", 0, ML_H)})]
            if kind == "qa":
                return [(qaT[:, i, :], bank[:, 0:SEQ], ACT.Copy, {"scale": HD ** -0.5})]
            if kind == "ka":
                return [(kaT[:, i, :], bank[:, 0:SEQ], ACT.Copy, {})]
            if kind == "va":
                return [(va[:, i, 0:256], bank[:, 0:256], ACT.Copy, {})]
            if kind == "vab":
                return [(va[:, i, 256:384], bank[:, 0:128], ACT.Copy, {}), (vb[:, i, 0:128], bank[:, 128:256], ACT.Copy, {})]
            if kind == "vb":
                return [(vb[:, i, 128:384], bank[:, 0:256], ACT.Copy, {})]
            if kind == "uc":
                return [(uc[:, i, :], bank[:, 0:SG_W], ACT.Gelu_apprx_tanh, {})]
            return [(vc[:, i, :], bank[:, 0:SG_W], ACT.Gelu_apprx_tanh, {})]

        def ffn_act(act, chain, l, n, cols):
            gu, dn, pre, post = f"w_gu{l}", f"w_dn{l}", f"ffnpre{l}", f"ffnpost{l}"
            x = xhT if l == 0 else xh
            for args in halves(gu, 0, PIECE):
                split_hi(act, gu, *args)
            for c in range(KD):
                act.wait_ge(sem("hs_ready"), (1 if l == 0 else 3) * KD + c - KD + 1)
                act.activation(x[:, c, 0:n], hs[:, c, cols], ACT.Copy, scale=V(pre, c)).then_inc(sem("xh_ready"), 1)
                if c < 4:
                    square(act, pre, c, hs[:, c, cols], n)
            for c in range(4, KD):
                square(act, pre, c, hs[:, c, cols], n)
            rsqrt(act, chain, pre, D, n)
            act.preload_act_table_set("silu_and_others")

            def silu(f, j):
                act.wait_ge(sem("gr_ready"), f + (l * NF + 1))
                act.activation(mix[:, 2 + j, 0:n], mix[:, j, 0:n], ACT.Silu).then_inc(sem("silu_ready"), 1)

            def body(slot, rnd, i):
                for j in range(2):
                    split_hi(act, gu, slot, rnd, i, j, PIECE)
                    silu(i * 2 + (j - 2), j)

            ring_steps(act, gu, body, first=1)
            for j in range(2):
                silu(NF - 2 + j, j)
            act.preload_act_table_set("natural_log_exp_and_others")

            def leave(c):
                act.wait_ge(sem("dn_psum"), 2 * (l * KD + c) + 2)
                act.activation(mix[:, c, 0:n], ps[:, 4 + c % 2, 0:n], ACT.Copy).then_inc(sem("mix_ready"), 1)
                square(act, post, c, ps[:, 4 + c % 2, 0:n], n)

            for i in range(KD):
                for args in halves(dn, i, FF // 2):
                    split_hi(act, dn, *args)
                if i:
                    leave(i - 1)
            leave(KD - 1)
            rsqrt(act, chain, post, D, n)

        @block.scalar
        def _(act):
            chain = Chain(act, "act_chain")
            act.preload_act_table_set("natural_log_exp_and_others")
            act.wait_ge(sem("hs_loaded"), 16)
            for c in range(KD):
                square(act, "mixpre0", c, hs[:, c, :], T)
            rsqrt(act, chain, "mixpre0", D, T)
            act.wait_ge(sem("brow_psum"), 1)
            act.wait_ge(sem("brow_ready"), 1)
            act.activation(brow[0:NH, P:2 * P], ps[0:NH, 7, 0:P], ACT.Copy).then_inc(sem("brow_ready"), 1)
            act.wait_ge(sem("iota_ready"), 1)
            for c in range(KD):
                act.wait_ge(sem("mix_psum"), c + 1)
                act.activation(mix[:, c, :], ps[:, c % 4, 0:T], ACT.Copy, scale=V("pool_scale", c))\
                   .then_inc(sem("mix_ready"), 1)
                square(act, "mixpost0", c, ps[:, c % 4, 0:T], T, scale=V("pool_scale", c))
            rsqrt(act, chain, "mixpost0", D, T)
            ffn_act(act, chain, 0, T, slice(0, T))

            for c in range(KD):
                act.wait_ge(sem("hs_ready"), KD + c + 1)
                square(act, "pre1", c, hs[:, c, :], T)
            rsqrt(act, chain, "pre1", D, T)
            for x in halves("w_q", 0, PIECE):
                split_hi(act, "w_q", *x)
            for c in range(KD):
                act.wait_ge(sem("h1_ready"), c + 1)
                act.activation(xh[:, c, :], h1[:, c, :], ACT.Copy).then_inc(sem("xh_ready"), 1)
            for j in range(2):
                act.wait_ge(sem("kv_psum"), j + 1)
                act.activation(kT[:, j, :], ps[:, j, 0:T], ACT.Identity, bias=V("b_k", j))\
                   .then_inc(sem("kT_ready"), 1)
            for x in halves("w_q", 1, PIECE) + halves("w_o", 0, PIECE):
                split_hi(act, "w_q" if x[2] else "w_o", *x)
            for g in range(NH // HEADS_PER_GROUP):
                act.wait_ge(sem("negm_ready"), g + 1)
                for i in range(2 * HEADS_PER_GROUP):
                    n = N_META + P if i % 2 == 0 else 2 * P
                    k = 2 * HEADS_PER_GROUP * g + i
                    v = lg[g % 2][:, i, 0:n]
                    act.activation(v, v, ACT.Exp, bias=small[:, 32 + k:33 + k], accum_out=small[:, 96 + k:97 + k])\
                       .then_inc(sem("exp_ready"), 1)
                k = 2 * HEADS_PER_GROUP * g
                act.activation(small[:, 64 + k:72 + k], small[:, 64 + k:72 + k], ACT.Exp).then_inc(sem("exp_ready"), 1)
                for h in range(HEADS_PER_GROUP * g, HEADS_PER_GROUP * (g + 1)):
                    act.wait_ge(sem("pt_psum"), h + 1)
                    if h >= 2:
                        act.wait_ge(sem("o_done"), h - 1)
                    act.activation(pT[h % 2][:, 0:3 * P], ps[:, 4 + h % 2, 0:3 * P], ACT.Copy).then_inc(sem("pt_ready"), 1)
                    act.activation(pT[h % 2][0:N_META, 3 * P:4 * P], ps[0:N_META, 4 + h % 2, 3 * P:4 * P], ACT.Copy)\
                       .then_inc(sem("pt_ready"), 1)
                    if h % 2 == 1:
                        c = h // 2
                        act.wait_ge(sem("o_done"), h + 1)
                        o = ps[:, 6 + c % 2, 0:SEQ].rearrange("p (b q) -> p b q", q=P)
                        act.activation(xh[:, c, :].rearrange("p (b q) -> p b q", q=P), o[:, :, ::-1], ACT.Copy)\
                           .then_inc(sem("oh_ready"), 1)
            for k in range(NB):
                split_hi(act, "w_o", *halves("w_o", 1, PIECE)[k])
                for c in range(2 * k, 2 * k + 2):
                    wo_out(act, c)
            for c in range(4, KD):
                wo_out(act, c)
            rsqrt(act, chain, "mixpost1", D, SEQ)
            ffn_act(act, chain, 1, SEQ, slice(N_META, T))

            for x in halves("w_z", 0, PIECE):
                split_hi(act, "w_z", *x)
            for c in range(KD):
                act.wait_ge(sem("hs_ready"), 3 * KD + c + 1)
                square(act, "norm1", c, hs[:, c, N_META:], SEQ)
            rsqrt(act, chain, "norm1", D, SEQ)
            for c in range(KD):
                act.wait_ge(sem("xn_ready"), c + 1)
                act.activation(xh[:, c, :], mix[:, c, 0:SEQ], ACT.Copy).then_inc(sem("xh_ready"), 1)
            n = 0
            for piece in range(14):
                if piece < 12:
                    split_hi(act, "w_z", *halves("w_z", piece // 2 + 1, PIECE)[piece % 2])
                for parts in Z_OUT[piece]:
                    act.wait_ge(sem("z_psum"), n + 1)
                    for q, (dst, src, func, kw) in enumerate(z_parts(parts, n)):
                        ins = act.activation(dst, src, func, **kw)
                    ins.then_inc(sem("z_evac"), 1)
                    n += 1

            act.preload_act_table_set("silu_and_others")
            act.wait_ge(sem("conv_done"), 2 * ML_H)
            act.activation(cv[0:ML_D, :, :], cv[0:ML_D, :, :], ACT.Silu).then_inc(sem("cv_ready"), 1)
            act.preload_act_table_set("natural_log_exp_and_others")
            chain(act.activation(gt[0:ML_H, 2, :], gt[0:ML_H, 1, :], ACT.Abs))
            chain(act.activation(gt[0:ML_H, 2, :], gt[0:ML_H, 2, :], ACT.Exp, scale=-1.0))
            act.activation(gt[0:ML_H, 2, :], gt[0:ML_H, 2, :], ACT.Ln, bias=1.0).then_inc(sem("gate_ln"), 1)
            act.activation(ob[0:ML_D, :, :], ob[0:ML_D, :, :], ACT.Exp, scale=-1.0).then_inc(sem("ob_exp"), 1)
            act.wait_ge(sem("sgu_centred"), 1)
            act.activation(mix[:, 0:2, 0:SG_W], vc, ACT.Square).then_inc(sem("sgu_sq"), 1)
            act.wait_ge(sem("sgu_var"), 1)
            chain(act.activation(small[:, 8:16], small[:, 8:16], ACT.Ln, scale=1.0 / SG_D, bias=EPS))
            act.activation(small[:, 8:16], small[:, 8:16], ACT.Exp, scale=-0.5).then_inc(sem("sgu_r"), 1)
            act.wait_ge(sem("gate_m"), 1)
            act.activation(gt[0:ML_H, 6, :], gt[0:ML_H, 6, :], ACT.Exp, scale=-1.0).then_inc(sem("em_ready"), 1)
            act.wait_ge(sem("sgu_y"), SG)
            for b in range(NB):
                act.activation(mix[:, 2 + b, 0:SG_W], uc[:, b, :], ACT.Square, accum_out=small[:, 16 + b:17 + b])\
                   .then_inc(sem("sgu_ysq"), 1)
            act.wait_ge(sem("sgu_ysq"), NB)
            chain(act.activation(small[:, 16:18], small[:, 16:18], ACT.Ln, scale=1.0 / SG_W, bias=EPS))
            act.activation(small[:, 16:18], small[:, 16:18], ACT.Exp, scale=-0.5).then_inc(sem("sgu_yr"), 1)

            for i in range(SB_H + 2):
                if i < SB_H:
                    act.wait_ge(sem("sb_z"), i + 1)
                    if i >= 2:
                        act.wait_ge(sem("sb_sp"), i - 1)
                    e = e1[:, i % 2, :]
                    chain(act.activation(e, ps[:, i % 3, 0:3 * P], ACT.Abs))
                    chain(act.activation(e, e, ACT.Exp, scale=-1.0))
                    act.activation(e, e, ACT.Ln, bias=1.0).then_inc(sem("sb_ln"), 1)
                if 1 <= i <= SB_H:
                    act.wait_ge(sem("sb_E"), i)
                    if i >= 3:
                        act.wait_ge(sem("sb_o"), i - 2)
                    act.activation(aw[:, (i - 1) % 2, :], ps[:, (i - 1) % 3, 0:3 * P], ACT.Exp).then_inc(sem("sb_exp"), 1)
                if i >= 3 and i % 2 == 1:
                    c = (i - 2) // 2
                    act.wait_ge(sem("sb_o"), i - 1)
                    act.activation(yaT[:, c, :], ps[:, 3 + c % 2, 0:SEQ], ACT.Copy).then_inc(sem("ya_ready"), 1)
                    square(act, "sb_out", c, ps[:, 3 + c % 2, 0:SEQ], SEQ)
            act.wait_ge(sem("yc_psum"), 1)
            act.activation(ycT.rearrange("p a b -> p (a b)"), ps[:, 7, :], ACT.Copy).then_inc(sem("yc_ready"), 1)
            rsqrt(act, chain, "sb_out", SB_W, SEQ)
            for h in range(ML_H):
                act.wait_ge(sem("ml_max"), 2 * h + 2)
                if h >= 2:
                    act.wait_ge(sem("ml_num"), h - 1)
                for b, cols in ((0, slice(0, SEQ)), (1, slice(SEQ, 3 * P))):
                    act.activation(aw[:, h % 2, cols], sp[:, h % 2, cols], ACT.Exp, scale=-1.0,
                                   bias=small[:, 20 + ML_H * b + h:21 + ML_H * b + h]).then_inc(sem("ml_exp"), 1)
                if h >= 2:
                    act.wait_ge(sem("ml_h"), h - 1)
                act.activation(e1[0:ML_D, h % 2, 0:SEQ], ps[0:ML_D, 5, SEQ:2 * SEQ], ACT.Copy).then_inc(sem("ml_em"), 1)
            act.wait_ge(sem("ml_h"), ML_H)
            act.activation(mix[0:ML_D, 0:ML_H, 0:SEQ], yb[0:ML_D, :, :], ACT.Square).then_inc(sem("ml_sq"), 1)
            act.wait_ge(sem("ml_ss"), 1)
            r4 = mix[0:ML_D, ML_H:2 * ML_H, 0:SEQ]
            for b in range(2):
                chain(act.activation(r4[:, 2 * b:2 * b + 2, :], ps[0:ML_D, b, :].rearrange("p (a t) -> p a t", t=SEQ),
                                     ACT.Ln, scale=1.0 / ML_D, bias=EPS))
            act.activation(r4, r4, ACT.Exp, scale=-0.5).then_inc(sem("ml_r"), 1)
            for x in halves("w_out", 0, 9 * P):
                split_hi(act, "w_out", *x)
            act.wait_ge(sem("yc_ready"), 1)
            for j, (src, rows) in enumerate(y_chunks()):
                if j < SB_C + ML_H:
                    act.wait_ge(sem("y_fin"), j + 1)
                act.activation(xh[0:rows, j, :], src, ACT.Copy).then_inc(sem("yh_ready"), 1)
            for i in range(1, 4):
                for x in halves("w_out", i, 9 * P):
                    split_hi(act, "w_out", *x)

            for c in range(KD):
                act.wait_ge(sem("hs_ready"), 4 * KD + c + 1)
                square(act, "norm2", c, hs[:, c, N_META:], SEQ)
            rsqrt(act, chain, "norm2", D, SEQ)
            for q in range(4):
                act.wait_ge(sem("h2_psum"), q + 1)
                act.activation(h2[:, q // 2, q % 2 * 512:(q % 2 + 1) * 512], ps[:, 1 + q, :], ACT.Copy)\
                   .then_inc(sem("h2_ready"), 1)
            act.wait_ge(sem("route_g"), 1)
            act.activation(small[:, 128:136], small[:, 128:136], ACT.Exp).then_inc(sem("route_gexp"), 1)
            act.wait_ge(sem("route_d"), 1)
            act.activation(small[:, 180:182], small[:, 180:182], ACT.Exp).then_inc(sem("route_ex"), 1)
            for c in range(1, KD, 2):
                act.wait_ge(sem("xs_psum"), c + 1)
                act.activation(xsT[:, c, 0:ROWS], ps[:, c % 4, :], ACT.Copy).then_inc(sem("xs_ready"), 1)
            for q in range(2):
                act.wait_ge(sem("comb_psum"), q + 1)
                act.activation(combr[:, 2 * q:2 * q + 2, :].rearrange("p a b -> p (a b)"), ps[:, 6 + q, :], ACT.Copy)\
                   .then_inc(sem("comb_ready"), 1)
            for c in range(KD):
                act.wait_ge(sem("pp_psum"), c + 1)
                act.activation(ppT[:, c, :], ps[:, 4 + c % 2, 0:SEQ], ACT.Copy).then_inc(sem("pp_ready"), 1)
            act.preload_act_table_set("silu_and_others")

            def gate(slot, rnd, e):
                count = act.value_load(route_i[0:1, 1, bass.ds(e, 1)], min_val=0, max_val=WIDE)

                def sums_ready():
                    act.wait_ge(sem("gu_done"), e + 1)
                    if not (type(e) is int and e == 0):
                        act.wait_ge(sem("ae_ready"), e)

                with act.If(count > NARROW):
                    sums_ready()
                    act.activation(sgate[:, :, :], ps[:, 0, :].rearrange("p (a b) -> p a b", b=WIDE), ACT.Silu)\
                       .then_inc(sem("sg_ready"), 1)
                with act.Else():
                    sums_ready()
                    act.activation(sgate[:, :, 0:NARROW], ps[:, 0, 0:2 * NARROW].rearrange("p (a b) -> p a b", b=NARROW),
                                   ACT.Silu).then_inc(sem("sg_ready"), 1)

            slot, rnd = tile_at(FIRST["w_exp"])
            gate(slot, rnd, 0)
            ring_steps(act, "w_exp", gate, first=1)
            act.preload_act_table_set("natural_log_exp_and_others")
            for q in range(1, 8, 2):
                act.wait_ge(sem("ysr_psum"), q + 1)
                act.activation(ysr[:, q // 2, 512:1024], ps[:, q, :], ACT.Copy).then_inc(sem("ysr_ready_a"), 1)

            for c in range(KD):
                act.wait_ge(sem("hs_ready"), 5 * KD + c + 1)
                square(act, "ple", c, hs[:, c, N_META:], SEQ)
            rsqrt(act, chain, "ple", D, SEQ)
            for x in halves("w_ple", 0, PIECE):
                split_hi(act, "w_ple", *x)
            for c in range(KD):
                act.wait_ge(sem("xn_ready"), 2 * KD + c + 1)
                act.activation(xh[:, c, :], mix[:, c, 0:SEQ], ACT.Copy).then_inc(sem("xh_ready"), 1)
            act.preload_act_table_set("sigmoid_and_others")
            act.wait_ge(sem("x_ready"), 5 * KD)
            for k in range(2):
                split_hi(act, "w_ple", *halves("w_ple", 1, PIECE)[k])
                for c in range(2 * k, 2 * k + 2):
                    ple_gate(act, c)
            for c in range(4, KD):
                ple_gate(act, c)
            act.preload_act_table_set("natural_log_exp_and_others")
            for c in range(KD):
                act.wait_ge(sem("hs_ready"), 6 * KD + c + 1)
                square(act, "final", c, hs[:, c, N_META:], SEQ)
            rsqrt(act, chain, "final", D, SEQ)

        def z_cols(outs, q):
            kind = outs[q][0]
            if outs[0][0] == "gate":
                return GATE_AT[q]
            if kind in ("conv", "ob"):
                return q * ML_D, ML_D
            return q * P, P

        def onehot(i):
            return small[:, 200 + i * NB * NE:200 + (i + 1) * NB * NE].rearrange("p (b e) -> p b e", b=NB)

        def ffn_pe(pe, mm3, sum_squares, l, n):
            gu, dn, pre, post = f"w_gu{l}", f"w_dn{l}", f"ffnpre{l}", f"ffnpost{l}"
            xa, xb = (xhT, xlT) if l == 0 else (xh, xl)
            base = FIRST_PIECE[gu]

            def piece(i, j, k0=None):
                f = i * 2 + j
                pe.wait_ge(sem("lo_done"), f + (base + 1))
                if not (type(i) is int and i == 0):
                    pe.wait_ge(sem("up_ready"), f + (l * NF - 1))
                for k in range(KD):
                    if type(i) is int and i == 0 and j == 0:
                        pe.wait_ge(sem("x_ready"), 2 * l * KD + k + 1)
                    for g in range(2):
                        at = slice(k * 256 + g * P, k * 256 + g * P + P)
                        ins = mm3(ps[:, 2 * j + g, 0:n], (wh[:, j, at], wl[:, j, at]), (xa[:, k, 0:n], xb[:, k, 0:n]),
                                  k == 0, k == KD - 1)
                ins.then_inc(sem("gu_psum"), 1)

            piece(0, 0)
            for c in range(KD):
                sum_squares(pre, c, n)
            piece(0, 1)
            with pe.Fori(1, NF // 2) as i:
                for j in range(2):
                    piece(i, j)
            pe.wait_ge(sem("act_split"), (l + 1) * NF)
            base = FIRST_PIECE[dn]
            for c in range(KD):
                if c >= 2:
                    pe.wait_ge(sem("sq_ready"), SQ0[post] + c - 1)
                for j in range(2):
                    pe.wait_ge(sem("lo_done"), base + 2 * c + j + 1)
                    for k in range(NF // 2):
                        at = slice(k * P, (k + 1) * P)
                        f = j * (NF // 2) + k
                        ins = mm3(ps[:, 4 + c % 2, 0:n], (wh[:, j, at], wl[:, j, at]),
                                  (acth[:, f, 0:n], actl[:, f, 0:n]), f == 0, f == NF - 1)
                    ins.then_inc(sem("dn_psum"), 1)
                if c:
                    sum_squares(post, c - 1, n)
            sum_squares(post, KD - 1, n)

        @block.tensor
        def _(pe):
            mm = pe.matmul

            def sum_squares(name, c, n, rows=P):
                k, last = SQ0[name] + c, dict((x, y) for x, y in NORMS)[name] - 1
                if c == 0 and NORM[name]:
                    pe.wait_ge(sem("r_ready"), NORM[name])
                pe.wait_ge(sem("sq_ready"), k + 1)
                mm(ps[:, 6, 0:n], ones[0:rows, :], sq[0:rows, k % 4, 0:n], start=(c == 0), stop=(c == last))\
                    .then_inc(sem("sq_used"), 1)

            def mm3(o, w, x, first, last, swap=False):
                (wh_, wl_), (xh_, xl_) = w, x
                for n, (p, q) in enumerate(((wh_, xh_), (wl_, xh_), (wh_, xl_))):
                    if swap:
                        p, q = q, p
                    ins = mm(o, p, q, start=first and n == 0, stop=last and n == 2)
                return ins

            pe.wait_ge(sem("ones_ready"), 2)
            for c in range(KD):
                sum_squares("mixpre0", c, T)
            pe.wait_ge(sem("consts_loaded"), 32)
            pe.wait_ge(sem("tables_loaded"), 64)
            mm(ps[0:NH, 7, 0:P], relb[:, :], C("buckets", rows=32), start=True, stop=True).then_inc(sem("brow_psum"), 1)
            slot, rnd = tile_at(FIRST["w_pool"])
            pe.wait_ge(sem(f"tile_ready{slot}"), 16 * (rnd + 1))
            pw = ring[:, slot, 0:2048].rearrange("p (g k n) -> p g k n", g=4, k=2)
            for c in range(KD):
                g = c // 2
                pe.wait_ge(sem("p_pool" if g < 2 else "p_dve"), g % 2 + 1)
                if c >= 4:
                    pe.wait_ge(sem("sq_ready"), SQ0["mixpost0"] + c - 3)
                for k in range(2):
                    ins = mm(ps[:, c % 4, 0:T], pw[:, g, k, c % 2 * P:c % 2 * P + P], pooled[:, 2 * g + k, :],
                             start=(k == 0), stop=(k == 1))
                ins.then_inc(sem("mix_psum"), 1)
                if c:
                    sum_squares("mixpost0", c - 1, T)
            sum_squares("mixpost0", KD - 1, T)
            ffn_pe(pe, mm3, sum_squares, 0, T)

            for c in range(KD):
                sum_squares("pre1", c, T)
            slot, rnd = tile_at(FIRST["w_kv"])
            pe.wait_ge(sem(f"tile_ready{slot}"), 16 * (rnd + 1))
            wkv = ring[:, slot, 0:3072].rearrange("p (k n) -> p k n", k=KD)
            for j in range(2):
                for k in range(KD):
                    pe.wait_ge(sem("kvin_ready"), k + 1)
                    ins = mm(ps[:, j, 0:T], wkv[:, k, j * P:(j + 1) * P], mix[:, k, :], start=(k == 0), stop=(k == KD - 1))
                ins.then_inc(sem("kv_psum"), 1)
            for j in range(NB + 1):
                cols = slice(0, N_META) if j == 0 else slice(N_META + (j - 1) * P, N_META + j * P)
                for k in range(KD):
                    ins = mm(ps[0:cols.stop - cols.start, 2, j * P:(j + 1) * P], mix[:, k, cols], wkv[:, k, 2 * P:3 * P],
                             start=(k == 0), stop=(k == KD - 1))
            ins.then_inc(sem("kv_psum"), 1)
            x = (xh, xl)
            pe.wait_ge(sem("kT_ready"), 2)
            pe.wait_ge(sem("v_ready"), 2)
            for c in range(KD):
                piece = FIRST_PIECE["w_q"] + c // 2
                pe.wait_ge(sem("lo_done"), piece + 1)
                if c >= 4:
                    pe.wait_ge(sem("q_ready"), c - 3)
                for k in range(KD):
                    pe.wait_ge(sem("x_ready"), KD + k + 1)
                    at = slice(k * 256 + c % 2 * P, k * 256 + c % 2 * P + P)
                    ins = mm3(ps[:, c % 4, 0:SEQ], (wh[:, piece % 2, at], wl[:, piece % 2, at]),
                              (xh[:, k, 0:SEQ], xl[:, k, 0:SEQ]), k == 0, k == KD - 1)
                ins.then_inc(sem("q_psum"), 1)

            def scores(g):
                for h in range(HEADS_PER_GROUP * g, HEADS_PER_GROUP * (g + 1)):
                    rows = slice(h % 2 * HD, h % 2 * HD + HD)
                    for b in range(NB):
                        i = NB * h + b
                        keys = slice(0, N_META + P) if b == 0 else slice(N_META, T)
                        if i >= 4:
                            pe.wait_ge(sem("lg_ready"), i - 3)
                        mm(ps[:, i % 4, 0:keys.stop - keys.start], qT[rows, h // 2, b * P:(b + 1) * P],
                           kT[rows, h // 8, keys], start=True, stop=True).then_inc(sem("s_psum"), 1)

            def values(h):
                i = 2 * (h % HEADS_PER_GROUP)
                p = lg[h // HEADS_PER_GROUP % 2]
                pe.wait_ge(sem("p_ready"), 2 * h + 2)
                if h >= 2:
                    pe.wait_ge(sem("pt_ready"), 2 * h - 2)
                t = ps[:, 4 + h % 2, :]
                pe.transpose(t[:, 0:P], p[:, i, N_META:N_META + P], ident)
                pe.transpose(t[:, P:2 * P], p[:, i + 1, 0:P], ident)
                pe.transpose(t[:, 2 * P:3 * P], p[:, i + 1, P:2 * P], ident)
                pe.transpose(t[0:N_META, 3 * P:4 * P], p[:, i, 0:N_META], ident).then_inc(sem("pt_psum"), 1)

            def outputs(h):
                pe.wait_ge(sem("pt_ready"), 2 * h + 2)
                if h % 2 == 0 and h >= 4:
                    pe.wait_ge(sem("o_ready"), h // 2 - 1)
                c = h // 2
                v = slice(h // 8 * HD, h // 8 * HD + HD)
                o = ps[h % 2 * HD:h % 2 * HD + HD, 6 + c % 2, 0:SEQ]
                t = pT[h % 2]
                mm(o[:, 0:P], vtok[0:N_META, 0, v], t[0:N_META, 3 * P:4 * P], start=True, stop=False)
                mm(o[:, 0:P], vtok[:, 1, v], t[:, 0:P], start=False, stop=True)
                mm(o[:, P:2 * P], vtok[:, 1, v], t[:, P:2 * P], start=True, stop=False)
                mm(o[:, P:2 * P], vtok[:, 2, v], t[:, 2 * P:3 * P], start=False, stop=True).then_inc(sem("o_done"), 1)

            pe.wait_ge(sem("q_ready"), KD)
            scores(0)
            for g in range(NH // HEADS_PER_GROUP):
                if g + 1 < NH // HEADS_PER_GROUP:
                    scores(g + 1)
                heads = range(HEADS_PER_GROUP * g, HEADS_PER_GROUP * (g + 1))
                for h in heads:
                    values(h)
                    if h > heads[0]:
                        outputs(h - 1)
                outputs(heads[-1])
            for c in range(KD):
                piece = FIRST_PIECE["w_o"] + c // 2
                pe.wait_ge(sem("lo_done"), piece + 1)
                if c >= 4:
                    pe.wait_ge(sem("sq_ready"), SQ0["mixpost1"] + c - 3)
                for k in range(KD):
                    pe.wait_ge(sem("o_ready"), k + 1)
                    at = slice(k * 256 + c % 2 * P, k * 256 + c % 2 * P + P)
                    ins = mm3(ps[:, c % 4, 0:SEQ], (wh[:, piece % 2, at], wl[:, piece % 2, at]),
                              (xh[:, k, 0:SEQ], xl[:, k, 0:SEQ]), k == 0, k == KD - 1)
                ins.then_inc(sem("wo_psum"), 1)
                if c:
                    sum_squares("mixpost1", c - 1, SEQ)
            sum_squares("mixpost1", KD - 1, SEQ)
            ffn_pe(pe, mm3, sum_squares, 1, SEQ)

            for c in range(KD):
                sum_squares("norm1", c, SEQ)
            n = 0
            for i, outs in enumerate(Z_OUT):
                piece = FIRST_PIECE["w_z"] + i
                pe.wait_ge(sem("lo_done"), piece + 1)
                for q, (kind, b) in enumerate(outs):
                    if n >= 4:
                        pe.wait_ge(sem("z_evac"), n - 3)
                    for k in range(KD):
                        pe.wait_ge(sem("x_ready"), 3 * KD + k + 1)
                        if kind in Z_TOKENS:
                            at = slice(k * 256, k * 256 + 256)
                            t = slice(b * P, b * P + P)
                            ins = mm3(ps[:, n % 4, 0:256], (wh[:, i % 2, at], wl[:, i % 2, at]),
                                      (xh[:, k, t], xl[:, k, t]), k == 0, k == KD - 1, swap=True)
                        else:
                            first, m = z_cols(outs, q)
                            at = slice(k * 256 + first, k * 256 + first + m)
                            ins = mm3(ps[0:m, n % 4, 0:SEQ], (wh[:, i % 2, at], wl[:, i % 2, at]),
                                      (xh[:, k, 0:SEQ], xl[:, k, 0:SEQ]), k == 0, k == KD - 1)
                    ins.then_inc(sem("z_psum"), 1)
                    n += 1
            pe.wait_ge(sem("sgu_v"), 1)
            pe.wait_ge(sem("sgw_masked"), 1)
            for g in range(SG):
                ins = mm(ps[:, 7, g * P:(g + 1) * P].rearrange("p (b c) -> p b c", b=NB), sgw[:, g, :],
                         vc[:, :, g * SG_D:(g + 1) * SG_D], start=True, stop=True)
            ins.then_inc(sem("sgu_psum"), 1)
            pe.wait_ge(sem("gate_g"), 1)
            for b in range(NB):
                ins = pe.transpose(ps[:, 5, b * ML_H:(b + 1) * ML_H], gt[0:ML_H, 3, b * P:(b + 1) * P], C("ident", ML_H, ML_H))
            ins.then_inc(sem("gcol_psum"), 1)

            def sb_scores(h):
                rows = slice(h % 2 * HD, h % 2 * HD + HD)
                if h >= 3:
                    pe.wait_ge(sem("sb_exp"), h - 2)
                q, k, z = qaT[rows, h // 2, :], kaT[rows, h // 2, :], ps[:, h % 3, :]
                mm(z[:, 0:SEQ], k[:, 0:P], q, start=True, stop=False, skip_group_check=True)
                mm(z[:, SEQ:3 * P], k[:, P:SEQ], q[:, P:SEQ], start=False, stop=False, skip_group_check=True)\
                    .then_inc(sem("sb_z"), 1)

            def sb_after(h):
                pe.wait_ge(sem("sb_sp"), h + 1)
                z, s = ps[:, h % 3, :], sp[:, h % 2, :]
                mm(z[:, 0:SEQ], C("negtri"), s[:, 0:SEQ], start=False, stop=False, skip_group_check=True)
                mm(z[:, P:SEQ], nones[:, :], s[:, SEQ:3 * P], start=False, stop=False, skip_group_check=True)
                mm(z[:, SEQ:3 * P], C("negtri"), s[:, SEQ:3 * P], start=False, stop=True, skip_group_check=True)\
                    .then_inc(sem("sb_E"), 1)

            def sb_values(h):
                c = h // 2
                pe.wait_ge(sem("sb_a"), h + 1)
                if h == 4:
                    pe.wait_ge(sem("sq_ready"), SQ0["sb_out"] + 1)
                o, w = ps[h % 2 * HD:h % 2 * HD + HD, 3 + c % 2, :], aw[:, h % 2, :]
                v = slice(h * HD, (h + 1) * HD)
                mm(o[:, 0:P], va[:, 0, v], w[:, 0:P], start=True, stop=True)
                mm(o[:, P:SEQ], va[:, 0, v], w[:, P:SEQ], start=True, stop=False)
                mm(o[:, P:SEQ], va[:, 1, v], w[:, SEQ:3 * P], start=False, stop=True).then_inc(sem("sb_o"), 1)

            pe.wait_ge(sem("z_evac"), Z_COUNT)
            for i in range(SB_H + 2):
                if i < SB_H:
                    sb_scores(i)
                if 1 <= i <= SB_H:
                    sb_after(i - 1)
                if i >= 2:
                    sb_values(i - 2)
            pe.wait_ge(sem("sgu_out"), NB)
            for c in range(SG_W // P):
                for b in range(NB):
                    ins = pe.transpose(ps[:, 7, c * SEQ + b * P:c * SEQ + b * P + P], uc[:, b, c * P:(c + 1) * P], ident)
            ins.then_inc(sem("yc_psum"), 1)
            for c in range(SB_C):
                sum_squares("sb_out", c, SEQ)

            pe.wait_ge(sem("cv_ready"), 1)
            pe.wait_ge(sem("em_ready"), 1)
            pe.wait_ge(sem("gcol_ready"), 1)
            pe.wait_ge(sem("yc_ready"), 1)
            pe.wait_ge(sem("sb_exp"), SB_H)
            for h in range(ML_H):
                if h:
                    pe.wait_ge(sem("ml_max"), 2 * h)
                    pe.wait_ge(sem("ml_em"), h)
                mm(ps[:, 5, :], ident[0:ML_H, h:h + 1].to_broadcast([ML_H, P]), gt[0:ML_H, 5:7, :].rearrange("p a t -> p (a t)"),
                   start=True, stop=True).then_inc(sem("ml_bc"), 1)
                if h >= 2:
                    pe.wait_ge(sem("ml_w"), h - 1)
                q, k, s = cv[0:ML_D, h, :], cv[0:ML_D, ML_H + h, :], ps[:, h % 2, :]
                mm(s[:, 0:SEQ], k[:, 0:P], q, start=True, stop=True)
                mm(s[:, SEQ:3 * P], k[:, P:SEQ], q[:, P:SEQ], start=True, stop=True).then_inc(sem("ml_s"), 1)
                pe.wait_ge(sem("ml_w"), h + 1)
                if h:
                    pe.wait_ge(sem("ml_h"), h)
                w, o = aw[:, h % 2, :], ps[0:ML_D, 7, :]
                v = slice(h * ML_D, (h + 1) * ML_D)
                for lhs0, lhs1, at in ((vb[:, 0, v], vb[:, 1, v], 0), (ones[:, 0:ML_D], ones[:, 0:ML_D], SEQ)):
                    mm(o[:, at:at + P], lhs0, w[:, 0:P], start=True, stop=True)
                    mm(o[:, at + P:at + SEQ], lhs0, w[:, P:SEQ], start=True, stop=False)
                    ins = mm(o[:, at + P:at + SEQ], lhs1, w[:, SEQ:3 * P], start=False, stop=True)
                ins.then_inc(sem("ml_num"), 1)
            pe.wait_ge(sem("ml_sq"), 1)
            for b in range(2):
                ins = mm(ps[0:ML_D, b, :].rearrange("p (a t) -> p a t", a=2), ones[0:ML_D, 0:ML_D],
                         mix[0:ML_D, 2 * b:2 * b + 2, 0:SEQ], start=True, stop=True)
            ins.then_inc(sem("ml_ss"), 1)
            pe.wait_ge(sem("ml_r"), 1)
            for c in range(KD):
                piece = FIRST_PIECE["w_out"] + c
                pe.wait_ge(sem("lo_done"), piece + 1)
                if c >= 4:
                    pe.wait_ge(sem("hs_ready"), 4 * KD + c - 3)
                for k, (_, rows) in enumerate(y_chunks()):
                    pe.wait_ge(sem("y_split"), k + 1)
                    at = slice(k * P, (k + 1) * P)
                    ins = mm3(ps[:, c % 4, 0:SEQ], (wh[0:rows, c % 2, at], wl[0:rows, c % 2, at]),
                              (xh[0:rows, k, :], xl[0:rows, k, :]), k == 0, k == 8)
                ins.then_inc(sem("wout_psum"), 1)

            for c in range(KD):
                sum_squares("norm2", c, SEQ)
            for b in range(NB):
                for k in range(KD):
                    pe.wait_ge(sem("xn_ready"), KD + k + 1)
                    ins = mm(ps[:, 0, b * 36:(b + 1) * 36], mix[:, k, b * P:(b + 1) * P], rw[:, k, :],
                             start=(k == 0), stop=(k == KD - 1))
            ins.then_inc(sem("router_psum"), 1)
            for b in range(NB):
                for c in range(KD):
                    q = b * 2 + c // 4
                    ins = pe.transpose(ps[:, 1 + q, c % 4 * P:c % 4 * P + P], mix[:, c, b * P:(b + 1) * P], ident)
                    if c % 4 == 3:
                        ins.then_inc(sem("h2_psum"), 1)
            pe.wait_ge(sem("onehot_ready"), 1)
            oh = onehot
            mm(ps[:, 5, 0:NE], C("strict"), oh(2)[:, 0, :], start=True, stop=True)
            mm(ps[:, 5, NE:2 * NE], ones[:, :], oh(2)[:, 0, :], start=True, stop=False)
            mm(ps[:, 5, NE:2 * NE], C("strict"), oh(2)[:, 1, :], start=False, stop=True)
            mm(ps[:, 5, 2 * NE:3 * NE], ones[:, :], oh(2)[:, 0, :], start=True, stop=False)
            mm(ps[:, 5, 2 * NE:3 * NE], ones[:, :], oh(2)[:, 1, :], start=False, stop=True).then_inc(sem("rank_psum"), 1)
            pe.wait_ge(sem("psel_ready"), 1)
            pe.wait_ge(sem("h2_ready"), 4)
            for c in range(KD):
                if c >= 4:
                    pe.wait_ge(sem("xs_ready" if c % 2 else "xs_ready_d"), c // 2 - 1)
                for b in range(NB):
                    ins = mm(ps[:, c % 4, :], h2[:, b, c * P:(c + 1) * P], psel[:, b, :], start=(b == 0), stop=(b == NB - 1))
                ins.then_inc(sem("xs_psum"), 1)
            pe.wait_ge(sem("combt_ready"), 1)
            for r in range(4):
                for b in range(NB):
                    ins = pe.transpose(ps[:, 6 + r // 2, r % 2 * SEQ + b * P:r % 2 * SEQ + b * P + P],
                                       combt[:, b, r * P:(r + 1) * P], ident)
                if r % 2:
                    ins.then_inc(sem("comb_psum"), 1)
            slot, rnd = tile_at(FIRST["w_proj"])
            pe.wait_ge(sem(f"tile_ready{slot}"), 16 * (rnd + 1))
            wp = ring[:, slot, 0:2048].rearrange("p (k n) -> p k n", k=2)
            pt = ring[:, slot, 2048:2560].rearrange("p (k t) -> p k t", k=2)
            pe.wait_ge(sem("comb_ready"), 2)
            for c in range(KD):
                if c >= 2:
                    pe.wait_ge(sem("pp_ready"), c - 1)
                for k in range(2):
                    ins = mm(ps[:, 4 + c % 2, 0:SEQ], wp[:, k, c * P:(c + 1) * P], pt[:, k, :], start=(k == 0), stop=(k == 1))
                ins.then_inc(sem("pp_psum"), 1)
            pe.wait_ge(sem("pp_ready"), KD)
            pe.wait_ge(sem("xs_ready"), KD // 2)
            pe.wait_ge(sem("xs_ready_d"), KD // 2)
            pe.wait_ge(sem("route_ready"), 2)

            def expert(slot, rnd, e):
                count = pe.value_load(route_i[0:1, 1, bass.ds(e, 1)], min_val=0, max_val=WIDE)
                pe.wait_ge(sem(f"tile_ready{slot}"), rnd * 16 + 16)
                pe.wait_ge(sem("xe_ready"), e + 1)
                if not (type(e) is int and e == 0):
                    pe.wait_ge(sem("ae_ready"), e)
                wg = ring[:, slot, 0:4096].rearrange("p (k n) -> p k n", k=KD)
                wd = ring[:, slot, 4096:6144].rearrange("p (k n) -> p k n", k=2)

                def gate_up(w):
                    for j in range(4):
                        for k in range(KD):
                            ins = mm(ps[:, j // 2, j % 2 * w:j % 2 * w + w], wg[:, k, j * P:(j + 1) * P], xe[slot][:, k, 0:w],
                                     start=(k == 0), stop=(k == KD - 1))
                    ins.then_inc(sem("gu_done"), 1)

                def down(w):
                    for c in range(KD):
                        o = ps[:, 2 + c // 2, c % 2 * w:c % 2 * w + w] if w == WIDE else ps[:, 2, c * w:(c + 1) * w]
                        for k in range(2):
                            ins = mm(o, wd[:, k, c * P:(c + 1) * P], ae[:, k, 0:w], start=(k == 0), stop=(k == 1))
                    ins.then_inc(sem("down_done"), 1)

                with pe.If(count > NARROW):
                    gate_up(WIDE)
                with pe.Else():
                    gate_up(NARROW)
                pe.wait_ge(sem("ae_ready"), e + 1)
                if not (type(e) is int and e == 0):
                    pe.wait_ge(sem("ys_ready"), e)
                with pe.If(count > NARROW):
                    down(WIDE)
                with pe.Else():
                    down(NARROW)

            slot, rnd = tile_at(FIRST["w_exp"])
            expert(slot, rnd, 0)
            ring_steps(pe, "w_exp", expert, first=1)
            pe.wait_ge(sem("ys_ready"), NE)
            for q in range(8):
                for k in range(4):
                    c = q % 2 * 4 + k
                    ins = pe.transpose(ps[:, q, k * P:(k + 1) * P], ysT[:, c, q // 2 * P:(q // 2 + 1) * P], ident)
                ins.then_inc(sem("ysr_psum"), 1)
            pe.wait_ge(sem("ysr_ready_a"), 4)
            pe.wait_ge(sem("ysr_ready"), 4)
            for c in range(KD):
                if c >= 4:
                    pe.wait_ge(sem("hs_ready"), 5 * KD + c - 3)
                for r in range(4):
                    ins = mm(ps[:, c % 4, 0:SEQ], ysr[:, r, c * P:(c + 1) * P], combr[:, r, :], start=(r == 0), stop=(r == 3))
                ins.then_inc(sem("moe_psum"), 1)

            for c in range(KD):
                sum_squares("ple", c, SEQ)
            for c in range(KD):
                piece = FIRST_PIECE["w_ple"] + c // 2
                pe.wait_ge(sem("lo_done"), piece + 1)
                if c >= 4:
                    pe.wait_ge(sem("ple_sig"), c - 3)
                for k in range(KD):
                    pe.wait_ge(sem("x_ready"), 4 * KD + k + 1)
                    at = slice(k * 256 + c % 2 * P, k * 256 + c % 2 * P + P)
                    ins = mm3(ps[:, c % 4, 0:SEQ], (wh[:, piece % 2, at], wl[:, piece % 2, at]),
                              (xh[:, k, 0:SEQ], xl[:, k, 0:SEQ]), k == 0, k == KD - 1)
                ins.then_inc(sem("ple_psum"), 1)
            for c in range(KD):
                sum_squares("final", c, SEQ)

        def normed(dve, dst, src, name, c, r):
            return dve.scalar_tensor_tensor(dst, src, V(name, c), r, ALU.mult, ALU.mult)

        def post_apply(dve, k, norm, n):
            dve.wait_ge(sem("r_ready"), NORM[norm] + 1)
            for c in range(KD):
                dve.wait_ge(sem("mix_ready"), k * KD + c + 1)
                normed(dve, mix[:, c, 0:n], mix[:, c, 0:n], norm, c, r_of(norm)[:, 0:n]).then_inc(sem("delta_ready"), 1)

        def x_low(dve, u, c, full, high, low):
            dve.wait_ge(sem("xh_ready"), u * KD + c + 1)
            dve.tensor_tensor(low, full, high.bitcast(F32), ALU.subtract).then_inc(sem("x_ready"), 1)

        def ffn_dve(dve, l, n, cols):
            gu, dn, pre, post = f"w_gu{l}", f"w_dn{l}", f"ffnpre{l}", f"ffnpost{l}"
            xa, xb = (xhT, xlT) if l == 0 else (xh, xl)
            r = r_of(pre)[:, 0:n]
            for args in halves(gu, 0, PIECE):
                split_lo(dve, gu, *args)
            for c in range(KD):
                dve.wait_ge(sem("xh_ready"), 2 * l * KD + c + 1)
                dve.scalar_tensor_tensor(xb[:, c, 0:n], hs[:, c, cols], V(pre, c), xa[:, c, 0:n].bitcast(F32),
                                         ALU.mult, ALU.subtract).then_inc(sem("x_ready"), 1)
            dve.wait_ge(sem("r_ready"), NORM[pre] + 1)

            def gate(f, j):
                dve.wait_ge(sem("gu_psum"), f + (l * NF + 1))
                dve.tensor_tensor(mix[:, j, 0:n], ps[:, 2 * j, 0:n], r, ALU.mult).then_inc(sem("gr_ready"), 1)

            def up(j):
                dve.tensor_tensor(mix[:, 4 + j, 0:n], ps[:, 2 * j + 1, 0:n], r, ALU.mult).then_inc(sem("up_ready"), 1)

            def body(slot, rnd, i):
                for j in range(2):
                    f = i * 2 + (j - 2)
                    if not (type(i) is int and i == 1):
                        dve.wait_ge(sem("act_ready"), f + (l * NF - 1))
                    gate(f, j)
                    split_lo(dve, gu, slot, rnd, i, j, PIECE)
                    up(j)

            body(*tile_at(FIRST[gu] + 1), 1)
            ring_steps(dve, gu, body, first=2)
            for j in range(2):
                dve.wait_ge(sem("act_ready"), NF - 2 + j + l * NF - 1)
                gate(NF - 2 + j, j)
                up(j)
            for i in range(KD):
                for args in halves(dn, i, FF // 2):
                    split_lo(dve, dn, *args)
            post_apply(dve, 2 * l + 1, post, n)

        def first_of_ties(dve, chain, values, top, order, key, oh):
            n = values.shape[-1]
            chain(dve.tensor_tensor(key, values, top.unsqueeze(2).to_broadcast([P, NB, n]), ALU.is_equal))
            chain(dve.tensor_tensor(key, key, order.unsqueeze(1).to_broadcast([P, NB, n]), ALU.mult))
            chain(dve.tensor_reduce(small[:, 410:412], key, AX.X, ALU.max))
            chain(dve.tensor_tensor(oh, key, small[:, 410:412].unsqueeze(2).to_broadcast([P, NB, n]), ALU.is_equal))

        def routing(dve, chain):
            scr = ysT[:, :, :].rearrange("p a b -> p (a b)")
            width = NGRP + NE
            rl = scr[:, 0:NB * width].rearrange("p (b n) -> p b n", b=NB)
            at = NB * width

            def room(n):
                nonlocal at
                at += NB * n
                return scr[:, at - NB * n:at].rearrange("p (b n) -> p b n", b=NB)

            key4, oh4, el, key, pos, desc = room(NGRP), room(NGRP), room(NE), room(NE), room(NE), scr[:, 1024:1024 + NE]
            gl = small[:, 128:136].rearrange("p (b n) -> p b n", b=NB)
            gmax, gsum, v1, v2, rec = (small[:, 140 + 2 * i:142 + 2 * i] for i in range(5))
            pos1, pos2, w1, w2 = (small[:, 160 + 2 * i:162 + 2 * i] for i in range(4))
            ex = small[:, 180:182]
            dve.wait_ge(sem("router_psum"), 1)
            chain(dve.tensor_tensor(rl, ps[:, 0, 0:NB * width].rearrange("p (b n) -> p b n", b=NB),
                                    R("router_b", width).unsqueeze(1).to_broadcast([P, NB, width]), ALU.add))
            chain(dve.tensor_reduce(gmax, rl[:, :, 0:NGRP], AX.X, ALU.max))
            dve.tensor_tensor(gl, rl[:, :, 0:NGRP], gmax.unsqueeze(2).to_broadcast([P, NB, NGRP]), ALU.subtract)\
               .then_inc(sem("route_g"), 1)
            first_of_ties(dve, chain, rl[:, :, 0:NGRP], gmax, R("desc", NGRP), key4, oh4)
            oh4x = oh4.unsqueeze(3).to_broadcast([P, NB, NGRP, EPG])
            el4 = el.rearrange("p b (g e) -> p b g e", e=EPG)
            key44 = key.rearrange("p b (g e) -> p b g e", e=EPG)
            chain(dve.tensor_scalar(key44, oh4x, 3e38, -3e38, ALU.mult, ALU.add))
            chain(dve.tensor_tensor(el4, rl[:, :, NGRP:].rearrange("p b (g e) -> p b g e", e=EPG), oh4x, ALU.mult))
            chain(dve.tensor_tensor(el, el, key, ALU.add))
            dve.wait_ge(sem("iota_ready"), 1)
            chain(dve.tensor_scalar(desc, iota[:, 0:NE], -1.0, float(NE), ALU.mult, ALU.add))
            chain(dve.tensor_reduce(v1, el, AX.X, ALU.max))
            first_of_ties(dve, chain, el, v1, desc, key, onehot(0))
            chain(dve.scalar_tensor_tensor(el, onehot(0), -3e38, el, ALU.mult, ALU.add))
            chain(dve.tensor_reduce(v2, el, AX.X, ALU.max))
            first_of_ties(dve, chain, el, v2, desc, key, onehot(1))
            dve.tensor_tensor(onehot(2), onehot(0), onehot(1), ALU.add).then_inc(sem("onehot_ready"), 1)
            dve.tensor_tensor(ex, v2, v1, ALU.subtract).then_inc(sem("route_d"), 1)
            dve.wait_ge(sem("rank_psum"), 1)
            count, incl = scr[:, 1100:1100 + NE], scr[:, 1200:1200 + NE]
            chain(dve.tensor_copy(count, ps[:, 5, 2 * NE:3 * NE]))
            chain(dve.tensor_tensor_scan(incl, count, count, 0.0, ALU.add, ALU.max))
            chain(dve.tensor_tensor(incl, incl, count, ALU.subtract))
            dve.tensor_copy(route_i[:, 0, :], incl).then_inc(sem("route_ready"), 1)
            dve.tensor_copy(route_i[:, 1, :], count).then_inc(sem("route_ready"), 1)
            chain(dve.tensor_tensor(pos, ps[:, 5, 0:NB * NE].rearrange("p (b e) -> p b e", b=NB),
                                    incl.unsqueeze(1).to_broadcast([P, NB, NE]), ALU.add))
            for oh, p in ((onehot(0), pos1), (onehot(1), pos2)):
                chain(dve.tensor_tensor(key, oh, pos, ALU.mult))
                chain(dve.tensor_reduce(p, key, AX.X, ALU.add))
            for b in range(NB):
                chain(dve.tensor_scalar(psel[:, b, :], iota[:, :], pos1[:, b:b + 1], None, ALU.is_equal))
                ins = dve.scalar_tensor_tensor(psel[:, b, :], iota[:, :], pos2[:, b:b + 1], psel[:, b, :],
                                               ALU.is_equal, ALU.add)
                if b == 0:
                    chain(ins)
            ins.then_inc(sem("psel_ready"), 1)
            dve.wait_ge(sem("route_gexp"), 1)
            dve.wait_ge(sem("route_ex"), 1)
            chain(dve.tensor_reduce(gsum, gl, AX.X, ALU.add))
            chain(dve.tensor_scalar(rec, ex, 1.0, None, ALU.add))
            chain(dve.tensor_tensor(rec, rec, gsum, ALU.mult))
            chain(dve.reciprocal(w1, rec))
            chain(dve.tensor_tensor(w2, ex, w1, ALU.mult))
            second = scr[:, 1536:1536 + ROWS]
            for b in range(NB):
                chain(dve.tensor_scalar(combt[:, b, :], iota[:, :], pos1[:, b:b + 1], w1[:, b:b + 1], ALU.is_equal, ALU.mult))
                chain(dve.tensor_scalar(second, iota[:, :], pos2[:, b:b + 1], w2[:, b:b + 1], ALU.is_equal, ALU.mult))
                ins = dve.tensor_tensor(combt[:, b, :], combt[:, b, :], second, ALU.add)
                if b == 0:
                    chain(ins)
            ins.then_inc(sem("combt_ready"), 1)

        @block.vector
        def _(dve):
            chain = Chain(dve, "dve_chain")
            dve.wait_ge(sem("consts_loaded"), 32)
            dve.wait_ge(sem("hs_loaded"), 16)
            dve.wait_ge(sem("r_ready"), 1)
            for c in range(KD):
                normed(dve, hp[:, c, PADT:], hs[:, c, :], "mixpre0", c, r_of("mixpre0")).then_inc(sem("h_ready"), 1)
            pool_groups(dve, chain, (2, 3), "p_dve")
            post_apply(dve, 0, "mixpost0", T)
            ffn_dve(dve, 0, T, slice(0, T))

            dve.wait_ge(sem("r_ready"), NORM["pre1"] + 1)
            dve.wait_ge(sem("dn_psum"), 2 * KD)
            r = r_of("pre1")
            for c in range(KD):
                normed(dve, mix[:, c, :], hs[:, c, :], "kv_norm", c, r).then_inc(sem("kvin_ready"), 1)
            for c in range(KD):
                normed(dve, h1[:, c, :], hs[:, c, N_META:], "mixpre1", c, r[:, N_META:]).then_inc(sem("h1_ready"), 1)
            for x in halves("w_q", 0, PIECE):
                split_lo(dve, "w_q", *x)
            for c in range(KD):
                x_low(dve, 1, c, h1[:, c, :], xh[:, c, :], xl[:, c, :])
            dve.wait_ge(sem("tables_loaded"), 64)
            dve.wait_ge(sem("kv_psum"), 3)
            b_v = R("b_v", P)
            dve.tensor_tensor(vtok[0:N_META, 0, :], ps[0:N_META, 2, 0:P], b_v[0:N_META, :], ALU.add).then_inc(sem("v_ready"), 1)
            dve.tensor_tensor(vtok[:, 1:3, :], ps[:, 2, P:3 * P].rearrange("p (b n) -> p b n", b=NB),
                              b_v.unsqueeze(1).to_broadcast([P, NB, P]), ALU.add).then_inc(sem("v_ready"), 1)
            low = {1: ("w_q", halves("w_q", 1, PIECE)[0]), 3: ("w_q", halves("w_q", 1, PIECE)[1]),
                   5: ("w_o", halves("w_o", 0, PIECE)[0]), 7: ("w_o", halves("w_o", 0, PIECE)[1])}
            for c in range(KD):
                dve.wait_ge(sem("q_psum"), c + 1)
                dve.tensor_scalar(qT[:, c, :].rearrange("p (b q) -> p b q", q=P)[:, :, ::-1],
                                  ps[:, c % 4, 0:SEQ].rearrange("p (b q) -> p b q", q=P), V("b_q", c), HD ** -0.5,
                                  ALU.add, ALU.mult).then_inc(sem("q_ready"), 1)
                if c in low:
                    split_lo(dve, low[c][0], *low[c][1])

            PER = NB * HEADS_PER_GROUP

            def logits(g):
                if g == 0:
                    dve.wait_ge(sem("bias_ready"), 16)
                for i in range(PER * g, PER * (g + 1)):
                    n, first = (N_META + P, P - N_META) if i % 2 == 0 else (2 * P, 0)
                    dve.wait_ge(sem("s_psum"), i + 1)
                    dve.tensor_tensor_reduce(out=lg[g % 2][:, i % PER, 0:n], in0=ps[:, i % 4, 0:n],
                                             in1=brev[:, i // 2, first:SEQ], scale=1.0, scalar=-3e38,
                                             op0=ALU.add, op1=ALU.max, accum_out=small[:, i:i + 1])\
                       .then_inc(sem("lg_ready"), 1)
                k = PER * g
                dve.wait_ge(sem("lg_ready"), PER * (g + 1))
                m = small[:, k:k + PER].rearrange("p (h b) -> p h b", b=NB)
                sink = R("sinks", HEADS_PER_GROUP, HEADS_PER_GROUP * g).unsqueeze(2).to_broadcast([P, HEADS_PER_GROUP, NB])
                chain(dve.tensor_tensor(m, m, sink, ALU.max))
                chain(dve.tensor_tensor(small[:, 64 + k:64 + k + PER].rearrange("p (h b) -> p h b", b=NB), sink, m, ALU.subtract))
                dve.tensor_scalar(small[:, 32 + k:32 + k + PER], small[:, k:k + PER], -1.0, None, ALU.mult)\
                   .then_inc(sem("negm_ready"), 1)

            GROUPS = NH // HEADS_PER_GROUP
            logits(0)
            for g in range(GROUPS):
                if g + 1 < GROUPS:
                    if g:
                        dve.wait_ge(sem("pt_psum"), HEADS_PER_GROUP * g)
                    logits(g + 1)
                k = PER * g
                dve.wait_ge(sem("exp_ready"), (PER + 1) * (g + 1))
                den = small[:, 96 + k:96 + k + PER]
                chain(dve.tensor_tensor(den, den, small[:, 64 + k:64 + k + PER], ALU.add))
                chain(dve.reciprocal(den, den))
                for i in range(PER):
                    n = N_META + P if i % 2 == 0 else 2 * P
                    v = lg[g % 2][:, i, 0:n]
                    dve.tensor_scalar(v, v, den[:, i:i + 1], None, ALU.mult).then_inc(sem("p_ready"), 1)
                for h in range(HEADS_PER_GROUP * g, HEADS_PER_GROUP * (g + 1)):
                    if h % 2 == 1:
                        c = h // 2
                        dve.wait_ge(sem("oh_ready"), c + 1)
                        o = ps[:, 6 + c % 2, 0:SEQ].rearrange("p (b q) -> p b q", q=P)[:, :, ::-1]
                        dve.tensor_tensor(xl[:, c, :].rearrange("p (b q) -> p b q", q=P), o,
                                          xh[:, c, :].bitcast(F32).rearrange("p (b q) -> p b q", q=P), ALU.subtract)\
                           .then_inc(sem("o_ready"), 1)
            for x in halves("w_o", 1, PIECE):
                split_lo(dve, "w_o", *x)
            post_apply(dve, 2, "mixpost1", SEQ)
            ffn_dve(dve, 1, SEQ, slice(N_META, T))

            for x in halves("w_z", 0, PIECE):
                split_lo(dve, "w_z", *x)

            def norm_input(name):
                dve.wait_ge(sem("r_ready"), NORM[name] + 1)
                for c in range(KD):
                    normed(dve, mix[:, c, 0:SEQ], hs[:, c, N_META:], name, c, r_of(name)[:, 0:SEQ])\
                        .then_inc(sem("xn_ready"), 1)

            norm_input("norm1")
            for c in range(KD):
                x_low(dve, 3, c, mix[:, c, 0:SEQ], xh[:, c, :], xl[:, c, :])
            for piece in range(2, 14):
                split_lo(dve, "w_z", *halves("w_z", piece // 2, PIECE)[piece % 2])
                if piece >= 4 and piece - 4 < 2 * ML_H:
                    conv(dve, chain, piece - 4, "conv_done")

            dve.wait_ge(sem("z_evac"), Z_COUNT)
            groups = vc.rearrange("p b (g c) -> p (b g) c", c=SG_D)
            NG = NB * SG
            chain(dve.tensor_reduce(small[:, 0:NG], groups, AX.X, ALU.add))
            dve.scalar_tensor_tensor(groups, small[:, 0:NG].unsqueeze(2).to_broadcast([P, NG, SG_D]), -1.0 / SG_D, groups,
                                     ALU.mult, ALU.add).then_inc(sem("sgu_centred"), 1)
            g4 = [gt[0:ML_H, i, :] for i in range(7)]
            dve.wait_ge(sem("gate_ln"), 1)
            chain(dve.tensor_scalar(g4[1], g4[1], 0.0, None, ALU.min))
            chain(dve.tensor_tensor_scan(g4[4], g4[1], g4[2], 0.0, ALU.add, ALU.subtract))
            dve.tensor_tensor(g4[3], g4[0], g4[4], ALU.subtract).then_inc(sem("gate_g"), 1)
            dve.wait_ge(sem("gate_g"), 1)
            chain(dve.tensor_tensor_scan(g4[5], g4[3], g4[3], 0.0, ALU.max, ALU.max))
            dve.tensor_tensor(g4[6], g4[4], g4[5], ALU.add).then_inc(sem("gate_m"), 1)
            dve.wait_ge(sem("sgu_sq"), 1)
            dve.tensor_reduce(small[:, 8:8 + NG].rearrange("p (b g) -> p b g", g=SG),
                              mix[:, 0:2, 0:SG_W].rearrange("p b (g c) -> p b g c", c=SG_D), AX.X, ALU.add)\
               .then_inc(sem("sgu_var"), 1)
            dve.wait_ge(sem("ob_exp"), 1)
            chain(dve.tensor_scalar(ob[0:ML_D, :, :], ob[0:ML_D, :, :], 1.0, None, ALU.add))
            chain(dve.reciprocal(ob[0:ML_D, :, :], ob[0:ML_D, :, :]))
            dve.wait_ge(sem("sgu_r"), 1)
            chain(dve.tensor_tensor(groups, groups, small[:, 8:8 + NG].unsqueeze(2).to_broadcast([P, NG, SG_D]), ALU.mult))
            chain(dve.tensor_tensor(vc, vc, R("ln_g", SG_W).unsqueeze(1).to_broadcast([P, NB, SG_W]), ALU.mult))
            dve.tensor_tensor(vc, vc, R("ln_b", SG_W).unsqueeze(1).to_broadcast([P, NB, SG_W]), ALU.add)\
               .then_inc(sem("sgu_v"), 1)
            dve.wait_ge(sem("gcol_psum"), 1)
            dve.tensor_copy(small[:, 20:20 + NB * ML_H], ps[:, 5, 0:NB * ML_H]).then_inc(sem("gcol_ready"), 1)
            dve.wait_ge(sem("sgu_psum"), 1)
            for g in range(SG):
                u = uc[:, :, g * SG_D:(g + 1) * SG_D]
                dve.scalar_tensor_tensor(u, ps[:, 7, g * P:(g + 1) * P].rearrange("p (b c) -> p b c", b=NB), V("sgu_b", g), u,
                                         ALU.add, ALU.mult).then_inc(sem("sgu_y"), 1)
            dve.wait_ge(sem("sgu_yr"), 1)
            for b in range(NB):
                dve.scalar_tensor_tensor(uc[:, b, :], uc[:, b, :], small[:, 16 + b:17 + b], R("sgu_out", SG_W),
                                         ALU.mult, ALU.mult).then_inc(sem("sgu_out"), 1)

            for i in range(SB_H):
                dve.wait_ge(sem("sb_ln"), i + 1)
                if i >= 2:
                    dve.wait_ge(sem("sb_E"), i - 1)
                s = sp[:, i % 2, :]
                chain(dve.scalar_tensor_tensor(s, ps[:, i % 3, 0:3 * P], 0.0, e1[:, i % 2, :], ALU.max, ALU.add))
                diag = s.rearrange("p (a b) -> p a b", a=3)[:, 0:3:2, :]
                dve.tensor_tensor(diag, diag, C("strict").unsqueeze(1).to_broadcast([P, 2, P]), ALU.mult)\
                   .then_inc(sem("sb_sp"), 1)

            for h in range(ML_H):
                dve.wait_ge(sem("ml_bc"), h + 1)
                for b, cols in ((0, slice(0, SEQ)), (1, slice(SEQ, 3 * P))):
                    at = 20 + ML_H * b + h
                    dve.tensor_scalar(sp[:, h % 2, cols], ps[:, 5, b * P:SEQ], small[:, at:at + 1], None, ALU.max)\
                       .then_inc(sem("ml_max"), 1)
                dve.wait_ge(sem("ml_s"), h + 1)
                dve.wait_ge(sem("ml_d"), h + 1)
                w = aw[:, h % 2, :]
                dve.scalar_tensor_tensor(w, ps[:, h % 2, 0:3 * P], ML_D ** -0.5, w, ALU.mult, ALU.mult)\
                   .then_inc(sem("ml_w"), 1)
                dve.wait_ge(sem("ml_num"), h + 1)
                dve.wait_ge(sem("ml_em"), h + 1)
                den = e1[0:ML_D, h % 2, 0:SEQ]
                raw = ps[0:ML_D, 7, SEQ:2 * SEQ]
                chain(dve.tensor_tensor(den, raw, den, ALU.max))
                chain(dve.scalar_tensor_tensor(den, raw, -1.0, den, ALU.mult, ALU.max))
                chain(dve.reciprocal(den, den))
                dve.tensor_tensor(yb[0:ML_D, h, :], ps[0:ML_D, 7, 0:SEQ], den, ALU.mult).then_inc(sem("ml_h"), 1)
            for x in halves("w_out", 0, 9 * P):
                split_lo(dve, "w_out", *x)
            dve.wait_ge(sem("r_ready"), NORM["sb_out"] + 1)
            dve.wait_ge(sem("ya_ready"), SB_C)
            for c in range(SB_C):
                normed(dve, yaT[:, c, :], yaT[:, c, :], "sb_out", c, r_of("sb_out")[:, 0:SEQ]).then_inc(sem("y_fin"), 1)
            dve.wait_ge(sem("ml_r"), 1)
            for h in range(ML_H):
                y = yb[0:ML_D, h, :]
                chain(dve.scalar_tensor_tensor(y, y, V("mnorm", h, ML_D), mix[0:ML_D, ML_H + h, 0:SEQ], ALU.mult, ALU.mult))
                dve.tensor_tensor(y, y, ob[0:ML_D, h, :], ALU.mult).then_inc(sem("y_fin"), 1)
            for j, (src, rows) in enumerate(y_chunks()):
                dve.wait_ge(sem("yh_ready"), j + 1)
                dve.tensor_tensor(xl[0:rows, j, :], src, xh[0:rows, j, :].bitcast(F32), ALU.subtract)\
                   .then_inc(sem("y_split"), 1)
            for c in range(KD):
                if c + 2 < KD:
                    split_lo(dve, "w_out", *halves("w_out", (c + 2) // 2, 9 * P)[c % 2])
                dve.wait_ge(sem("wout_psum"), c + 1)
                dve.tensor_tensor(hs[:, c, N_META:], hs[:, c, N_META:], ps[:, c % 4, 0:SEQ], ALU.add)\
                   .then_inc(sem("hs_ready"), 1)

            norm_input("norm2")
            routing(dve, chain)
            for c in range(0, KD, 2):
                dve.wait_ge(sem("xs_psum"), c + 1)
                dve.tensor_copy(xsT[:, c, 0:ROWS], ps[:, c % 4, :]).then_inc(sem("xs_ready_d"), 1)

            def expert(slot, rnd, e):
                start = dve.value_load(route_i[0:1, 0, bass.ds(e, 1)], min_val=0, max_val=ROWS)
                count = dve.value_load(route_i[0:1, 1, bass.ds(e, 1)], min_val=0, max_val=WIDE)
                with dve.If(count > NARROW):
                    dve.wait_ge(sem("sg_ready"), e + 1)
                    dve.tensor_tensor(ae[:, :, :], sgate[:, :, :], ps[:, 1, :].rearrange("p (a b) -> p a b", b=WIDE), ALU.mult)\
                       .then_inc(sem("ae_ready"), 1)
                with dve.Else():
                    dve.wait_ge(sem("sg_ready"), e + 1)
                    dve.tensor_tensor(ae[:, :, 0:NARROW], sgate[:, :, 0:NARROW],
                                      ps[:, 1, 0:2 * NARROW].rearrange("p (a b) -> p a b", b=NARROW), ALU.mult)\
                       .then_inc(sem("ae_ready"), 1)
                with dve.If(count > NARROW):
                    dve.wait_ge(sem("down_done"), e + 1)
                    dve.tensor_copy(ysT[:, :, bass.ds(start, WIDE)],
                                    ps[:, 2:6, :].rearrange("p a (b n) -> p (a b) n", n=WIDE)).then_inc(sem("ys_ready"), 1)
                with dve.Else():
                    dve.wait_ge(sem("down_done"), e + 1)
                    dve.tensor_copy(ysT[:, :, bass.ds(start, NARROW)],
                                    ps[:, 2, :].rearrange("p (c n) -> p c n", n=NARROW)).then_inc(sem("ys_ready"), 1)

            ring_steps(dve, "w_exp", expert)
            for q in range(0, 8, 2):
                dve.wait_ge(sem("ysr_psum"), q + 1)
                dve.tensor_copy(ysr[:, q // 2, 0:512], ps[:, q, :]).then_inc(sem("ysr_ready"), 1)
            for c in range(KD):
                dve.wait_ge(sem("moe_psum"), c + 1)
                dve.tensor_tensor(hs[:, c, N_META:], hs[:, c, N_META:], ps[:, c % 4, 0:SEQ], ALU.add)\
                   .then_inc(sem("hs_ready"), 1)

            for x in halves("w_ple", 0, PIECE):
                split_lo(dve, "w_ple", *x)
            norm_input("ple")
            for c in range(KD):
                x_low(dve, 4, c, mix[:, c, 0:SEQ], xh[:, c, :], xl[:, c, :])
            for c in range(KD):
                if c in (0, 2):
                    split_lo(dve, "w_ple", *halves("w_ple", 1, PIECE)[c // 2])
                dve.wait_ge(sem("ple_sig"), c + 1)
                dve.wait_ge(sem("pp_ready"), KD)
                dve.tensor_tensor(mix[:, c, 0:SEQ], mix[:, c, 0:SEQ], ppT[:, c, :], ALU.mult).then_inc(sem("delta_ready"), 1)
            dve.wait_ge(sem("r_ready"), NORM["final"] + 1)
            for c in range(KD):
                normed(dve, mix[:, c, 0:SEQ], hs[:, c, N_META:], "final", c, r_of("final")[:, 0:SEQ])\
                    .then_inc(sem("out_ready"), 1)


def _pieces(w, cols):
    import numpy as _np
    n = w.shape[1] // cols
    x = w.reshape(w.shape[0] // P, P, n // 2, 2, cols)
    return _np.ascontiguousarray(x.transpose(2, 1, 3, 0, 4)).reshape(n // 2, P, -1)


def _t5_buckets():
    import math
    import numpy as _np
    n, far = 32, 128
    half = n // 2
    d = _np.arange(P)
    df = _np.maximum(d, 1).astype(_np.float32)
    large = half + (_np.log(df / _np.float32(half)) / _np.float32(math.log(far / half))
                    * _np.float32(n - half)).astype(_np.int32)
    return _np.where(d < half, d, _np.minimum(large, n - 1))


def kernel(**inputs):
    import numpy as _np
    import concourse.bacc as _bacc
    from concourse import mybir as _mybir
    from concourse.bass_utils import run_bass_kernel_spmd as _run

    x = {k: _np.asarray(v) for k, v in inputs.items()}
    f32 = _np.float32
    a = {}
    seq = _np.concatenate([x["meta_tokens"], x["x"][0]], axis=0)
    a["hT"] = seq.T.reshape(KD, P, T).transpose(1, 0, 2)

    vec = _np.zeros((P, NV), f32)

    def put(name, v, rows=P):
        v = v.reshape(-1, rows).T
        vec[0:rows, VCOL[name]:VCOL[name] + v.shape[1]] = v

    for l in range(2):
        put(f"mixpre{l}", x["norm_mix_pre"][l])
        put(f"mixpost{l}", x["norm_mix_post"][l])
        put(f"ffnpre{l}", x["norm_ffn_pre"][l])
        put(f"ffnpost{l}", x["norm_ffn_post"][l])
    put("kv_norm", x["kv_norm"])
    put("pool_scale", x["pool_scale"][0])
    put("norm1", x["norm1_g_2"][0])
    put("norm2", x["norm2_g_2"][0])
    put("ple", x["ple_norm_g_2"][0])
    put("final", x["final_g_2"])
    put("b_q", x["b_q"][0])
    put("b_o", x["b_o"][0])
    put("b_k", _np.concatenate([x["b_k"][0:HD], x["b_k"][0:HD], x["b_k"][HD:], x["b_k"][HD:]]))
    put("sb_out", x["sb_out_g_2"][0])
    put("conv_w", x["conv_w_2"][0].reshape(4, 2 * ML_H, ML_D).transpose(1, 0, 2), ML_D)
    put("conv_b", x["conv_b_2"][0], ML_D)
    put("mnorm", x["mnorm_g_2"][0], ML_D)
    put("igate_b", x["igate_b_2"][0], ML_H)
    put("fgate_b", x["fgate_b_2"][0], ML_H)
    put("sgu_b", x["sgu_b_2"][0])
    a["vec"] = vec

    row = _np.concatenate([x["sinks"][0], x["b_v"], x["sgu_ln_g_2"][0], x["sgu_ln_b_2"][0], x["sgu_out_g_2"][0],
                           x["router_gb_2"][0], x["router_eb_2"][0], _np.arange(NGRP, 0, -1).astype(f32)])
    a["row"] = _np.broadcast_to(row[None], (P, NR))

    cst = _np.zeros((P, NC), f32)
    i, j = _np.arange(P)[:, None], _np.arange(P)[None, :]
    cst[:, CCOL["ident"]:CCOL["ident"] + P] = i == j
    cst[:, CCOL["strict"]:CCOL["strict"] + P] = i < j
    cst[:, CCOL["negtri"]:CCOL["negtri"] + P] = -(i >= j).astype(f32)
    cst[:, CCOL["sgumask"]:CCOL["sgumask"] + P] = i // 64 <= j // 64
    for g, w in enumerate(WINDOWS):
        at = CCOL["invcnt"] + g * PADT
        cst[:, at:at + PADT] = f32(1) / _np.minimum(_np.arange(1, PADT + 1), w).astype(f32)
    cst[0:32, CCOL["buckets"]:CCOL["buckets"] + P] = _np.arange(32)[:, None] == _t5_buckets()[::-1][None, :]
    a["cst"] = cst
    a["rel_bias"] = x["rel_bias"]
    rw = _np.concatenate([x["router_gw_2"][0], x["router_ew_2"][0]], axis=1)
    a["rw"] = rw.reshape(KD, P, -1).transpose(1, 0, 2)
    a["sgw"] = x["sgu_w_2"][0].transpose(2, 0, 1)

    a["w_pool"] = x["pool_w"][0].reshape(4, 2, P, 256).transpose(2, 0, 1, 3).reshape(1, P, 2048)
    for l in range(2):
        gu = x["w_gate_up"][l].reshape(KD, P, 2, NF // 2, 2, P)
        a[f"w_gu{l}"] = gu.transpose(3, 1, 4, 0, 2, 5).reshape(NF // 2, P, 4096)
        dn = x["w_down"][l].reshape(NF, P, KD, P)
        a[f"w_dn{l}"] = dn.transpose(2, 1, 0, 3).reshape(KD, P, FF)
    wk = x["w_k"]
    kv = _np.concatenate([wk[:, 0:HD], wk[:, 0:HD], wk[:, HD:], wk[:, HD:], x["w_v"]], axis=1)
    a["w_kv"] = kv.reshape(KD, P, 384).transpose(1, 0, 2).reshape(1, P, 3072)
    a["w_q"] = _pieces(x["w_q"][0], 256)
    a["w_o"] = _pieces(x["w_o"][0], 256)
    a["w_ple"] = _pieces(x["ple_gate_w_2"][0], 256)
    w = x["w_in_2"][0]
    at, part = 0, {}
    for name, n in (("qa", SB_W), ("ka", SB_W), ("va", SB_W), ("qb", 384), ("kb", 384), ("vb", 384), ("ob", 384),
                    ("i", ML_H), ("f", ML_H), ("uc", SG_W), ("vc", SG_W)):
        part[name] = w[:, at:at + n]
        at += n

    def pad(*cols):
        c = _np.concatenate(cols, axis=1)
        return _np.concatenate([c, _np.zeros((D, 256 - c.shape[1]), f32)], axis=1)

    ob = part["ob"]
    z = [pad(part[n][:, s:s + 192]) for n in ("qb", "kb") for s in (0, 192)] + [
        pad(ob[:, 0:192]), pad(part["i"], ob[:, 192:288], part["f"], ob[:, 288:384]),
        part["qa"][:, 0:256], pad(part["qa"][:, 256:], part["ka"][:, 0:128]), part["ka"][:, 128:],
        part["va"][:, 0:256], pad(part["va"][:, 256:], part["vb"][:, 0:128]), part["vb"][:, 128:],
        part["uc"], part["vc"]]
    a["w_z"] = _pieces(_np.concatenate(z, axis=1), 256)
    wo = x["w_out_2"][0]
    chunks = [wo[c * P:(c + 1) * P] for c in range(SB_C)]
    chunks += [_np.concatenate([wo[SB_W + h * ML_D:SB_W + (h + 1) * ML_D], _np.zeros((P - ML_D, D), f32)]) for h in range(ML_H)]
    chunks += [wo[768 + c * P:768 + (c + 1) * P] for c in range(2)]
    a["w_out"] = _np.stack(chunks).reshape(9, P, 4, 2, P).transpose(2, 1, 3, 0, 4).reshape(4, P, 2304)
    pj = x["ple_proj_w_2"][0].reshape(2, P, D).transpose(1, 0, 2).reshape(P, 2048)
    pT = x["p_2"][0, 0].T.reshape(2, P, SEQ).transpose(1, 0, 2).reshape(P, 512)
    a["w_proj"] = _np.concatenate([pj, pT], axis=1)[None]
    gu = _np.concatenate([x["w_gate_2"][0], x["w_up_2"][0]], axis=2)
    gu = gu.reshape(NE, KD, P, 512).transpose(0, 2, 1, 3).reshape(NE, P, 4096)
    dn = x["w_down_2"][0].reshape(NE, 2, P, D).transpose(0, 2, 1, 3).reshape(NE, P, 2048)
    a["w_exp"] = _np.concatenate([gu, dn], axis=2)

    nc = _bacc.Bacc("TRN2", target_bir_lowering=False, num_devices=1)
    arrays, args = {}, {}
    for name, v in a.items():
        v = _np.ascontiguousarray(v)
        arrays[f"in_{name}"] = v
        args[name] = nc.dram_tensor(f"in_{name}", v.shape, _mybir.dt.from_np(v.dtype), kind="ExternalInput").ap()
    out = nc.dram_tensor("out_y", (P, KD, SEQ), _mybir.dt.float32, kind="ExternalOutput").ap()
    bass_two_blocks(nc, args, out)
    got = _run(nc, [arrays], core_ids=[0]).results[0]["out_y"]
    return got.transpose(2, 1, 0).reshape(1, SEQ, D)
```

```python
import numpy as np
import concourse.bass as bass
from concourse import mybir
from contextlib import ExitStack

F32 = mybir.dt.float32
F32R = mybir.dt.float32r
I32 = mybir.dt.int32
ACT = mybir.ActivationFunctionType
ALU = mybir.AluOpType
AX = mybir.AxisListType

P = 128
D = 1024
KD = D // P
N_META = 16
SEQ = 256
T = N_META + SEQ
NB = SEQ // P
FF = 2816
NF = FF // P
WINDOWS = (2, 4, 8, 16)
PADT = max(WINDOWS)
NH = 16
HD = 64
HEADS_PER_GROUP = 4
EPS = 1e-6
NEG = -1e30
SB_H = 6
SB_W = SB_H * HD
SB_C = SB_W // P
ML_H = 4
ML_D = 96
SG = 4
SG_D = 64
SG_W = SG * SG_D
NE = 32
NGRP = 4
EPG = NE // NGRP
ROWS = 2 * SEQ
HALF = P
FEW = 32
XS = ROWS + FEW
XS_ALL = (KD - 1) * XS + ROWS + SEQ
WIDE = SEQ
EPIECE = 1024
EPIECES = 6
EBUFS = 3
FE = 256

SLOTS = 3
SLOT = 6144
PIECE = 2048
STREAM = [("w_pool", 1, 2048), ("w_gu0", NF // 2, 4096), ("w_dn0", KD, FF), ("w_kv", 1, 3072),
          ("w_q", 2, 4096), ("w_o", 2, 4096), ("w_gu1", NF // 2, 4096), ("w_dn1", KD, FF),
          ("w_z", 7, 4096), ("w_out", 4, 2304), ("w_proj", 1, 2560), ("w_exp", NE, SLOT),
          ("w_ple", 2, 4096)]
UNSPLIT = ("w_pool", "w_kv", "w_proj", "w_exp")
FIRST, FIRST_PIECE = {}, {}


def tile_of(name, i):
    return FIRST[name] + i


_t = _p = 0
for _name, _n, _ in STREAM:
    FIRST[_name], FIRST_PIECE[_name] = _t, _p
    _t += _n
    _p += 0 if _name in UNSPLIT else 2 * _n

NORMS = [("mixpre0", 8), ("mixpost0", 8), ("ffnpre0", 8), ("ffnpost0", 8), ("pre1", 8),
         ("mixpost1", 8), ("ffnpre1", 8), ("ffnpost1", 8), ("norm1", 8), ("sb_out", SB_C),
         ("norm2", 8), ("ple", 8), ("final", 8)]
NORM, SQ0 = {}, {}
_s = 0
for _i, (_name, _n) in enumerate(NORMS):
    NORM[_name], SQ0[_name] = _i, _s
    _s += _n

VECS = [("mixpre0", 8), ("mixpost0", 8), ("ffnpre0", 8), ("ffnpost0", 8), ("mixpre1", 8),
        ("mixpost1", 8), ("ffnpre1", 8), ("ffnpost1", 8), ("kv_norm", 8), ("pool_scale", 8),
        ("norm1", 8), ("norm2", 8), ("ple", 8), ("final", 8), ("b_q", 8), ("b_o", 8), ("b_k", 2),
        ("sb_out", SB_C), ("conv_w", 32), ("conv_b", 8), ("mnorm", ML_H), ("igate_b", 1),
        ("fgate_b", 1), ("sgu_b", SG)]
VCOL, NV = {}, 0
for _name, _n in VECS:
    VCOL[_name] = NV
    NV += _n
ROWV = [("sinks", NH), ("b_v", 128), ("ln_g", SG_W), ("ln_b", SG_W), ("sgu_out", SG_W),
        ("router_b", NGRP + NE), ("desc", NGRP)]
RCOL, NR = {}, 0
for _name, _n in ROWV:
    RCOL[_name] = NR
    NR += _n
CONST = [("ident", P), ("strict", P), ("negtri", P), ("sgumask", P),
         ("invcnt", len(WINDOWS) * PADT), ("buckets", P)]
CCOL, NC = {}, 0
for _name, _n in CONST:
    CCOL[_name] = NC
    NC += _n

Z_OUT = [[("conv", 0), ("conv", 1)], [("conv", 2), ("conv", 3)], [("conv", 4), ("conv", 5)],
         [("conv", 6), ("conv", 7)], [("ob", 0), ("ob", 1)],
         [("gate", 0), ("ob", 2), ("gate", 1), ("ob", 3)], [("qa", 0), ("qa", 1)],
         [("qa", 2), ("ka", 0)], [("ka", 1), ("ka", 2)], [("va", 0), ("va", 1)],
         [("vab", 0), ("vab", 1)], [("vb", 0), ("vb", 1)], [("uc", 0), ("uc", 1)], [("vc", 0), ("vc", 1)]]
Z_TOKENS = ("va", "vab", "vb", "uc", "vc")
Z_COUNT = sum(len(x) for x in Z_OUT)
GATE_AT = [(0, ML_H + ML_D), (ML_H, ML_D), (ML_H + ML_D, ML_H + ML_D), (2 * ML_H + ML_D, ML_D)]


def bass_two_blocks(nc, a, out):
    y_rows = nc.dram_tensor("y_rows", (ROWS + WIDE, D), F32, kind="Internal").ap()
    bias_rows = nc.dram_tensor("bias_rows", (NH, 3 * P), F32, kind="Internal").ap()

    ctx = ExitStack()
    with ctx:
        def sb(name, shape, dt=F32, within=None):
            return (within or ctx).enter_context(nc.sbuf_tensor(name, shape, dt))

        sems = {}

        def sem(name):
            if name not in sems:
                sems[name] = ctx.enter_context(nc.semaphore(name))
            return sems[name]

        ring = sb("ring", [P, SLOTS, SLOT])
        hs = sb("hs", [P, KD, T])
        mix = sb("mix", [P, KD, T])
        rstd = sb("rstd", [P, 2, T])
        sq = sb("sq", [P, 4, T])
        vec = sb("vec", [P, NV])
        row = sb("row", [P, NR])
        cst = sb("cst", [P, NC])
        rw = sb("rw", [P, KD, NGRP + NE])
        sgw = sb("sgw", [P, SG, P])
        relb = sb("relb", [32, NH])
        ones = sb("ones", [P, P])
        nones = sb("nones", [P, P])
        iota = sb("iota", [P, ROWS])
        small = sb("small", [P, 420])
        route_i = sb("route_i", [P, 2, NE], I32)

        with ExitStack() as turn:
            wh = sb("wh", [P, 2, PIECE], F32R, turn)
            wl = sb("wl", [P, 2, PIECE], F32R, turn)
        with ExitStack() as turn:
            ewh = sb("ewh", [P, EBUFS, EPIECE], F32R, turn)
            ewl = sb("ewl", [P, EBUFS, EPIECE], F32R, turn)
            sgate = sb("sgate", [P, 2, FE], F32, turn)
            he = sb("he", [P, 2, FE], F32, turn)
            heTh = sb("heTh", [P, 2, FE // P, P], F32R, turn)
            heTl = sb("heTl", [P, 2, FE // P, P], F32R, turn)
        with ExitStack() as turn:
            rscr = sb("rscr", [P, 2 * PIECE], F32, turn)
            psel = sb("psel", [P, NB, ROWS], F32R, turn)
            combt = sb("combt", [P, NB, ROWS], F32, turn)
        ctx.enter_context(nc.sbuf_tensor("split_room", [P, 4 * PIECE], F32))
        with ExitStack() as turn:
            xh = sb("xh", [P, 9, SEQ], F32R, turn)
            xl = sb("xl", [P, 9, SEQ], F32R, turn)
        with ExitStack() as turn:
            xhT = sb("xhT", [P, KD, T], F32R, turn)
            sb("xgap", [P, 9 * SEQ - KD * T], F32, turn)
            xlT = sb("xlT", [P, KD, T], F32R, turn)
        with ExitStack() as turn:
            xtra = sb("xtra", [P, 2, 9 * SEQ], F32, turn)
        with ExitStack() as turn:
            h2h = sb("h2h", [P, NB, D], F32R, turn)
            h2l = sb("h2l", [P, NB, D], F32R, turn)
        ctx.enter_context(nc.sbuf_tensor("x_room", [P, 18 * SEQ], F32))
        with ExitStack() as turn:
            acth = sb("acth", [P, NF, T], F32R, turn)
            actl = sb("actl", [P, NF, T], F32R, turn)
        with ExitStack() as turn:
            xs = sb("xs", [P, XS_ALL], F32, turn)
            xeh = sb("xeh", [P, KD, WIDE], F32R, turn)
            xel = sb("xel", [P, KD, WIDE], F32R, turn)
        with ExitStack() as turn:
            sb("xs_and_xeh", [P, XS_ALL + KD * WIDE], F32, turn)
            xew = sb("xew", [P, KD, WIDE], F32, turn)
            combr = sb("combr", [P, 4, SEQ], F32, turn)
            ppT = sb("ppT", [P, KD, SEQ], F32, turn)
        work = sb("work", [P, 2 * NF * T])

        ps = ctx.enter_context(nc.psum_tensor("ps", [P, 8, 512], F32))

        def carve():
            at = [0]

            def take(*shape):
                n = 1
                for s in shape:
                    n *= s
                v = work[:, at[0]:at[0] + n]
                at[0] += n
                assert at[0] <= 2 * NF * T
                if len(shape) == 2:
                    v = v.rearrange("p (a b) -> p a b", b=shape[1])
                if len(shape) == 3:
                    v = v.rearrange("p (a b c) -> p a b c", b=shape[1], c=shape[2])
                return v
            return take

        take = carve()
        hp = take(KD, PADT + T)
        win = take(2 * len(WINDOWS), 2, PADT + T)
        pooled = take(KD, T)
        brow = take(3 * P)
        take = carve()
        lg = [take(2 * HEADS_PER_GROUP, SEQ) for _ in range(2)]
        h1 = lg[0]
        qT = take(KD, SEQ)
        kT = take(2, T)
        vtok = take(NB + 1, P)
        brev = take(NH, SEQ)
        pT = [mix[:, 2 * i:2 * i + 2, :].rearrange("p a b -> p (a b)")[:, 0:4 * P] for i in range(2)]
        take = carve()
        qaT = take(SB_C, SEQ)
        kaT = take(SB_C, SEQ)
        va = take(NB, SB_W)
        vb = take(NB, ML_H * ML_D)
        ob = take(ML_H, SEQ)
        uc = take(NB, SG_W)
        vc = take(NB, SG_W)
        cv = take(2 * ML_H, SEQ)
        e1 = take(2, 3 * P)
        sp = take(2, 3 * P)
        aw = take(2, 3 * P)
        yaT = take(SB_C, SEQ)
        yb = take(ML_H, SEQ)
        ycT = take(NB, SEQ)
        zpre = [ring[:, s, 4096:4096 + 4 * (SEQ + 3)].rearrange("p (a b) -> p a b", b=SEQ + 3)
                for s in range(2)]
        gt = ring[:, 2, 4096:4096 + 7 * SEQ].rearrange("p (a b) -> p a b", b=SEQ)
        ysr = ring[:, tile_of("w_exp", NE - 1) % SLOTS, 0:4 * D].rearrange("p (a b) -> p a b", b=D)
        ye = [v[:, 0:2 * D].rearrange("p (a b) -> p a b", b=D)
              for v in (mix[:, :, :].rearrange("p a b -> p (a b)"), xtra[:, 0, :], xtra[:, 1, :])]

        def V(name, i=0, rows=P):
            return vec[0:rows, VCOL[name] + i:VCOL[name] + i + 1]

        def R(name, n, at=0):
            return row[:, RCOL[name] + at:RCOL[name] + at + n]

        def C(name, n=P, rows=P, at=0):
            return cst[0:rows, CCOL[name] + at:CCOL[name] + at + n]

        ident = C("ident")

        def tile_at(t):
            return t % SLOTS, t // SLOTS

        def ring_steps(eng, name, body, first=0, last=None):
            n = dict((x, y) for x, y, _ in STREAM)[name] if last is None else last
            turns = (n - first) // SLOTS
            if turns >= 2:
                with eng.Fori(0, turns) as k:
                    for j in range(SLOTS):
                        slot, rnd = tile_at(FIRST[name] + first + j)
                        body(slot, k + rnd, k * SLOTS + (first + j))
            else:
                turns = 0
            for i in range(first + turns * SLOTS, n):
                slot, rnd = tile_at(FIRST[name] + i)
                body(slot, rnd, i)

        def owner(t):
            return next((name, t - FIRST[name]) for name, n, _ in STREAM if t - FIRST[name] < n)

        def tile_done(name, i):
            by_product = {"w_pool": ("mix_psum", KD), "w_kv": ("kv_psum", 3), "w_proj": ("pp_psum", KD),
                          "w_exp": ("elo_done", i * EPIECES + 2)}
            return by_product.get(name) or ("lo_done", i * 2 + (FIRST_PIECE[name] + 2))

        def piece_done(name, q):
            if name == "w_z":
                return "z_psum", sum(len(x) for x in Z_OUT[:q + 1])
            return {"w_gu0": ("gu_psum", q + 1), "w_dn0": ("dn_psum", q + 1), "w_q": ("q_psum", q * 2 + 2),
                    "w_o": ("wo_psum", q * 2 + 2), "w_gu1": ("gu_psum", q + (NF + 1)),
                    "w_dn1": ("dn_psum", q + (2 * KD + 1)), "w_out": ("wout_psum", q + 1),
                    "w_ple": ("ple_psum", q * 2 + 2)}[name]

        def gu_piece_of(e):
            return 0 if type(e) is int and e == 0 else e * EPIECES - 2

        def dn_piece_of(e):
            return NE * EPIECES - 2 if type(e) is int and e == NE - 1 else e * EPIECES + 8

        def expert_buffer(j, down, e):
            first = gu_piece_of(e if type(e) is int else 1) if not down else dn_piece_of(e if type(e) is int else 0)
            return (first + j) % EBUFS

        def expert_tile(slot, rnd, e):
            return rnd - tile_at(next(t for t in range(FIRST["w_exp"], FIRST["w_exp"] + SLOTS) if t % SLOTS == slot))[1]

        def value(eng, which, e):
            return eng.value_load(route_i[0:1, which, bass.ds(e, 1)], min_val=0, max_val=WIDE if which else ROWS)

        def for_halves(eng, count, body):
            with eng.If(count > HALF):
                body(2)
            with eng.Else():
                body(1)

        SPLIT = [(name, 2 * n) for name, n, _ in STREAM if name not in UNSPLIT]

        class Chain:

            def __init__(self, eng, name):
                self.eng, self.sem, self.n = eng, sem(name), 0

            def __call__(self, ins):
                self.n += 1
                ins.then_inc(self.sem, 1)
                self.eng.wait_ge(self.sem, self.n)

        block = ctx.enter_context(nc.Block())

        @block.sync
        def _(sp_):
            sp_.dma_start(hs[:, :, :], a["hT"]).then_inc(sem("hs_loaded"), 16)
            sp_.dma_start(vec[:, :], a["vec"]).then_inc(sem("consts_loaded"), 16)
            sp_.dma_start(cst[:, :], a["cst"]).then_inc(sem("consts_loaded"), 16)

            def load(name, size):
                def body(slot, rnd, i):
                    if type(i) is not int or i >= SLOTS:
                        done, count = tile_done(name, i - SLOTS)
                        sp_.wait_ge(sem(done), count)
                    elif FIRST[name] + i >= SLOTS:
                        done, count = tile_done(*owner(FIRST[name] + i - SLOTS))
                        sp_.wait_ge(sem(done), count)
                    src = a[name][bass.ds(i, 1), :, :] if type(i) is not int else a[name][i:i + 1, :, :]
                    sp_.dma_start(ring[:, slot, 0:size], src.rearrange("a p n -> p (a n)"))\
                       .then_inc(sem(f"tile_ready{slot}"), 16)
                return body

            def stream(name):
                size = dict((x, z) for x, _, z in STREAM)[name]
                body = load(name, size)
                n = dict((x, y) for x, y, _ in STREAM)[name]
                for i in range(min(SLOTS, n)):
                    body(*tile_at(FIRST[name] + i), i)
                ring_steps(sp_, name, body, first=min(SLOTS, n))

            stream("w_pool")
            sp_.dma_start(row[:, :], a["row"]).then_inc(sem("tables_loaded"), 16)
            sp_.dma_start(relb[:, :], a["rel_bias"]).then_inc(sem("tables_loaded"), 16)
            sp_.dma_start(rw[:, :, :], a["rw"]).then_inc(sem("tables_loaded"), 16)
            sp_.dma_start(sgw[:, :, :], a["sgw"]).then_inc(sem("tables_loaded"), 16)
            sp_.wait_ge(sem("brow_ready"), 2)
            sp_.dma_start(bias_rows, brow[0:NH, :]).then_inc(sem("bias_out"), 16)
            stream("w_gu0")
            stream("w_dn0")
            stream("w_kv")
            sp_.wait_ge(sem("bias_out"), 16)
            sp_.wait_ge(sem("dn_psum"), 2 * KD)
            skew = bass.AP(bias_rows.tensor, 0, [[1, P], [3 * P, NH], [1, SEQ]])
            sp_.dma_start(brev, skew).then_inc(sem("bias_ready"), 16)
            for name in ("w_q", "w_o", "w_gu1", "w_dn1", "w_z", "w_out", "w_proj"):
                if name == "w_proj":
                    sp_.wait_ge(sem("y_split"), 9)
                stream(name)

            def gate_up(slot, rnd, e):
                if type(e) is not int or e >= SLOTS:
                    sp_.wait_ge(sem("elo_done"), gu_piece_of(e - SLOTS) + 4)
                else:
                    done, count = tile_done(*owner(FIRST["w_exp"] + e - SLOTS))
                    sp_.wait_ge(sem(done), count)
                sp_.dma_start(ring[:, slot, 0:4096], a["w_eg"][bass.ds(e, 1), :, :].rearrange("a p n -> p (a n)"))\
                   .then_inc(sem(f"tile_ready{slot}"), 16)

            def down(slot, rnd, e):
                if type(e) is not int or e >= SLOTS:
                    sp_.wait_ge(sem("elo_done"), dn_piece_of(e - SLOTS) + 2)
                sp_.dma_start(ring[:, slot, 4096:SLOT], a["w_ed"][bass.ds(e, 1), :, :].rearrange("a p n -> p (a n)"))\
                   .then_inc(sem(f"down_ready{slot}"), 16)

            def both(slot, rnd, e):
                gate_up((slot + 1) % SLOTS, None, e + 1)
                down(slot, None, e)

            gate_up(*tile_at(FIRST["w_exp"]), 0)
            for e in range(SLOTS + 1):
                both(*tile_at(FIRST["w_exp"] + e), e)
            ring_steps(sp_, "w_exp", both, first=SLOTS + 1, last=NE - 1)
            down(*tile_at(FIRST["w_exp"] + NE - 1), NE - 1)
            sp_.wait_ge(sem("elo_done"), NE * EPIECES)
            sp_.wait_ge(sem("y_stored"), 16 * NE)
            sp_.dma_start(ysr, y_rows[0:ROWS, :].rearrange("(r p) n -> p r n", p=P)).then_inc(sem("ysr_loaded"), 16)
            stream("w_ple")
            for c in range(KD):
                sp_.wait_ge(sem("out_ready"), c + 1)
                sp_.dma_start(out[:, c, :], mix[:, c, 0:SEQ]).then_inc(sem("out_stored"), 16)
            sp_.wait_ge(sem("out_stored"), 16 * KD)

        def pool_groups(eng, chain, groups, done):
            for g in groups:
                eng.wait_ge(sem("h_ready"), 2 * g + 2)
                eng.wait_ge(sem("hp_padded"), 1)
                if g == groups[0]:
                    eng.wait_ge(sem("consts_loaded"), 32)
                cur, lo, w, k = hp[:, 2 * g:2 * g + 2, :], 0, 1, 0
                while w < WINDOWS[g]:
                    new = win[:, 2 * g + k % 2, :, :]
                    chain(eng.tensor_tensor(new[:, :, lo + w:], cur[:, :, lo + w:], cur[:, :, lo:PADT + T - w], ALU.add))
                    cur, lo, w, k = new, lo + w, 2 * w, k + 1
                h = hp[:, 2 * g:2 * g + 2, PADT:]
                p = pooled[:, 2 * g:2 * g + 2, :]
                inv = C("invcnt", PADT, at=g * PADT).unsqueeze(1).to_broadcast([P, 2, PADT])
                fix = win[:, 2 * g + k % 2, :, 0:PADT]
                chain(eng.tensor_scalar(p[:, :, PADT:], cur[:, :, 2 * PADT:], 1.0 / w, None, ALU.mult))
                chain(eng.tensor_tensor(p[:, :, PADT:], p[:, :, PADT:], h[:, :, PADT:], ALU.subtract))
                chain(eng.tensor_tensor(fix, cur[:, :, PADT:2 * PADT], inv, ALU.mult))
                eng.tensor_tensor(p[:, :, 0:PADT], fix, h[:, :, 0:PADT], ALU.subtract).then_inc(sem(done), 1)

        def residual_add(pool, k, cols):
            n = cols.stop - cols.start
            for c in range(KD):
                pool.wait_ge(sem("delta_ready"), k * KD + c + 1)
                pool.tensor_tensor(hs[:, c, cols], hs[:, c, cols], mix[:, c, 0:n], ALU.add)\
                    .then_inc(sem("hs_ready"), 1)

        def residual_add_gate(pool):
            for c in range(KD):
                pool.wait_ge(sem("delta_ready"), 4 * KD + c + 1)
                pool.tensor_tensor(hs[:, c, N_META:], hs[:, c, N_META:], mix[:, c, 0:SEQ], ALU.add)\
                    .then_inc(sem("hs_ready"), 1)

        def ffn_pool(pool, l, n):
            with pool.Fori(0, NF // 2) as i:
                for j in range(2):
                    f = i * 2 + j
                    pool.wait_ge(sem("silu_ready"), f + (l * NF + 1))
                    pool.wait_ge(sem("up_ready"), f + (l * NF + 1))
                    pool.tensor_tensor(mix[:, 6 + j, 0:n], mix[:, 2 + j, 0:n], mix[:, 4 + j, 0:n], ALU.mult)\
                        .then_inc(sem("act_ready"), 1)
                    pool.wait_ge(sem("act_ready"), f + (l * NF + 1))
                    pool.tensor_copy(acth[:, bass.ds(f, 1), 0:n], mix[:, 6 + j:7 + j, 0:n])\
                        .then_inc(sem("acth_ready"), 1)
                    pool.wait_ge(sem("acth_ready"), f + (l * NF + 1))
                    pool.tensor_tensor(actl[:, bass.ds(f, 1), 0:n], mix[:, 6 + j:7 + j, 0:n],
                                       acth[:, bass.ds(f, 1), 0:n].bitcast(F32), ALU.subtract)\
                        .then_inc(sem("act_split"), 1)

        def conv(eng, chain, j, done):
            eng.wait_ge(sem("z_evac"), j + 1)
            eng.wait_ge(sem("zpre_padded"), 2)
            src, dst = zpre[j // ML_H][0:ML_D, j % ML_H, :], cv[0:ML_D, j, :]
            chain(eng.tensor_scalar(dst, src[:, 0:SEQ], V("conv_w", 4 * j, ML_D), V("conv_b", j, ML_D), ALU.mult, ALU.add))
            for k in range(1, 4):
                ins = eng.scalar_tensor_tensor(dst, src[:, k:k + SEQ], V("conv_w", 4 * j + k, ML_D), dst, ALU.mult, ALU.add)
                if k < 3:
                    chain(ins)
            ins.then_inc(sem(done), 1)

        @block.gpsimd
        def _(pool):
            chain = Chain(pool, "pool_chain")
            pool.memset(ones[:, :], 1.0).then_inc(sem("ones_ready"), 1)
            pool.memset(nones[:, :], -1.0).then_inc(sem("ones_ready"), 1)
            pool.memset(hp[:, :, 0:PADT], 0.0).then_inc(sem("hp_padded"), 1)
            pool.memset(brow[0:NH, :], NEG).then_inc(sem("brow_ready"), 1)
            pool.iota(mix[:, 0:2, 0:SEQ].bitcast(I32), pattern=[[SEQ, 2], [1, SEQ]], base=0, channel_multiplier=0)\
                .then_inc(sem("iota_i"), 1)
            pool.wait_ge(sem("iota_i"), 1)
            pool.tensor_copy(iota[:, :].rearrange("p (a b) -> p a b", a=2), mix[:, 0:2, 0:SEQ].bitcast(I32))\
                .then_inc(sem("iota_ready"), 1)

            pool.wait_ge(sem("consts_loaded"), 32)
            pool.wait_ge(sem("tables_loaded"), 64)
            pool.tensor_tensor(sgw[:, :, :], sgw[:, :, :], C("sgumask").unsqueeze(1).to_broadcast([P, SG, P]), ALU.mult)\
                .then_inc(sem("sgw_masked"), 1)

            pool_groups(pool, chain, (0, 1), "p_pool")
            residual_add(pool, 0, slice(0, T))
            ffn_pool(pool, 0, T)
            residual_add(pool, 1, slice(0, T))
            residual_add(pool, 2, slice(N_META, T))
            ffn_pool(pool, 1, SEQ)
            residual_add(pool, 3, slice(N_META, T))

            for s in range(2):
                pool.memset(zpre[s][0:ML_D, :, 0:3], 0.0).then_inc(sem("zpre_padded"), 1)
            for i in range(SB_H):
                pool.wait_ge(sem("sb_exp"), i + 1)
                v = aw[:, i % 2, :].rearrange("p (a b) -> p a b", a=3)[:, 0:3:2, :]
                pool.affine_select(out=v, in_=v, compare_op=ALU.is_gt, fill=0.0, base=0,
                                   pattern=[[0, 2], [1, P]], channel_multiplier=-1).then_inc(sem("sb_a"), 1)
            for h in range(ML_H):
                pool.wait_ge(sem("ml_exp"), 2 * h + 2)
                v = aw[:, h % 2, :].rearrange("p (a b) -> p a b", a=3)[:, 0:3:2, :]
                pool.affine_select(out=v, in_=v, compare_op=ALU.is_ge, fill=0.0, base=0,
                                   pattern=[[0, 2], [1, P]], channel_multiplier=-1).then_inc(sem("ml_d"), 1)

            pool.wait_ge(sem("hs_ready"), 5 * KD)
            for k in range(KD):
                at = k * XS + ROWS
                n = FEW if k < KD - 1 else WIDE
                pool.tensor_copy(xs[:, at:at + n], iota[:, 0:n]).then_inc(sem("xs_padded"), 1)
            for x in (xeh, xel):
                for k in range(KD):
                    pool.tensor_copy(x[:, k, FEW:HALF], iota[:, FEW:HALF]).then_inc(sem("xs_padded"), 1)
            pool.wait_ge(sem("xs_padded"), 3 * KD)
            pool.wait_ge(sem("route_ready"), 2)
            for ready in ("xs_ready", "xs_ready_d"):
                pool.wait_ge(sem(ready), KD // 2)

            def window(slot, rnd, e):
                start, count = value(pool, 0, e), value(pool, 1, e)

                def rows(n):
                    for j in range(4):
                        if type(e) is not int or e:
                            pool.wait_ge(sem("e_used"), gu_piece_of(e - 1) + (j + 1))
                        pair = slice(2 * j, 2 * j + 2)
                        for k in range(2 * j, 2 * j + 2):
                            src = xs[:, bass.ds(start + k * XS, n)]
                            pool.tensor_copy(xew[:, k, 0:n], src).then_inc(sem("xew_ready"), 1)
                            pool.tensor_copy(xeh[:, k, 0:n], src).then_inc(sem("xew_ready"), 1)
                        pool.wait_ge(sem("xew_ready"), e * (2 * KD) + (4 * j + 4))
                        pool.tensor_tensor(xel[:, pair, 0:n], xew[:, pair, 0:n], xeh[:, pair, 0:n].bitcast(F32), ALU.subtract)\
                            .then_inc(sem("xe_ready"), 1)

                with pool.If(count > FEW):
                    with pool.If(count > HALF):
                        rows(WIDE)
                    with pool.Else():
                        rows(HALF)
                with pool.Else():
                    rows(FEW)

            def store(slot, rnd, e):
                start, count = value(pool, 0, e), value(pool, 1, e)

                def rows(n, halves):
                    pool.wait_ge(sem("y_ready"), e + 1)
                    if type(e) is not int or e:
                        pool.wait_ge(sem("y_stored"), e * 16)
                    dst = y_rows[bass.ds(start, n * halves), :].rearrange("(a p) n -> p a n", p=n)
                    pool.dma_start(dst, ye[slot][0:n, 0:halves, :]).then_inc(sem("y_stored"), 16)

                with pool.If(count > HALF):
                    rows(HALF, 2)
                with pool.Else():
                    with pool.If(count > FEW):
                        rows(HALF, 1)
                    with pool.Else():
                        rows(FEW, 1)

            def window_and_store(slot, rnd, e):
                window(slot, rnd, e)
                store(slot, None, e - SLOTS)

            for e in range(SLOTS):
                window(None, None, e)
            window_and_store(*tile_at(FIRST["w_exp"] + SLOTS), SLOTS)
            ring_steps(pool, "w_exp", window_and_store, first=SLOTS + 1)
            for e in range(NE - SLOTS, NE):
                store(tile_at(FIRST["w_exp"] + e)[0], None, e)
            residual_add_gate(pool)

        def r_of(name):
            return rstd[:, NORM[name] % 2, :]

        def square(act, name, c, src, n, rows=P, **kw):
            k = SQ0[name] + c
            if k >= 4:
                act.wait_ge(sem("sq_used"), k - 3)
            act.activation(sq[0:rows, k % 4, 0:n], src, ACT.Square, **kw).then_inc(sem("sq_ready"), 1)

        def rsqrt(act, chain, name, width, n):
            r = r_of(name)[:, 0:n]
            act.wait_ge(sem("sq_used"), SQ0[name] + dict(NORMS)[name])
            chain(act.activation(r, ps[:, 6, 0:n], ACT.Ln, scale=1.0 / width, bias=EPS))
            act.activation(r, r, ACT.Exp, scale=-0.5).then_inc(sem("r_ready"), 1)

        def split_hi(act, name, slot, rnd, i, j, size):
            if j == 0:
                act.wait_ge(sem(f"tile_ready{slot}"), rnd * 16 + 16)
            if type(i) is not int or i > 0:
                done, count = piece_done(name, i * 2 + (j - 2))
                act.wait_ge(sem(done), count)
            elif FIRST_PIECE[name]:
                before, n = SPLIT[[x for x, _ in SPLIT].index(name) - 1]
                done, count = piece_done(before, n + j - 2)
                act.wait_ge(sem(done), count)
            act.activation(wh[:, j, 0:size], ring[:, slot, j * size:(j + 1) * size], ACT.Copy)\
               .then_inc(sem("hi_done"), 1)

        def split_lo(dve, name, slot, rnd, i, j, size):
            piece = i * 2 + (FIRST_PIECE[name] + j)
            dve.wait_ge(sem("hi_done"), piece + 1)
            dve.tensor_tensor(wl[:, j, 0:size], ring[:, slot, j * size:(j + 1) * size],
                              wh[:, j, 0:size].bitcast(F32), ALU.subtract).then_inc(sem("lo_done"), 1)

        def halves(name, i, size):
            slot, rnd = tile_at(FIRST[name] + i)
            return [(slot, rnd, i, j, size) for j in range(2)]

        def wo_out(act, c):
            act.wait_ge(sem("wo_psum"), c + 1)
            act.activation(mix[:, c, 0:SEQ], ps[:, c % 4, 0:SEQ], ACT.Identity, bias=V("b_o", c))\
               .then_inc(sem("mix_ready"), 1)
            square(act, "mixpost1", c, ps[:, c % 4, 0:SEQ], SEQ, bias=V("b_o", c))

        def ple_gate(act, c):
            act.wait_ge(sem("ple_psum"), c + 1)
            act.activation(mix[:, c, 0:SEQ], ps[:, c % 4, 0:SEQ], ACT.Sigmoid).then_inc(sem("ple_sig"), 1)

        def y_chunks():
            return [(yaT[:, c, :], P) for c in range(SB_C)] + [(yb[0:ML_D, h, :], ML_D) for h in range(ML_H)] \
                + [(ycT[:, c, :], P) for c in range(NB)]

        def z_parts(parts, n):
            bank = ps[:, n % 4, :]
            kind, i = parts
            if kind == "conv":
                return [(zpre[i // ML_H][0:ML_D, i % ML_H, 3:], bank[0:ML_D, 0:SEQ], ACT.Copy, {})]
            if kind == "ob":
                return [(ob[0:ML_D, i, :], bank[0:ML_D, 0:SEQ], ACT.Copy, {})]
            if kind == "gate":
                return [(gt[0:ML_H, i, :], bank[0:ML_H, 0:SEQ], ACT.Identity,
                         {"bias": V("fgate_b" if i else "igate_b", 0, ML_H)})]
            if kind == "qa":
                return [(qaT[:, i, :], bank[:, 0:SEQ], ACT.Copy, {"scale": HD ** -0.5})]
            if kind == "ka":
                return [(kaT[:, i, :], bank[:, 0:SEQ], ACT.Copy, {})]
            if kind == "va":
                return [(va[:, i, 0:256], bank[:, 0:256], ACT.Copy, {})]
            if kind == "vab":
                return [(va[:, i, 256:384], bank[:, 0:128], ACT.Copy, {}), (vb[:, i, 0:128], bank[:, 128:256], ACT.Copy, {})]
            if kind == "vb":
                return [(vb[:, i, 128:384], bank[:, 0:256], ACT.Copy, {})]
            if kind == "uc":
                return [(uc[:, i, :], bank[:, 0:SG_W], ACT.Gelu_apprx_tanh, {})]
            return [(vc[:, i, :], bank[:, 0:SG_W], ACT.Gelu_apprx_tanh, {})]

        def ffn_act(act, chain, l, n, cols):
            gu, dn, pre, post = f"w_gu{l}", f"w_dn{l}", f"ffnpre{l}", f"ffnpost{l}"
            x = xhT if l == 0 else xh
            for args in halves(gu, 0, PIECE):
                split_hi(act, gu, *args)
            for c in range(KD):
                act.wait_ge(sem("hs_ready"), (1 if l == 0 else 3) * KD + c - KD + 1)
                act.activation(x[:, c, 0:n], hs[:, c, cols], ACT.Copy, scale=V(pre, c)).then_inc(sem("xh_ready"), 1)
                if c < 4:
                    square(act, pre, c, hs[:, c, cols], n)
            for c in range(4, KD):
                square(act, pre, c, hs[:, c, cols], n)
            rsqrt(act, chain, pre, D, n)
            act.preload_act_table_set("silu_and_others")

            def silu(f, j):
                act.wait_ge(sem("gr_ready"), f + (l * NF + 1))
                act.activation(mix[:, 2 + j, 0:n], mix[:, j, 0:n], ACT.Silu).then_inc(sem("silu_ready"), 1)

            def body(slot, rnd, i):
                for j in range(2):
                    split_hi(act, gu, slot, rnd, i, j, PIECE)
                    silu(i * 2 + (j - 2), j)

            ring_steps(act, gu, body, first=1)
            for j in range(2):
                silu(NF - 2 + j, j)
            act.preload_act_table_set("natural_log_exp_and_others")

            def leave(c):
                act.wait_ge(sem("dn_psum"), 2 * (l * KD + c) + 2)
                act.activation(mix[:, c, 0:n], ps[:, 4 + c % 2, 0:n], ACT.Copy).then_inc(sem("mix_ready"), 1)
                square(act, post, c, ps[:, 4 + c % 2, 0:n], n)

            for i in range(KD):
                for args in halves(dn, i, FF // 2):
                    split_hi(act, dn, *args)
                if i:
                    leave(i - 1)
            leave(KD - 1)
            rsqrt(act, chain, post, D, n)

        @block.scalar
        def _(act):
            chain = Chain(act, "act_chain")
            act.preload_act_table_set("natural_log_exp_and_others")
            act.wait_ge(sem("hs_loaded"), 16)
            for c in range(KD):
                square(act, "mixpre0", c, hs[:, c, :], T)
            rsqrt(act, chain, "mixpre0", D, T)
            act.wait_ge(sem("brow_psum"), 1)
            act.wait_ge(sem("brow_ready"), 1)
            act.activation(brow[0:NH, P:2 * P], ps[0:NH, 7, 0:P], ACT.Copy).then_inc(sem("brow_ready"), 1)
            act.wait_ge(sem("iota_ready"), 1)
            for c in range(KD):
                act.wait_ge(sem("mix_psum"), c + 1)
                act.activation(mix[:, c, :], ps[:, c % 4, 0:T], ACT.Copy, scale=V("pool_scale", c))\
                   .then_inc(sem("mix_ready"), 1)
                square(act, "mixpost0", c, ps[:, c % 4, 0:T], T, scale=V("pool_scale", c))
            rsqrt(act, chain, "mixpost0", D, T)
            ffn_act(act, chain, 0, T, slice(0, T))

            for c in range(KD):
                act.wait_ge(sem("hs_ready"), KD + c + 1)
                square(act, "pre1", c, hs[:, c, :], T)
            rsqrt(act, chain, "pre1", D, T)
            for x in halves("w_q", 0, PIECE):
                split_hi(act, "w_q", *x)
            for c in range(KD):
                act.wait_ge(sem("h1_ready"), c + 1)
                act.activation(xh[:, c, :], h1[:, c, :], ACT.Copy).then_inc(sem("xh_ready"), 1)
            for j in range(2):
                act.wait_ge(sem("kv_psum"), j + 1)
                act.activation(kT[:, j, :], ps[:, j, 0:T], ACT.Identity, bias=V("b_k", j))\
                   .then_inc(sem("kT_ready"), 1)
            for x in halves("w_q", 1, PIECE) + halves("w_o", 0, PIECE):
                split_hi(act, "w_q" if x[2] else "w_o", *x)
            for g in range(NH // HEADS_PER_GROUP):
                act.wait_ge(sem("negm_ready"), g + 1)
                for i in range(2 * HEADS_PER_GROUP):
                    n = N_META + P if i % 2 == 0 else 2 * P
                    k = 2 * HEADS_PER_GROUP * g + i
                    v = lg[g % 2][:, i, 0:n]
                    act.activation(v, v, ACT.Exp, bias=small[:, 32 + k:33 + k], accum_out=small[:, 96 + k:97 + k])\
                       .then_inc(sem("exp_ready"), 1)
                k = 2 * HEADS_PER_GROUP * g
                act.activation(small[:, 64 + k:72 + k], small[:, 64 + k:72 + k], ACT.Exp).then_inc(sem("exp_ready"), 1)
                for h in range(HEADS_PER_GROUP * g, HEADS_PER_GROUP * (g + 1)):
                    act.wait_ge(sem("pt_psum"), h + 1)
                    if h >= 2:
                        act.wait_ge(sem("o_done"), h - 1)
                    act.activation(pT[h % 2][:, 0:3 * P], ps[:, 4 + h % 2, 0:3 * P], ACT.Copy).then_inc(sem("pt_ready"), 1)
                    act.activation(pT[h % 2][0:N_META, 3 * P:4 * P], ps[0:N_META, 4 + h % 2, 3 * P:4 * P], ACT.Copy)\
                       .then_inc(sem("pt_ready"), 1)
                    if h % 2 == 1:
                        c = h // 2
                        act.wait_ge(sem("o_done"), h + 1)
                        o = ps[:, 6 + c % 2, 0:SEQ].rearrange("p (b q) -> p b q", q=P)
                        act.activation(xh[:, c, :].rearrange("p (b q) -> p b q", q=P), o[:, :, ::-1], ACT.Copy)\
                           .then_inc(sem("oh_ready"), 1)
            for k in range(NB):
                split_hi(act, "w_o", *halves("w_o", 1, PIECE)[k])
                for c in range(2 * k, 2 * k + 2):
                    wo_out(act, c)
            for c in range(4, KD):
                wo_out(act, c)
            rsqrt(act, chain, "mixpost1", D, SEQ)
            ffn_act(act, chain, 1, SEQ, slice(N_META, T))

            for x in halves("w_z", 0, PIECE):
                split_hi(act, "w_z", *x)
            for c in range(KD):
                act.wait_ge(sem("hs_ready"), 3 * KD + c + 1)
                square(act, "norm1", c, hs[:, c, N_META:], SEQ)
            rsqrt(act, chain, "norm1", D, SEQ)
            for c in range(KD):
                act.wait_ge(sem("xn_ready"), c + 1)
                act.activation(xh[:, c, :], mix[:, c, 0:SEQ], ACT.Copy).then_inc(sem("xh_ready"), 1)
            n = 0
            for piece in range(14):
                if piece < 12:
                    split_hi(act, "w_z", *halves("w_z", piece // 2 + 1, PIECE)[piece % 2])
                for parts in Z_OUT[piece]:
                    act.wait_ge(sem("z_psum"), n + 1)
                    for q, (dst, src, func, kw) in enumerate(z_parts(parts, n)):
                        ins = act.activation(dst, src, func, **kw)
                    ins.then_inc(sem("z_evac"), 1)
                    n += 1

            act.preload_act_table_set("silu_and_others")
            act.wait_ge(sem("conv_done"), 2 * ML_H)
            act.activation(cv[0:ML_D, :, :], cv[0:ML_D, :, :], ACT.Silu).then_inc(sem("cv_ready"), 1)
            act.preload_act_table_set("natural_log_exp_and_others")
            chain(act.activation(gt[0:ML_H, 2, :], gt[0:ML_H, 1, :], ACT.Abs))
            chain(act.activation(gt[0:ML_H, 2, :], gt[0:ML_H, 2, :], ACT.Exp, scale=-1.0))
            act.activation(gt[0:ML_H, 2, :], gt[0:ML_H, 2, :], ACT.Ln, bias=1.0).then_inc(sem("gate_ln"), 1)
            act.activation(ob[0:ML_D, :, :], ob[0:ML_D, :, :], ACT.Exp, scale=-1.0).then_inc(sem("ob_exp"), 1)
            act.wait_ge(sem("sgu_centred"), 1)
            act.activation(mix[:, 0:2, 0:SG_W], vc, ACT.Square).then_inc(sem("sgu_sq"), 1)
            act.wait_ge(sem("sgu_var"), 1)
            chain(act.activation(small[:, 8:16], small[:, 8:16], ACT.Ln, scale=1.0 / SG_D, bias=EPS))
            act.activation(small[:, 8:16], small[:, 8:16], ACT.Exp, scale=-0.5).then_inc(sem("sgu_r"), 1)
            act.wait_ge(sem("gate_m"), 1)
            act.activation(gt[0:ML_H, 6, :], gt[0:ML_H, 6, :], ACT.Exp, scale=-1.0).then_inc(sem("em_ready"), 1)
            act.wait_ge(sem("sgu_y"), SG)
            for b in range(NB):
                act.activation(mix[:, 2 + b, 0:SG_W], uc[:, b, :], ACT.Square, accum_out=small[:, 16 + b:17 + b])\
                   .then_inc(sem("sgu_ysq"), 1)
            act.wait_ge(sem("sgu_ysq"), NB)
            chain(act.activation(small[:, 16:18], small[:, 16:18], ACT.Ln, scale=1.0 / SG_W, bias=EPS))
            act.activation(small[:, 16:18], small[:, 16:18], ACT.Exp, scale=-0.5).then_inc(sem("sgu_yr"), 1)

            for i in range(SB_H + 2):
                if i < SB_H:
                    act.wait_ge(sem("sb_z"), i + 1)
                    if i >= 2:
                        act.wait_ge(sem("sb_sp"), i - 1)
                    e = e1[:, i % 2, :]
                    chain(act.activation(e, ps[:, i % 3, 0:3 * P], ACT.Abs))
                    chain(act.activation(e, e, ACT.Exp, scale=-1.0))
                    act.activation(e, e, ACT.Ln, bias=1.0).then_inc(sem("sb_ln"), 1)
                if 1 <= i <= SB_H:
                    act.wait_ge(sem("sb_E"), i)
                    if i >= 3:
                        act.wait_ge(sem("sb_o"), i - 2)
                    act.activation(aw[:, (i - 1) % 2, :], ps[:, (i - 1) % 3, 0:3 * P], ACT.Exp).then_inc(sem("sb_exp"), 1)
                if i >= 3 and i % 2 == 1:
                    c = (i - 2) // 2
                    act.wait_ge(sem("sb_o"), i - 1)
                    act.activation(yaT[:, c, :], ps[:, 3 + c % 2, 0:SEQ], ACT.Copy).then_inc(sem("ya_ready"), 1)
                    square(act, "sb_out", c, ps[:, 3 + c % 2, 0:SEQ], SEQ)
            act.wait_ge(sem("yc_psum"), 1)
            act.activation(ycT.rearrange("p a b -> p (a b)"), ps[:, 7, :], ACT.Copy).then_inc(sem("yc_ready"), 1)
            rsqrt(act, chain, "sb_out", SB_W, SEQ)
            for h in range(ML_H):
                act.wait_ge(sem("ml_max"), 2 * h + 2)
                if h >= 2:
                    act.wait_ge(sem("ml_num"), h - 1)
                for b, cols in ((0, slice(0, SEQ)), (1, slice(SEQ, 3 * P))):
                    act.activation(aw[:, h % 2, cols], sp[:, h % 2, cols], ACT.Exp, scale=-1.0,
                                   bias=small[:, 20 + ML_H * b + h:21 + ML_H * b + h]).then_inc(sem("ml_exp"), 1)
                if h >= 2:
                    act.wait_ge(sem("ml_h"), h - 1)
                act.activation(e1[0:ML_D, h % 2, 0:SEQ], ps[0:ML_D, 5, SEQ:2 * SEQ], ACT.Copy).then_inc(sem("ml_em"), 1)
            act.wait_ge(sem("ml_h"), ML_H)
            act.activation(mix[0:ML_D, 0:ML_H, 0:SEQ], yb[0:ML_D, :, :], ACT.Square).then_inc(sem("ml_sq"), 1)
            act.wait_ge(sem("ml_ss"), 1)
            r4 = mix[0:ML_D, ML_H:2 * ML_H, 0:SEQ]
            for b in range(2):
                chain(act.activation(r4[:, 2 * b:2 * b + 2, :], ps[0:ML_D, b, :].rearrange("p (a t) -> p a t", t=SEQ),
                                     ACT.Ln, scale=1.0 / ML_D, bias=EPS))
            act.activation(r4, r4, ACT.Exp, scale=-0.5).then_inc(sem("ml_r"), 1)
            for x in halves("w_out", 0, 9 * P):
                split_hi(act, "w_out", *x)
            act.wait_ge(sem("yc_ready"), 1)
            for j, (src, rows) in enumerate(y_chunks()):
                if j < SB_C + ML_H:
                    act.wait_ge(sem("y_fin"), j + 1)
                act.activation(xh[0:rows, j, :], src, ACT.Copy).then_inc(sem("yh_ready"), 1)
            for i in range(1, 4):
                for x in halves("w_out", i, 9 * P):
                    split_hi(act, "w_out", *x)

            for c in range(KD):
                act.wait_ge(sem("hs_ready"), 4 * KD + c + 1)
                square(act, "norm2", c, hs[:, c, N_META:], SEQ)
            rsqrt(act, chain, "norm2", D, SEQ)
            for q in range(4):
                act.wait_ge(sem("h2_psum"), q + 1)
                act.activation(h2h[:, q // 2, q % 2 * 512:(q % 2 + 1) * 512], ps[:, 1 + q, :], ACT.Copy)\
                   .then_inc(sem("h2_ready"), 1)
            act.wait_ge(sem("route_g"), 1)
            act.activation(small[:, 128:136], small[:, 128:136], ACT.Exp).then_inc(sem("route_gexp"), 1)
            act.wait_ge(sem("route_d"), 1)
            act.activation(small[:, 180:182], small[:, 180:182], ACT.Exp).then_inc(sem("route_ex"), 1)
            for c in range(1, KD, 2):
                act.wait_ge(sem("xs_psum"), c + 1)
                act.activation(xs[:, c * XS:c * XS + ROWS], ps[:, c % 4, :], ACT.Copy).then_inc(sem("xs_ready"), 1)
            for q in range(2):
                act.wait_ge(sem("comb_psum"), q + 1)
                act.activation(combr[:, 2 * q:2 * q + 2, :].rearrange("p a b -> p (a b)"), ps[:, 6 + q, :], ACT.Copy)\
                   .then_inc(sem("comb_ready"), 1)
            for c in range(KD):
                act.wait_ge(sem("pp_psum"), c + 1)
                act.activation(ppT[:, c, :], ps[:, 4 + c % 2, 0:SEQ], ACT.Copy).then_inc(sem("pp_ready"), 1)
            act.preload_act_table_set("silu_and_others")

            def high(e, j, is_down, slot):
                g = (dn_piece_of(e) if is_down else gu_piece_of(e)) + j
                b = expert_buffer(j, is_down, e)
                if type(g) is not int or g >= EBUFS:
                    act.wait_ge(sem("e_used"), g - (EBUFS - 1))
                at = (4096 if is_down else 0) + j * EPIECE
                act.activation(ewh[:, b, :], ring[:, slot, at:at + EPIECE], ACT.Copy).then_inc(sem("ehi_done"), 1)

            def silu(e, count):
                def body(halves):
                    act.wait_ge(sem("e_used"), gu_piece_of(e) + 4)
                    act.activation(sgate[:, 0:halves, :], ps[:, 0:halves, 0:FE], ACT.Silu).then_inc(sem("sg_ready"), 1)
                for_halves(act, count, body)

            def transposed(e, count):
                def body(halves):
                    act.wait_ge(sem("het_psum"), e + 1)
                    act.activation(heTh[:, 0:halves, :, :].rearrange("p a c n -> p a (c n)"),
                                   ps[:, 6:6 + halves, 0:FE], ACT.Copy).then_inc(sem("heth_ready"), 1)
                for_halves(act, count, body)

            def leave(e, slot, count):
                def body(halves):
                    act.wait_ge(sem("e_used"), dn_piece_of(e) + 2)
                    if type(e) is not int or e >= SLOTS:
                        act.wait_ge(sem("y_stored"), e * 16 - 16 * (SLOTS - 1))
                    act.activation(ye[slot][:, 0:halves, :].rearrange("p a n -> p (a n)"),
                                   ps[:, 2:2 + 2 * halves, :].rearrange("p a n -> p (a n)"), ACT.Copy)\
                       .then_inc(sem("y_ready"), 1)
                for_halves(act, count, body)

            def step(slot, rnd, e):
                nxt = (slot + 1) % SLOTS
                act.wait_ge(sem(f"tile_ready{nxt}"), (rnd + (1 if nxt == 0 else 0)) * 16 + 16)
                high(e + 1, 0, False, nxt)
                count = value(act, 1, e)
                silu(e, count)
                high(e + 1, 1, False, nxt)
                high(e + 1, 2, False, nxt)
                transposed(e, count)
                if type(e) is not int or e:
                    leave(e - 1, (slot - 1) % SLOTS, value(act, 1, e - 1))
                high(e + 1, 3, False, nxt)
                act.wait_ge(sem(f"down_ready{slot}"), expert_tile(slot, rnd, e) * 16 + 16)
                for j in range(2):
                    high(e, j, True, slot)

            slot, rnd = tile_at(FIRST["w_exp"])
            act.wait_ge(sem(f"tile_ready{slot}"), rnd * 16 + 16)
            for j in range(4):
                high(0, j, False, slot)
            for e in range(SLOTS + 1):
                step(*tile_at(FIRST["w_exp"] + e), e)
            ring_steps(act, "w_exp", step, first=SLOTS + 1, last=NE - 1)
            last = NE - 1
            slot, rnd = tile_at(FIRST["w_exp"] + last)
            act.wait_ge(sem(f"down_ready{slot}"), expert_tile(slot, rnd, last) * 16 + 16)
            silu(last, value(act, 1, last))
            high(last, 0, True, slot)
            transposed(last, value(act, 1, last))
            leave(last - 1, (slot - 1) % SLOTS, value(act, 1, last - 1))
            high(last, 1, True, slot)
            leave(last, slot, value(act, 1, last))
            act.preload_act_table_set("natural_log_exp_and_others")

            for c in range(KD):
                act.wait_ge(sem("hs_ready"), 5 * KD + c + 1)
                square(act, "ple", c, hs[:, c, N_META:], SEQ)
            rsqrt(act, chain, "ple", D, SEQ)
            for x in halves("w_ple", 0, PIECE):
                split_hi(act, "w_ple", *x)
            for c in range(KD):
                act.wait_ge(sem("xn_ready"), 2 * KD + c + 1)
                act.activation(xh[:, c, :], mix[:, c, 0:SEQ], ACT.Copy).then_inc(sem("xh_ready"), 1)
            act.preload_act_table_set("sigmoid_and_others")
            act.wait_ge(sem("x_ready"), 5 * KD)
            for k in range(2):
                split_hi(act, "w_ple", *halves("w_ple", 1, PIECE)[k])
                for c in range(2 * k, 2 * k + 2):
                    ple_gate(act, c)
            for c in range(4, KD):
                ple_gate(act, c)
            act.preload_act_table_set("natural_log_exp_and_others")
            for c in range(KD):
                act.wait_ge(sem("hs_ready"), 6 * KD + c + 1)
                square(act, "final", c, hs[:, c, N_META:], SEQ)
            rsqrt(act, chain, "final", D, SEQ)

        def z_cols(outs, q):
            kind = outs[q][0]
            if outs[0][0] == "gate":
                return GATE_AT[q]
            if kind in ("conv", "ob"):
                return q * ML_D, ML_D
            return q * P, P

        def onehot(i):
            return small[:, 200 + i * NB * NE:200 + (i + 1) * NB * NE].rearrange("p (b e) -> p b e", b=NB)

        def ffn_pe(pe, mm3, sum_squares, l, n):
            gu, dn, pre, post = f"w_gu{l}", f"w_dn{l}", f"ffnpre{l}", f"ffnpost{l}"
            xa, xb = (xhT, xlT) if l == 0 else (xh, xl)
            base = FIRST_PIECE[gu]

            def piece(i, j, k0=None):
                f = i * 2 + j
                pe.wait_ge(sem("lo_done"), f + (base + 1))
                if not (type(i) is int and i == 0):
                    pe.wait_ge(sem("up_ready"), f + (l * NF - 1))
                for k in range(KD):
                    if type(i) is int and i == 0 and j == 0:
                        pe.wait_ge(sem("x_ready"), 2 * l * KD + k + 1)
                    for g in range(2):
                        at = slice(k * 256 + g * P, k * 256 + g * P + P)
                        ins = mm3(ps[:, 2 * j + g, 0:n], (wh[:, j, at], wl[:, j, at]), (xa[:, k, 0:n], xb[:, k, 0:n]),
                                  k == 0, k == KD - 1)
                ins.then_inc(sem("gu_psum"), 1)

            piece(0, 0)
            for c in range(KD):
                sum_squares(pre, c, n)
            piece(0, 1)
            with pe.Fori(1, NF // 2) as i:
                for j in range(2):
                    piece(i, j)
            pe.wait_ge(sem("act_split"), (l + 1) * NF)
            base = FIRST_PIECE[dn]
            for c in range(KD):
                if c >= 2:
                    pe.wait_ge(sem("sq_ready"), SQ0[post] + c - 1)
                for j in range(2):
                    pe.wait_ge(sem("lo_done"), base + 2 * c + j + 1)
                    for k in range(NF // 2):
                        at = slice(k * P, (k + 1) * P)
                        f = j * (NF // 2) + k
                        ins = mm3(ps[:, 4 + c % 2, 0:n], (wh[:, j, at], wl[:, j, at]),
                                  (acth[:, f, 0:n], actl[:, f, 0:n]), f == 0, f == NF - 1)
                    ins.then_inc(sem("dn_psum"), 1)
                if c:
                    sum_squares(post, c - 1, n)
            sum_squares(post, KD - 1, n)

        @block.tensor
        def _(pe):
            mm = pe.matmul

            def sum_squares(name, c, n, rows=P):
                k, last = SQ0[name] + c, dict((x, y) for x, y in NORMS)[name] - 1
                if c == 0 and NORM[name]:
                    pe.wait_ge(sem("r_ready"), NORM[name])
                pe.wait_ge(sem("sq_ready"), k + 1)
                mm(ps[:, 6, 0:n], ones[0:rows, :], sq[0:rows, k % 4, 0:n], start=(c == 0), stop=(c == last))\
                    .then_inc(sem("sq_used"), 1)

            def mm3(o, w, x, first, last, swap=False):
                (wh_, wl_), (xh_, xl_) = w, x
                for n, (p, q) in enumerate(((wh_, xh_), (wl_, xh_), (wh_, xl_))):
                    if swap:
                        p, q = q, p
                    ins = mm(o, p, q, start=first and n == 0, stop=last and n == 2)
                return ins

            pe.wait_ge(sem("ones_ready"), 2)
            for c in range(KD):
                sum_squares("mixpre0", c, T)
            pe.wait_ge(sem("consts_loaded"), 32)
            pe.wait_ge(sem("tables_loaded"), 64)
            mm(ps[0:NH, 7, 0:P], relb[:, :], C("buckets", rows=32), start=True, stop=True).then_inc(sem("brow_psum"), 1)
            slot, rnd = tile_at(FIRST["w_pool"])
            pe.wait_ge(sem(f"tile_ready{slot}"), 16 * (rnd + 1))
            pw = ring[:, slot, 0:2048].rearrange("p (g k n) -> p g k n", g=4, k=2)
            for c in range(KD):
                g = c // 2
                pe.wait_ge(sem("p_pool" if g < 2 else "p_dve"), g % 2 + 1)
                if c >= 4:
                    pe.wait_ge(sem("sq_ready"), SQ0["mixpost0"] + c - 3)
                for k in range(2):
                    ins = mm(ps[:, c % 4, 0:T], pw[:, g, k, c % 2 * P:c % 2 * P + P], pooled[:, 2 * g + k, :],
                             start=(k == 0), stop=(k == 1))
                ins.then_inc(sem("mix_psum"), 1)
                if c:
                    sum_squares("mixpost0", c - 1, T)
            sum_squares("mixpost0", KD - 1, T)
            ffn_pe(pe, mm3, sum_squares, 0, T)

            for c in range(KD):
                sum_squares("pre1", c, T)
            slot, rnd = tile_at(FIRST["w_kv"])
            pe.wait_ge(sem(f"tile_ready{slot}"), 16 * (rnd + 1))
            wkv = ring[:, slot, 0:3072].rearrange("p (k n) -> p k n", k=KD)
            for j in range(2):
                for k in range(KD):
                    pe.wait_ge(sem("kvin_ready"), k + 1)
                    ins = mm(ps[:, j, 0:T], wkv[:, k, j * P:(j + 1) * P], mix[:, k, :], start=(k == 0), stop=(k == KD - 1))
                ins.then_inc(sem("kv_psum"), 1)
            for j in range(NB + 1):
                cols = slice(0, N_META) if j == 0 else slice(N_META + (j - 1) * P, N_META + j * P)
                for k in range(KD):
                    ins = mm(ps[0:cols.stop - cols.start, 2, j * P:(j + 1) * P], mix[:, k, cols], wkv[:, k, 2 * P:3 * P],
                             start=(k == 0), stop=(k == KD - 1))
            ins.then_inc(sem("kv_psum"), 1)
            x = (xh, xl)
            pe.wait_ge(sem("kT_ready"), 2)
            pe.wait_ge(sem("v_ready"), 2)
            for c in range(KD):
                piece = FIRST_PIECE["w_q"] + c // 2
                pe.wait_ge(sem("lo_done"), piece + 1)
                if c >= 4:
                    pe.wait_ge(sem("q_ready"), c - 3)
                for k in range(KD):
                    pe.wait_ge(sem("x_ready"), KD + k + 1)
                    at = slice(k * 256 + c % 2 * P, k * 256 + c % 2 * P + P)
                    ins = mm3(ps[:, c % 4, 0:SEQ], (wh[:, piece % 2, at], wl[:, piece % 2, at]),
                              (xh[:, k, 0:SEQ], xl[:, k, 0:SEQ]), k == 0, k == KD - 1)
                ins.then_inc(sem("q_psum"), 1)

            def scores(g):
                for h in range(HEADS_PER_GROUP * g, HEADS_PER_GROUP * (g + 1)):
                    rows = slice(h % 2 * HD, h % 2 * HD + HD)
                    for b in range(NB):
                        i = NB * h + b
                        keys = slice(0, N_META + P) if b == 0 else slice(N_META, T)
                        if i >= 4:
                            pe.wait_ge(sem("lg_ready"), i - 3)
                        mm(ps[:, i % 4, 0:keys.stop - keys.start], qT[rows, h // 2, b * P:(b + 1) * P],
                           kT[rows, h // 8, keys], start=True, stop=True).then_inc(sem("s_psum"), 1)

            def values(h):
                i = 2 * (h % HEADS_PER_GROUP)
                p = lg[h // HEADS_PER_GROUP % 2]
                pe.wait_ge(sem("p_ready"), 2 * h + 2)
                if h >= 2:
                    pe.wait_ge(sem("pt_ready"), 2 * h - 2)
                t = ps[:, 4 + h % 2, :]
                pe.transpose(t[:, 0:P], p[:, i, N_META:N_META + P], ident)
                pe.transpose(t[:, P:2 * P], p[:, i + 1, 0:P], ident)
                pe.transpose(t[:, 2 * P:3 * P], p[:, i + 1, P:2 * P], ident)
                pe.transpose(t[0:N_META, 3 * P:4 * P], p[:, i, 0:N_META], ident).then_inc(sem("pt_psum"), 1)

            def outputs(h):
                pe.wait_ge(sem("pt_ready"), 2 * h + 2)
                if h % 2 == 0 and h >= 4:
                    pe.wait_ge(sem("o_ready"), h // 2 - 1)
                c = h // 2
                v = slice(h // 8 * HD, h // 8 * HD + HD)
                o = ps[h % 2 * HD:h % 2 * HD + HD, 6 + c % 2, 0:SEQ]
                t = pT[h % 2]
                mm(o[:, 0:P], vtok[0:N_META, 0, v], t[0:N_META, 3 * P:4 * P], start=True, stop=False)
                mm(o[:, 0:P], vtok[:, 1, v], t[:, 0:P], start=False, stop=True)
                mm(o[:, P:2 * P], vtok[:, 1, v], t[:, P:2 * P], start=True, stop=False)
                mm(o[:, P:2 * P], vtok[:, 2, v], t[:, 2 * P:3 * P], start=False, stop=True).then_inc(sem("o_done"), 1)

            pe.wait_ge(sem("q_ready"), KD)
            scores(0)
            for g in range(NH // HEADS_PER_GROUP):
                if g + 1 < NH // HEADS_PER_GROUP:
                    scores(g + 1)
                heads = range(HEADS_PER_GROUP * g, HEADS_PER_GROUP * (g + 1))
                for h in heads:
                    values(h)
                    if h > heads[0]:
                        outputs(h - 1)
                outputs(heads[-1])
            for c in range(KD):
                piece = FIRST_PIECE["w_o"] + c // 2
                pe.wait_ge(sem("lo_done"), piece + 1)
                if c >= 4:
                    pe.wait_ge(sem("sq_ready"), SQ0["mixpost1"] + c - 3)
                for k in range(KD):
                    pe.wait_ge(sem("o_ready"), k + 1)
                    at = slice(k * 256 + c % 2 * P, k * 256 + c % 2 * P + P)
                    ins = mm3(ps[:, c % 4, 0:SEQ], (wh[:, piece % 2, at], wl[:, piece % 2, at]),
                              (xh[:, k, 0:SEQ], xl[:, k, 0:SEQ]), k == 0, k == KD - 1)
                ins.then_inc(sem("wo_psum"), 1)
                if c:
                    sum_squares("mixpost1", c - 1, SEQ)
            sum_squares("mixpost1", KD - 1, SEQ)
            ffn_pe(pe, mm3, sum_squares, 1, SEQ)

            for c in range(KD):
                sum_squares("norm1", c, SEQ)
            n = 0
            for i, outs in enumerate(Z_OUT):
                piece = FIRST_PIECE["w_z"] + i
                pe.wait_ge(sem("lo_done"), piece + 1)
                for q, (kind, b) in enumerate(outs):
                    if n >= 4:
                        pe.wait_ge(sem("z_evac"), n - 3)
                    for k in range(KD):
                        pe.wait_ge(sem("x_ready"), 3 * KD + k + 1)
                        if kind in Z_TOKENS:
                            at = slice(k * 256, k * 256 + 256)
                            t = slice(b * P, b * P + P)
                            ins = mm3(ps[:, n % 4, 0:256], (wh[:, i % 2, at], wl[:, i % 2, at]),
                                      (xh[:, k, t], xl[:, k, t]), k == 0, k == KD - 1, swap=True)
                        else:
                            first, m = z_cols(outs, q)
                            at = slice(k * 256 + first, k * 256 + first + m)
                            ins = mm3(ps[0:m, n % 4, 0:SEQ], (wh[:, i % 2, at], wl[:, i % 2, at]),
                                      (xh[:, k, 0:SEQ], xl[:, k, 0:SEQ]), k == 0, k == KD - 1)
                    ins.then_inc(sem("z_psum"), 1)
                    n += 1
            pe.wait_ge(sem("sgu_v"), 1)
            pe.wait_ge(sem("sgw_masked"), 1)
            for g in range(SG):
                ins = mm(ps[:, 7, g * P:(g + 1) * P].rearrange("p (b c) -> p b c", b=NB), sgw[:, g, :],
                         vc[:, :, g * SG_D:(g + 1) * SG_D], start=True, stop=True)
            ins.then_inc(sem("sgu_psum"), 1)
            pe.wait_ge(sem("gate_g"), 1)
            for b in range(NB):
                ins = pe.transpose(ps[:, 5, b * ML_H:(b + 1) * ML_H], gt[0:ML_H, 3, b * P:(b + 1) * P], C("ident", ML_H, ML_H))
            ins.then_inc(sem("gcol_psum"), 1)

            def sb_scores(h):
                rows = slice(h % 2 * HD, h % 2 * HD + HD)
                if h >= 3:
                    pe.wait_ge(sem("sb_exp"), h - 2)
                q, k, z = qaT[rows, h // 2, :], kaT[rows, h // 2, :], ps[:, h % 3, :]
                mm(z[:, 0:SEQ], k[:, 0:P], q, start=True, stop=False, skip_group_check=True)
                mm(z[:, SEQ:3 * P], k[:, P:SEQ], q[:, P:SEQ], start=False, stop=False, skip_group_check=True)\
                    .then_inc(sem("sb_z"), 1)

            def sb_after(h):
                pe.wait_ge(sem("sb_sp"), h + 1)
                z, s = ps[:, h % 3, :], sp[:, h % 2, :]
                mm(z[:, 0:SEQ], C("negtri"), s[:, 0:SEQ], start=False, stop=False, skip_group_check=True)
                mm(z[:, P:SEQ], nones[:, :], s[:, SEQ:3 * P], start=False, stop=False, skip_group_check=True)
                mm(z[:, SEQ:3 * P], C("negtri"), s[:, SEQ:3 * P], start=False, stop=True, skip_group_check=True)\
                    .then_inc(sem("sb_E"), 1)

            def sb_values(h):
                c = h // 2
                pe.wait_ge(sem("sb_a"), h + 1)
                if h == 4:
                    pe.wait_ge(sem("sq_ready"), SQ0["sb_out"] + 1)
                o, w = ps[h % 2 * HD:h % 2 * HD + HD, 3 + c % 2, :], aw[:, h % 2, :]
                v = slice(h * HD, (h + 1) * HD)
                mm(o[:, 0:P], va[:, 0, v], w[:, 0:P], start=True, stop=True)
                mm(o[:, P:SEQ], va[:, 0, v], w[:, P:SEQ], start=True, stop=False)
                mm(o[:, P:SEQ], va[:, 1, v], w[:, SEQ:3 * P], start=False, stop=True).then_inc(sem("sb_o"), 1)

            pe.wait_ge(sem("z_evac"), Z_COUNT)
            for i in range(SB_H + 2):
                if i < SB_H:
                    sb_scores(i)
                if 1 <= i <= SB_H:
                    sb_after(i - 1)
                if i >= 2:
                    sb_values(i - 2)
            pe.wait_ge(sem("sgu_out"), NB)
            for c in range(SG_W // P):
                for b in range(NB):
                    ins = pe.transpose(ps[:, 7, c * SEQ + b * P:c * SEQ + b * P + P], uc[:, b, c * P:(c + 1) * P], ident)
            ins.then_inc(sem("yc_psum"), 1)
            for c in range(SB_C):
                sum_squares("sb_out", c, SEQ)

            pe.wait_ge(sem("cv_ready"), 1)
            pe.wait_ge(sem("em_ready"), 1)
            pe.wait_ge(sem("gcol_ready"), 1)
            pe.wait_ge(sem("yc_ready"), 1)
            pe.wait_ge(sem("sb_exp"), SB_H)
            for h in range(ML_H):
                if h:
                    pe.wait_ge(sem("ml_max"), 2 * h)
                    pe.wait_ge(sem("ml_em"), h)
                mm(ps[:, 5, :], ident[0:ML_H, h:h + 1].to_broadcast([ML_H, P]), gt[0:ML_H, 5:7, :].rearrange("p a t -> p (a t)"),
                   start=True, stop=True).then_inc(sem("ml_bc"), 1)
                if h >= 2:
                    pe.wait_ge(sem("ml_w"), h - 1)
                q, k, s = cv[0:ML_D, h, :], cv[0:ML_D, ML_H + h, :], ps[:, h % 2, :]
                mm(s[:, 0:SEQ], k[:, 0:P], q, start=True, stop=True)
                mm(s[:, SEQ:3 * P], k[:, P:SEQ], q[:, P:SEQ], start=True, stop=True).then_inc(sem("ml_s"), 1)
                pe.wait_ge(sem("ml_w"), h + 1)
                if h:
                    pe.wait_ge(sem("ml_h"), h)
                w, o = aw[:, h % 2, :], ps[0:ML_D, 7, :]
                v = slice(h * ML_D, (h + 1) * ML_D)
                for lhs0, lhs1, at in ((vb[:, 0, v], vb[:, 1, v], 0), (ones[:, 0:ML_D], ones[:, 0:ML_D], SEQ)):
                    mm(o[:, at:at + P], lhs0, w[:, 0:P], start=True, stop=True)
                    mm(o[:, at + P:at + SEQ], lhs0, w[:, P:SEQ], start=True, stop=False)
                    ins = mm(o[:, at + P:at + SEQ], lhs1, w[:, SEQ:3 * P], start=False, stop=True)
                ins.then_inc(sem("ml_num"), 1)
            pe.wait_ge(sem("ml_sq"), 1)
            for b in range(2):
                ins = mm(ps[0:ML_D, b, :].rearrange("p (a t) -> p a t", a=2), ones[0:ML_D, 0:ML_D],
                         mix[0:ML_D, 2 * b:2 * b + 2, 0:SEQ], start=True, stop=True)
            ins.then_inc(sem("ml_ss"), 1)
            pe.wait_ge(sem("ml_r"), 1)
            for c in range(KD):
                piece = FIRST_PIECE["w_out"] + c
                pe.wait_ge(sem("lo_done"), piece + 1)
                if c >= 4:
                    pe.wait_ge(sem("hs_ready"), 4 * KD + c - 3)
                for k, (_, rows) in enumerate(y_chunks()):
                    pe.wait_ge(sem("y_split"), k + 1)
                    at = slice(k * P, (k + 1) * P)
                    ins = mm3(ps[:, c % 4, 0:SEQ], (wh[0:rows, c % 2, at], wl[0:rows, c % 2, at]),
                              (xh[0:rows, k, :], xl[0:rows, k, :]), k == 0, k == 8)
                ins.then_inc(sem("wout_psum"), 1)

            for c in range(KD):
                sum_squares("norm2", c, SEQ)
            for b in range(NB):
                for k in range(KD):
                    pe.wait_ge(sem("xn_ready"), KD + k + 1)
                    ins = mm(ps[:, 0, b * 36:(b + 1) * 36], mix[:, k, b * P:(b + 1) * P], rw[:, k, :],
                             start=(k == 0), stop=(k == KD - 1))
            ins.then_inc(sem("router_psum"), 1)
            for b in range(NB):
                for c in range(KD):
                    q = b * 2 + c // 4
                    ins = pe.transpose(ps[:, 1 + q, c % 4 * P:c % 4 * P + P], mix[:, c, b * P:(b + 1) * P], ident)
                    if c % 4 == 3:
                        ins.then_inc(sem("h2_psum"), 1)
            pe.wait_ge(sem("onehot_ready"), 1)
            oh = onehot
            mm(ps[:, 5, 0:NE], C("strict"), oh(2)[:, 0, :], start=True, stop=True)
            mm(ps[:, 5, NE:2 * NE], ones[:, :], oh(2)[:, 0, :], start=True, stop=False)
            mm(ps[:, 5, NE:2 * NE], C("strict"), oh(2)[:, 1, :], start=False, stop=True)
            mm(ps[:, 5, 2 * NE:3 * NE], ones[:, :], oh(2)[:, 0, :], start=True, stop=False)
            mm(ps[:, 5, 2 * NE:3 * NE], ones[:, :], oh(2)[:, 1, :], start=False, stop=True).then_inc(sem("rank_psum"), 1)
            pe.wait_ge(sem("psel_ready"), 1)
            pe.wait_ge(sem("h2l_ready"), 4)
            for c in range(KD):
                if c >= 4:
                    pe.wait_ge(sem("xs_ready" if c % 2 else "xs_ready_d"), c // 2 - 1)
                for b in range(NB):
                    for src in (h2h, h2l):
                        ins = mm(ps[:, c % 4, :], src[:, b, c * P:(c + 1) * P], psel[:, b, :],
                                 start=(b == 0 and src is h2h), stop=(b == NB - 1 and src is h2l))
                ins.then_inc(sem("xs_psum"), 1)
            pe.wait_ge(sem("combt_ready"), 1)
            for r in range(4):
                for b in range(NB):
                    ins = pe.transpose(ps[:, 6 + r // 2, r % 2 * SEQ + b * P:r % 2 * SEQ + b * P + P],
                                       combt[:, b, r * P:(r + 1) * P], ident)
                if r % 2:
                    ins.then_inc(sem("comb_psum"), 1)
            slot, rnd = tile_at(FIRST["w_proj"])
            pe.wait_ge(sem(f"tile_ready{slot}"), 16 * (rnd + 1))
            wp = ring[:, slot, 0:2048].rearrange("p (k n) -> p k n", k=2)
            pt = ring[:, slot, 2048:2560].rearrange("p (k t) -> p k t", k=2)
            pe.wait_ge(sem("comb_ready"), 2)
            for c in range(KD):
                if c >= 2:
                    pe.wait_ge(sem("pp_ready"), c - 1)
                for k in range(2):
                    ins = mm(ps[:, 4 + c % 2, 0:SEQ], wp[:, k, c * P:(c + 1) * P], pt[:, k, :], start=(k == 0), stop=(k == 1))
                ins.then_inc(sem("pp_psum"), 1)
            pe.wait_ge(sem("pp_ready"), KD)
            pe.wait_ge(sem("xs_ready"), KD // 2)
            pe.wait_ge(sem("xs_ready_d"), KD // 2)
            pe.wait_ge(sem("route_ready"), 2)

            def gate_up(e, count):
                def body(halves):
                    for j in range(4):
                        pe.wait_ge(sem("elo_done"), gu_piece_of(e) + (j + 1))
                        pe.wait_ge(sem("xe_ready"), e * 4 + (j + 1))
                        if j == 0 and (type(e) is not int or e):
                            pe.wait_ge(sem("he_ready"), e)
                        b = expert_buffer(j, False, e)
                        for i in range(2):
                            k = 2 * j + i
                            w = slice(i * 512, (i + 1) * 512)
                            for half in range(halves):
                                x = [v[:, k, half * HALF:(half + 1) * HALF] for v in (xeh, xel)]
                                ins = mm3(ps[:, half, :], x, (ewh[:, b, w], ewl[:, b, w]), k == 0, k == KD - 1)
                        ins.then_inc(sem("e_used"), 1)
                for_halves(pe, count, body)

            def transposes(e, count):
                def body(halves):
                    pe.wait_ge(sem("he_ready"), e + 1)
                    for half in range(halves):
                        for c in range(FE // P):
                            ins = pe.transpose(ps[:, 6 + half, c * P:(c + 1) * P], he[:, half, c * P:(c + 1) * P], ident)
                    ins.then_inc(sem("het_psum"), 1)
                for_halves(pe, count, body)

            def down(e, count):
                def body(halves):
                    for k in range(2):
                        pe.wait_ge(sem("elo_done"), dn_piece_of(e) + (k + 1))
                        if k == 0:
                            pe.wait_ge(sem("het_ready"), e + 1)
                            if type(e) is not int or e:
                                pe.wait_ge(sem("y_ready"), e)
                        b = expert_buffer(k, True, e)
                        for i in range(2):
                            w = slice(i * 512, (i + 1) * 512)
                            for half in range(halves):
                                ins = mm3(ps[:, 2 + 2 * half + i, :], (heTh[:, half, k, :], heTl[:, half, k, :]),
                                          (ewh[:, b, w], ewl[:, b, w]), k == 0, k == 1)
                        ins.then_inc(sem("e_used"), 1)
                for_halves(pe, count, body)

            def step(slot, rnd, e):
                transposes(e, value(pe, 1, e))
                gate_up(e + 1, value(pe, 1, e + 1))
                down(e, value(pe, 1, e))

            gate_up(0, value(pe, 1, 0))
            step(*tile_at(FIRST["w_exp"]), 0)
            ring_steps(pe, "w_exp", step, first=1, last=NE - 1)
            transposes(NE - 1, value(pe, 1, NE - 1))
            down(NE - 1, value(pe, 1, NE - 1))
            pe.wait_ge(sem("ysr_loaded"), 16)
            pe.wait_ge(sem("y_ready"), NE)
            for c in range(KD):
                if c >= 4:
                    pe.wait_ge(sem("hs_ready"), 5 * KD + c - 3)
                for r in range(4):
                    ins = mm(ps[:, c % 4, 0:SEQ], ysr[:, r, c * P:(c + 1) * P], combr[:, r, :], start=(r == 0), stop=(r == 3))
                ins.then_inc(sem("moe_psum"), 1)

            for c in range(KD):
                sum_squares("ple", c, SEQ)
            for c in range(KD):
                piece = FIRST_PIECE["w_ple"] + c // 2
                pe.wait_ge(sem("lo_done"), piece + 1)
                if c >= 4:
                    pe.wait_ge(sem("ple_sig"), c - 3)
                for k in range(KD):
                    pe.wait_ge(sem("x_ready"), 4 * KD + k + 1)
                    at = slice(k * 256 + c % 2 * P, k * 256 + c % 2 * P + P)
                    ins = mm3(ps[:, c % 4, 0:SEQ], (wh[:, piece % 2, at], wl[:, piece % 2, at]),
                              (xh[:, k, 0:SEQ], xl[:, k, 0:SEQ]), k == 0, k == KD - 1)
                ins.then_inc(sem("ple_psum"), 1)
            for c in range(KD):
                sum_squares("final", c, SEQ)

        def normed(dve, dst, src, name, c, r):
            return dve.scalar_tensor_tensor(dst, src, V(name, c), r, ALU.mult, ALU.mult)

        def post_apply(dve, k, norm, n):
            dve.wait_ge(sem("r_ready"), NORM[norm] + 1)
            for c in range(KD):
                dve.wait_ge(sem("mix_ready"), k * KD + c + 1)
                normed(dve, mix[:, c, 0:n], mix[:, c, 0:n], norm, c, r_of(norm)[:, 0:n]).then_inc(sem("delta_ready"), 1)

        def x_low(dve, u, c, full, high, low):
            dve.wait_ge(sem("xh_ready"), u * KD + c + 1)
            dve.tensor_tensor(low, full, high.bitcast(F32), ALU.subtract).then_inc(sem("x_ready"), 1)

        def ffn_dve(dve, l, n, cols):
            gu, dn, pre, post = f"w_gu{l}", f"w_dn{l}", f"ffnpre{l}", f"ffnpost{l}"
            xa, xb = (xhT, xlT) if l == 0 else (xh, xl)
            r = r_of(pre)[:, 0:n]
            for args in halves(gu, 0, PIECE):
                split_lo(dve, gu, *args)
            for c in range(KD):
                dve.wait_ge(sem("xh_ready"), 2 * l * KD + c + 1)
                dve.scalar_tensor_tensor(xb[:, c, 0:n], hs[:, c, cols], V(pre, c), xa[:, c, 0:n].bitcast(F32),
                                         ALU.mult, ALU.subtract).then_inc(sem("x_ready"), 1)
            dve.wait_ge(sem("r_ready"), NORM[pre] + 1)

            def gate(f, j):
                dve.wait_ge(sem("gu_psum"), f + (l * NF + 1))
                dve.tensor_tensor(mix[:, j, 0:n], ps[:, 2 * j, 0:n], r, ALU.mult).then_inc(sem("gr_ready"), 1)

            def up(j):
                dve.tensor_tensor(mix[:, 4 + j, 0:n], ps[:, 2 * j + 1, 0:n], r, ALU.mult).then_inc(sem("up_ready"), 1)

            def body(slot, rnd, i):
                for j in range(2):
                    f = i * 2 + (j - 2)
                    if not (type(i) is int and i == 1):
                        dve.wait_ge(sem("act_ready"), f + (l * NF - 1))
                    gate(f, j)
                    split_lo(dve, gu, slot, rnd, i, j, PIECE)
                    up(j)

            body(*tile_at(FIRST[gu] + 1), 1)
            ring_steps(dve, gu, body, first=2)
            for j in range(2):
                dve.wait_ge(sem("act_ready"), NF - 2 + j + l * NF - 1)
                gate(NF - 2 + j, j)
                up(j)
            for i in range(KD):
                for args in halves(dn, i, FF // 2):
                    split_lo(dve, dn, *args)
            post_apply(dve, 2 * l + 1, post, n)

        def first_of_ties(dve, chain, values, top, order, key, oh):
            n = values.shape[-1]
            chain(dve.tensor_tensor(key, values, top.unsqueeze(2).to_broadcast([P, NB, n]), ALU.is_equal))
            chain(dve.tensor_tensor(key, key, order.unsqueeze(1).to_broadcast([P, NB, n]), ALU.mult))
            chain(dve.tensor_reduce(small[:, 410:412], key, AX.X, ALU.max))
            chain(dve.tensor_tensor(oh, key, small[:, 410:412].unsqueeze(2).to_broadcast([P, NB, n]), ALU.is_equal))

        def routing(dve, chain):
            scr = rscr
            width = NGRP + NE
            rl = scr[:, 0:NB * width].rearrange("p (b n) -> p b n", b=NB)
            at = NB * width

            def room(n):
                nonlocal at
                at += NB * n
                return scr[:, at - NB * n:at].rearrange("p (b n) -> p b n", b=NB)

            key4, oh4, el, key, pos, desc = room(NGRP), room(NGRP), room(NE), room(NE), room(NE), scr[:, 1024:1024 + NE]
            gl = small[:, 128:136].rearrange("p (b n) -> p b n", b=NB)
            gmax, gsum, v1, v2, rec = (small[:, 140 + 2 * i:142 + 2 * i] for i in range(5))
            pos1, pos2, w1, w2 = (small[:, 160 + 2 * i:162 + 2 * i] for i in range(4))
            ex = small[:, 180:182]
            dve.wait_ge(sem("router_psum"), 1)
            chain(dve.tensor_tensor(rl, ps[:, 0, 0:NB * width].rearrange("p (b n) -> p b n", b=NB),
                                    R("router_b", width).unsqueeze(1).to_broadcast([P, NB, width]), ALU.add))
            chain(dve.tensor_reduce(gmax, rl[:, :, 0:NGRP], AX.X, ALU.max))
            dve.tensor_tensor(gl, rl[:, :, 0:NGRP], gmax.unsqueeze(2).to_broadcast([P, NB, NGRP]), ALU.subtract)\
               .then_inc(sem("route_g"), 1)
            first_of_ties(dve, chain, rl[:, :, 0:NGRP], gmax, R("desc", NGRP), key4, oh4)
            oh4x = oh4.unsqueeze(3).to_broadcast([P, NB, NGRP, EPG])
            el4 = el.rearrange("p b (g e) -> p b g e", e=EPG)
            key44 = key.rearrange("p b (g e) -> p b g e", e=EPG)
            chain(dve.tensor_scalar(key44, oh4x, 3e38, -3e38, ALU.mult, ALU.add))
            chain(dve.tensor_tensor(el4, rl[:, :, NGRP:].rearrange("p b (g e) -> p b g e", e=EPG), oh4x, ALU.mult))
            chain(dve.tensor_tensor(el, el, key, ALU.add))
            dve.wait_ge(sem("iota_ready"), 1)
            chain(dve.tensor_scalar(desc, iota[:, 0:NE], -1.0, float(NE), ALU.mult, ALU.add))
            chain(dve.tensor_reduce(v1, el, AX.X, ALU.max))
            first_of_ties(dve, chain, el, v1, desc, key, onehot(0))
            chain(dve.scalar_tensor_tensor(el, onehot(0), -3e38, el, ALU.mult, ALU.add))
            chain(dve.tensor_reduce(v2, el, AX.X, ALU.max))
            first_of_ties(dve, chain, el, v2, desc, key, onehot(1))
            dve.tensor_tensor(onehot(2), onehot(0), onehot(1), ALU.add).then_inc(sem("onehot_ready"), 1)
            dve.tensor_tensor(ex, v2, v1, ALU.subtract).then_inc(sem("route_d"), 1)
            dve.wait_ge(sem("rank_psum"), 1)
            count, incl = scr[:, 1100:1100 + NE], scr[:, 1200:1200 + NE]
            chain(dve.tensor_copy(count, ps[:, 5, 2 * NE:3 * NE]))
            chain(dve.tensor_tensor_scan(incl, count, count, 0.0, ALU.add, ALU.max))
            chain(dve.tensor_tensor(incl, incl, count, ALU.subtract))
            dve.tensor_copy(route_i[:, 0, :], incl).then_inc(sem("route_ready"), 1)
            dve.tensor_copy(route_i[:, 1, :], count).then_inc(sem("route_ready"), 1)
            chain(dve.tensor_tensor(pos, ps[:, 5, 0:NB * NE].rearrange("p (b e) -> p b e", b=NB),
                                    incl.unsqueeze(1).to_broadcast([P, NB, NE]), ALU.add))
            for oh, p in ((onehot(0), pos1), (onehot(1), pos2)):
                chain(dve.tensor_tensor(key, oh, pos, ALU.mult))
                chain(dve.tensor_reduce(p, key, AX.X, ALU.add))
            for b in range(NB):
                first = scr[:, 2048 + b * ROWS:2048 + (b + 1) * ROWS]
                chain(dve.tensor_scalar(first, iota[:, :], pos1[:, b:b + 1], None, ALU.is_equal))
                ins = dve.scalar_tensor_tensor(psel[:, b, :], iota[:, :], pos2[:, b:b + 1], first, ALU.is_equal, ALU.add)
            ins.then_inc(sem("psel_ready"), 1)
            dve.wait_ge(sem("route_gexp"), 1)
            dve.wait_ge(sem("route_ex"), 1)
            chain(dve.tensor_reduce(gsum, gl, AX.X, ALU.add))
            chain(dve.tensor_scalar(rec, ex, 1.0, None, ALU.add))
            chain(dve.tensor_tensor(rec, rec, gsum, ALU.mult))
            chain(dve.reciprocal(w1, rec))
            chain(dve.tensor_tensor(w2, ex, w1, ALU.mult))
            second = scr[:, 1536:1536 + ROWS]
            for b in range(NB):
                chain(dve.tensor_scalar(combt[:, b, :], iota[:, :], pos1[:, b:b + 1], w1[:, b:b + 1], ALU.is_equal, ALU.mult))
                chain(dve.tensor_scalar(second, iota[:, :], pos2[:, b:b + 1], w2[:, b:b + 1], ALU.is_equal, ALU.mult))
                ins = dve.tensor_tensor(combt[:, b, :], combt[:, b, :], second, ALU.add)
                if b == 0:
                    chain(ins)
            ins.then_inc(sem("combt_ready"), 1)

        @block.vector
        def _(dve):
            chain = Chain(dve, "dve_chain")
            dve.wait_ge(sem("consts_loaded"), 32)
            dve.wait_ge(sem("hs_loaded"), 16)
            dve.wait_ge(sem("r_ready"), 1)
            for c in range(KD):
                normed(dve, hp[:, c, PADT:], hs[:, c, :], "mixpre0", c, r_of("mixpre0")).then_inc(sem("h_ready"), 1)
            pool_groups(dve, chain, (2, 3), "p_dve")
            post_apply(dve, 0, "mixpost0", T)
            ffn_dve(dve, 0, T, slice(0, T))

            dve.wait_ge(sem("r_ready"), NORM["pre1"] + 1)
            dve.wait_ge(sem("dn_psum"), 2 * KD)
            r = r_of("pre1")
            for c in range(KD):
                normed(dve, mix[:, c, :], hs[:, c, :], "kv_norm", c, r).then_inc(sem("kvin_ready"), 1)
            for c in range(KD):
                normed(dve, h1[:, c, :], hs[:, c, N_META:], "mixpre1", c, r[:, N_META:]).then_inc(sem("h1_ready"), 1)
            for x in halves("w_q", 0, PIECE):
                split_lo(dve, "w_q", *x)
            for c in range(KD):
                x_low(dve, 1, c, h1[:, c, :], xh[:, c, :], xl[:, c, :])
            dve.wait_ge(sem("tables_loaded"), 64)
            dve.wait_ge(sem("kv_psum"), 3)
            b_v = R("b_v", P)
            dve.tensor_tensor(vtok[0:N_META, 0, :], ps[0:N_META, 2, 0:P], b_v[0:N_META, :], ALU.add).then_inc(sem("v_ready"), 1)
            dve.tensor_tensor(vtok[:, 1:3, :], ps[:, 2, P:3 * P].rearrange("p (b n) -> p b n", b=NB),
                              b_v.unsqueeze(1).to_broadcast([P, NB, P]), ALU.add).then_inc(sem("v_ready"), 1)
            low = {1: ("w_q", halves("w_q", 1, PIECE)[0]), 3: ("w_q", halves("w_q", 1, PIECE)[1]),
                   5: ("w_o", halves("w_o", 0, PIECE)[0]), 7: ("w_o", halves("w_o", 0, PIECE)[1])}
            for c in range(KD):
                dve.wait_ge(sem("q_psum"), c + 1)
                dve.tensor_scalar(qT[:, c, :].rearrange("p (b q) -> p b q", q=P)[:, :, ::-1],
                                  ps[:, c % 4, 0:SEQ].rearrange("p (b q) -> p b q", q=P), V("b_q", c), HD ** -0.5,
                                  ALU.add, ALU.mult).then_inc(sem("q_ready"), 1)
                if c in low:
                    split_lo(dve, low[c][0], *low[c][1])

            PER = NB * HEADS_PER_GROUP

            def logits(g):
                if g == 0:
                    dve.wait_ge(sem("bias_ready"), 16)
                for i in range(PER * g, PER * (g + 1)):
                    n, first = (N_META + P, P - N_META) if i % 2 == 0 else (2 * P, 0)
                    dve.wait_ge(sem("s_psum"), i + 1)
                    dve.tensor_tensor_reduce(out=lg[g % 2][:, i % PER, 0:n], in0=ps[:, i % 4, 0:n],
                                             in1=brev[:, i // 2, first:SEQ], scale=1.0, scalar=-3e38,
                                             op0=ALU.add, op1=ALU.max, accum_out=small[:, i:i + 1])\
                       .then_inc(sem("lg_ready"), 1)
                k = PER * g
                dve.wait_ge(sem("lg_ready"), PER * (g + 1))
                m = small[:, k:k + PER].rearrange("p (h b) -> p h b", b=NB)
                sink = R("sinks", HEADS_PER_GROUP, HEADS_PER_GROUP * g).unsqueeze(2).to_broadcast([P, HEADS_PER_GROUP, NB])
                chain(dve.tensor_tensor(m, m, sink, ALU.max))
                chain(dve.tensor_tensor(small[:, 64 + k:64 + k + PER].rearrange("p (h b) -> p h b", b=NB), sink, m, ALU.subtract))
                dve.tensor_scalar(small[:, 32 + k:32 + k + PER], small[:, k:k + PER], -1.0, None, ALU.mult)\
                   .then_inc(sem("negm_ready"), 1)

            GROUPS = NH // HEADS_PER_GROUP
            logits(0)
            for g in range(GROUPS):
                if g + 1 < GROUPS:
                    if g:
                        dve.wait_ge(sem("pt_psum"), HEADS_PER_GROUP * g)
                    logits(g + 1)
                k = PER * g
                dve.wait_ge(sem("exp_ready"), (PER + 1) * (g + 1))
                den = small[:, 96 + k:96 + k + PER]
                chain(dve.tensor_tensor(den, den, small[:, 64 + k:64 + k + PER], ALU.add))
                chain(dve.reciprocal(den, den))
                for i in range(PER):
                    n = N_META + P if i % 2 == 0 else 2 * P
                    v = lg[g % 2][:, i, 0:n]
                    dve.tensor_scalar(v, v, den[:, i:i + 1], None, ALU.mult).then_inc(sem("p_ready"), 1)
                for h in range(HEADS_PER_GROUP * g, HEADS_PER_GROUP * (g + 1)):
                    if h % 2 == 1:
                        c = h // 2
                        dve.wait_ge(sem("oh_ready"), c + 1)
                        o = ps[:, 6 + c % 2, 0:SEQ].rearrange("p (b q) -> p b q", q=P)[:, :, ::-1]
                        dve.tensor_tensor(xl[:, c, :].rearrange("p (b q) -> p b q", q=P), o,
                                          xh[:, c, :].bitcast(F32).rearrange("p (b q) -> p b q", q=P), ALU.subtract)\
                           .then_inc(sem("o_ready"), 1)
            for x in halves("w_o", 1, PIECE):
                split_lo(dve, "w_o", *x)
            post_apply(dve, 2, "mixpost1", SEQ)
            ffn_dve(dve, 1, SEQ, slice(N_META, T))

            for x in halves("w_z", 0, PIECE):
                split_lo(dve, "w_z", *x)

            def norm_input(name):
                dve.wait_ge(sem("r_ready"), NORM[name] + 1)
                for c in range(KD):
                    normed(dve, mix[:, c, 0:SEQ], hs[:, c, N_META:], name, c, r_of(name)[:, 0:SEQ])\
                        .then_inc(sem("xn_ready"), 1)

            norm_input("norm1")
            for c in range(KD):
                x_low(dve, 3, c, mix[:, c, 0:SEQ], xh[:, c, :], xl[:, c, :])
            for piece in range(2, 14):
                split_lo(dve, "w_z", *halves("w_z", piece // 2, PIECE)[piece % 2])
                if piece >= 4 and piece - 4 < 2 * ML_H:
                    conv(dve, chain, piece - 4, "conv_done")

            dve.wait_ge(sem("z_evac"), Z_COUNT)
            groups = vc.rearrange("p b (g c) -> p (b g) c", c=SG_D)
            NG = NB * SG
            chain(dve.tensor_reduce(small[:, 0:NG], groups, AX.X, ALU.add))
            dve.scalar_tensor_tensor(groups, small[:, 0:NG].unsqueeze(2).to_broadcast([P, NG, SG_D]), -1.0 / SG_D, groups,
                                     ALU.mult, ALU.add).then_inc(sem("sgu_centred"), 1)
            g4 = [gt[0:ML_H, i, :] for i in range(7)]
            dve.wait_ge(sem("gate_ln"), 1)
            chain(dve.tensor_scalar(g4[1], g4[1], 0.0, None, ALU.min))
            chain(dve.tensor_tensor_scan(g4[4], g4[1], g4[2], 0.0, ALU.add, ALU.subtract))
            dve.tensor_tensor(g4[3], g4[0], g4[4], ALU.subtract).then_inc(sem("gate_g"), 1)
            dve.wait_ge(sem("gate_g"), 1)
            chain(dve.tensor_tensor_scan(g4[5], g4[3], g4[3], 0.0, ALU.max, ALU.max))
            dve.tensor_tensor(g4[6], g4[4], g4[5], ALU.add).then_inc(sem("gate_m"), 1)
            dve.wait_ge(sem("sgu_sq"), 1)
            dve.tensor_reduce(small[:, 8:8 + NG].rearrange("p (b g) -> p b g", g=SG),
                              mix[:, 0:2, 0:SG_W].rearrange("p b (g c) -> p b g c", c=SG_D), AX.X, ALU.add)\
               .then_inc(sem("sgu_var"), 1)
            dve.wait_ge(sem("ob_exp"), 1)
            chain(dve.tensor_scalar(ob[0:ML_D, :, :], ob[0:ML_D, :, :], 1.0, None, ALU.add))
            chain(dve.reciprocal(ob[0:ML_D, :, :], ob[0:ML_D, :, :]))
            dve.wait_ge(sem("sgu_r"), 1)
            chain(dve.tensor_tensor(groups, groups, small[:, 8:8 + NG].unsqueeze(2).to_broadcast([P, NG, SG_D]), ALU.mult))
            chain(dve.tensor_tensor(vc, vc, R("ln_g", SG_W).unsqueeze(1).to_broadcast([P, NB, SG_W]), ALU.mult))
            dve.tensor_tensor(vc, vc, R("ln_b", SG_W).unsqueeze(1).to_broadcast([P, NB, SG_W]), ALU.add)\
               .then_inc(sem("sgu_v"), 1)
            dve.wait_ge(sem("gcol_psum"), 1)
            dve.tensor_copy(small[:, 20:20 + NB * ML_H], ps[:, 5, 0:NB * ML_H]).then_inc(sem("gcol_ready"), 1)
            dve.wait_ge(sem("sgu_psum"), 1)
            for g in range(SG):
                u = uc[:, :, g * SG_D:(g + 1) * SG_D]
                dve.scalar_tensor_tensor(u, ps[:, 7, g * P:(g + 1) * P].rearrange("p (b c) -> p b c", b=NB), V("sgu_b", g), u,
                                         ALU.add, ALU.mult).then_inc(sem("sgu_y"), 1)
            dve.wait_ge(sem("sgu_yr"), 1)
            for b in range(NB):
                dve.scalar_tensor_tensor(uc[:, b, :], uc[:, b, :], small[:, 16 + b:17 + b], R("sgu_out", SG_W),
                                         ALU.mult, ALU.mult).then_inc(sem("sgu_out"), 1)

            for i in range(SB_H):
                dve.wait_ge(sem("sb_ln"), i + 1)
                if i >= 2:
                    dve.wait_ge(sem("sb_E"), i - 1)
                s = sp[:, i % 2, :]
                chain(dve.scalar_tensor_tensor(s, ps[:, i % 3, 0:3 * P], 0.0, e1[:, i % 2, :], ALU.max, ALU.add))
                diag = s.rearrange("p (a b) -> p a b", a=3)[:, 0:3:2, :]
                dve.tensor_tensor(diag, diag, C("strict").unsqueeze(1).to_broadcast([P, 2, P]), ALU.mult)\
                   .then_inc(sem("sb_sp"), 1)

            for h in range(ML_H):
                dve.wait_ge(sem("ml_bc"), h + 1)
                for b, cols in ((0, slice(0, SEQ)), (1, slice(SEQ, 3 * P))):
                    at = 20 + ML_H * b + h
                    dve.tensor_scalar(sp[:, h % 2, cols], ps[:, 5, b * P:SEQ], small[:, at:at + 1], None, ALU.max)\
                       .then_inc(sem("ml_max"), 1)
                dve.wait_ge(sem("ml_s"), h + 1)
                dve.wait_ge(sem("ml_d"), h + 1)
                w = aw[:, h % 2, :]
                dve.scalar_tensor_tensor(w, ps[:, h % 2, 0:3 * P], ML_D ** -0.5, w, ALU.mult, ALU.mult)\
                   .then_inc(sem("ml_w"), 1)
                dve.wait_ge(sem("ml_num"), h + 1)
                dve.wait_ge(sem("ml_em"), h + 1)
                den = e1[0:ML_D, h % 2, 0:SEQ]
                raw = ps[0:ML_D, 7, SEQ:2 * SEQ]
                chain(dve.tensor_tensor(den, raw, den, ALU.max))
                chain(dve.scalar_tensor_tensor(den, raw, -1.0, den, ALU.mult, ALU.max))
                chain(dve.reciprocal(den, den))
                dve.tensor_tensor(yb[0:ML_D, h, :], ps[0:ML_D, 7, 0:SEQ], den, ALU.mult).then_inc(sem("ml_h"), 1)
            for x in halves("w_out", 0, 9 * P):
                split_lo(dve, "w_out", *x)
            dve.wait_ge(sem("r_ready"), NORM["sb_out"] + 1)
            dve.wait_ge(sem("ya_ready"), SB_C)
            for c in range(SB_C):
                normed(dve, yaT[:, c, :], yaT[:, c, :], "sb_out", c, r_of("sb_out")[:, 0:SEQ]).then_inc(sem("y_fin"), 1)
            dve.wait_ge(sem("ml_r"), 1)
            for h in range(ML_H):
                y = yb[0:ML_D, h, :]
                chain(dve.scalar_tensor_tensor(y, y, V("mnorm", h, ML_D), mix[0:ML_D, ML_H + h, 0:SEQ], ALU.mult, ALU.mult))
                dve.tensor_tensor(y, y, ob[0:ML_D, h, :], ALU.mult).then_inc(sem("y_fin"), 1)
            for j, (src, rows) in enumerate(y_chunks()):
                dve.wait_ge(sem("yh_ready"), j + 1)
                dve.tensor_tensor(xl[0:rows, j, :], src, xh[0:rows, j, :].bitcast(F32), ALU.subtract)\
                   .then_inc(sem("y_split"), 1)
            for c in range(KD):
                if c + 2 < KD:
                    split_lo(dve, "w_out", *halves("w_out", (c + 2) // 2, 9 * P)[c % 2])
                dve.wait_ge(sem("wout_psum"), c + 1)
                dve.tensor_tensor(hs[:, c, N_META:], hs[:, c, N_META:], ps[:, c % 4, 0:SEQ], ALU.add)\
                   .then_inc(sem("hs_ready"), 1)

            norm_input("norm2")
            for q in range(4):
                dve.wait_ge(sem("h2_ready"), q + 1)
                at = slice(q % 2 * 512, (q % 2 + 1) * 512)
                dve.tensor_tensor(h2l[:, q // 2, at], ps[:, 1 + q, :], h2h[:, q // 2, at].bitcast(F32), ALU.subtract)\
                   .then_inc(sem("h2l_ready"), 1)
            routing(dve, chain)
            for c in range(0, KD, 2):
                dve.wait_ge(sem("xs_psum"), c + 1)
                dve.tensor_copy(xs[:, c * XS:c * XS + ROWS], ps[:, c % 4, :]).then_inc(sem("xs_ready_d"), 1)

            def low(e, j, is_down, slot):
                g = (dn_piece_of(e) if is_down else gu_piece_of(e)) + j
                b = expert_buffer(j, is_down, e)
                dve.wait_ge(sem("ehi_done"), g + 1)
                at = (4096 if is_down else 0) + j * EPIECE
                dve.tensor_tensor(ewl[:, b, :], ring[:, slot, at:at + EPIECE], ewh[:, b, :].bitcast(F32), ALU.subtract)\
                   .then_inc(sem("elo_done"), 1)

            def gated(e, count):
                def body(halves):
                    dve.wait_ge(sem("sg_ready"), e + 1)
                    dve.tensor_tensor(he[:, 0:halves, :], sgate[:, 0:halves, :], ps[:, 0:halves, FE:2 * FE], ALU.mult)\
                       .then_inc(sem("he_ready"), 1)
                for_halves(dve, count, body)

            def transposed(e, count):
                def body(halves):
                    dve.wait_ge(sem("heth_ready"), e + 1)
                    dve.tensor_tensor(heTl[:, 0:halves, :, :].rearrange("p a c n -> p a (c n)"), ps[:, 6:6 + halves, 0:FE],
                                      heTh[:, 0:halves, :, :].bitcast(F32).rearrange("p a c n -> p a (c n)"), ALU.subtract)\
                       .then_inc(sem("het_ready"), 1)
                for_halves(dve, count, body)

            def step(slot, rnd, e):
                nxt = (slot + 1) % SLOTS
                low(e + 1, 0, False, nxt)
                count = value(dve, 1, e)
                gated(e, count)
                low(e + 1, 1, False, nxt)
                low(e + 1, 2, False, nxt)
                transposed(e, count)
                low(e + 1, 3, False, nxt)
                for j in range(2):
                    low(e, j, True, slot)

            slot, rnd = tile_at(FIRST["w_exp"])
            for j in range(4):
                low(0, j, False, slot)
            step(slot, rnd, 0)
            ring_steps(dve, "w_exp", step, first=1, last=NE - 1)
            last = NE - 1
            slot, rnd = tile_at(FIRST["w_exp"] + last)
            gated(last, value(dve, 1, last))
            low(last, 0, True, slot)
            transposed(last, value(dve, 1, last))
            low(last, 1, True, slot)
            for c in range(KD):
                dve.wait_ge(sem("moe_psum"), c + 1)
                dve.tensor_tensor(hs[:, c, N_META:], hs[:, c, N_META:], ps[:, c % 4, 0:SEQ], ALU.add)\
                   .then_inc(sem("hs_ready"), 1)

            for x in halves("w_ple", 0, PIECE):
                split_lo(dve, "w_ple", *x)
            norm_input("ple")
            for c in range(KD):
                x_low(dve, 4, c, mix[:, c, 0:SEQ], xh[:, c, :], xl[:, c, :])
            for c in range(KD):
                if c in (0, 2):
                    split_lo(dve, "w_ple", *halves("w_ple", 1, PIECE)[c // 2])
                dve.wait_ge(sem("ple_sig"), c + 1)
                dve.wait_ge(sem("pp_ready"), KD)
                dve.tensor_tensor(mix[:, c, 0:SEQ], mix[:, c, 0:SEQ], ppT[:, c, :], ALU.mult).then_inc(sem("delta_ready"), 1)
            dve.wait_ge(sem("r_ready"), NORM["final"] + 1)
            for c in range(KD):
                normed(dve, mix[:, c, 0:SEQ], hs[:, c, N_META:], "final", c, r_of("final")[:, 0:SEQ])\
                    .then_inc(sem("out_ready"), 1)


def _pieces(w, cols):
    import numpy as _np
    n = w.shape[1] // cols
    x = w.reshape(w.shape[0] // P, P, n // 2, 2, cols)
    return _np.ascontiguousarray(x.transpose(2, 1, 3, 0, 4)).reshape(n // 2, P, -1)


def _t5_buckets():
    import math
    import numpy as _np
    n, far = 32, 128
    half = n // 2
    d = _np.arange(P)
    df = _np.maximum(d, 1).astype(_np.float32)
    large = half + (_np.log(df / _np.float32(half)) / _np.float32(math.log(far / half))
                    * _np.float32(n - half)).astype(_np.int32)
    return _np.where(d < half, d, _np.minimum(large, n - 1))


def kernel(**inputs):
    import numpy as _np
    import concourse.bacc as _bacc
    from concourse import mybir as _mybir
    from concourse.bass_utils import run_bass_kernel_spmd as _run

    x = {k: _np.asarray(v) for k, v in inputs.items()}
    f32 = _np.float32
    a = {}
    seq = _np.concatenate([x["meta_tokens"], x["x"][0]], axis=0)
    a["hT"] = seq.T.reshape(KD, P, T).transpose(1, 0, 2)

    vec = _np.zeros((P, NV), f32)

    def put(name, v, rows=P):
        v = v.reshape(-1, rows).T
        vec[0:rows, VCOL[name]:VCOL[name] + v.shape[1]] = v

    for l in range(2):
        put(f"mixpre{l}", x["norm_mix_pre"][l])
        put(f"mixpost{l}", x["norm_mix_post"][l])
        put(f"ffnpre{l}", x["norm_ffn_pre"][l])
        put(f"ffnpost{l}", x["norm_ffn_post"][l])
    put("kv_norm", x["kv_norm"])
    put("pool_scale", x["pool_scale"][0])
    put("norm1", x["norm1_g_2"][0])
    put("norm2", x["norm2_g_2"][0])
    put("ple", x["ple_norm_g_2"][0])
    put("final", x["final_g_2"])
    put("b_q", x["b_q"][0])
    put("b_o", x["b_o"][0])
    put("b_k", _np.concatenate([x["b_k"][0:HD], x["b_k"][0:HD], x["b_k"][HD:], x["b_k"][HD:]]))
    put("sb_out", x["sb_out_g_2"][0])
    put("conv_w", x["conv_w_2"][0].reshape(4, 2 * ML_H, ML_D).transpose(1, 0, 2), ML_D)
    put("conv_b", x["conv_b_2"][0], ML_D)
    put("mnorm", x["mnorm_g_2"][0], ML_D)
    put("igate_b", x["igate_b_2"][0], ML_H)
    put("fgate_b", x["fgate_b_2"][0], ML_H)
    put("sgu_b", x["sgu_b_2"][0])
    a["vec"] = vec

    row = _np.concatenate([x["sinks"][0], x["b_v"], x["sgu_ln_g_2"][0], x["sgu_ln_b_2"][0], x["sgu_out_g_2"][0],
                           x["router_gb_2"][0], x["router_eb_2"][0], _np.arange(NGRP, 0, -1).astype(f32)])
    a["row"] = _np.broadcast_to(row[None], (P, NR))

    cst = _np.zeros((P, NC), f32)
    i, j = _np.arange(P)[:, None], _np.arange(P)[None, :]
    cst[:, CCOL["ident"]:CCOL["ident"] + P] = i == j
    cst[:, CCOL["strict"]:CCOL["strict"] + P] = i < j
    cst[:, CCOL["negtri"]:CCOL["negtri"] + P] = -(i >= j).astype(f32)
    cst[:, CCOL["sgumask"]:CCOL["sgumask"] + P] = i // 64 <= j // 64
    for g, w in enumerate(WINDOWS):
        at = CCOL["invcnt"] + g * PADT
        cst[:, at:at + PADT] = f32(1) / _np.minimum(_np.arange(1, PADT + 1), w).astype(f32)
    cst[0:32, CCOL["buckets"]:CCOL["buckets"] + P] = _np.arange(32)[:, None] == _t5_buckets()[::-1][None, :]
    a["cst"] = cst
    a["rel_bias"] = x["rel_bias"]
    rw = _np.concatenate([x["router_gw_2"][0], x["router_ew_2"][0]], axis=1)
    a["rw"] = rw.reshape(KD, P, -1).transpose(1, 0, 2)
    a["sgw"] = x["sgu_w_2"][0].transpose(2, 0, 1)

    a["w_pool"] = x["pool_w"][0].reshape(4, 2, P, 256).transpose(2, 0, 1, 3).reshape(1, P, 2048)
    for l in range(2):
        gu = x["w_gate_up"][l].reshape(KD, P, 2, NF // 2, 2, P)
        a[f"w_gu{l}"] = gu.transpose(3, 1, 4, 0, 2, 5).reshape(NF // 2, P, 4096)
        dn = x["w_down"][l].reshape(NF, P, KD, P)
        a[f"w_dn{l}"] = dn.transpose(2, 1, 0, 3).reshape(KD, P, FF)
    wk = x["w_k"]
    kv = _np.concatenate([wk[:, 0:HD], wk[:, 0:HD], wk[:, HD:], wk[:, HD:], x["w_v"]], axis=1)
    a["w_kv"] = kv.reshape(KD, P, 384).transpose(1, 0, 2).reshape(1, P, 3072)
    a["w_q"] = _pieces(x["w_q"][0], 256)
    a["w_o"] = _pieces(x["w_o"][0], 256)
    a["w_ple"] = _pieces(x["ple_gate_w_2"][0], 256)
    w = x["w_in_2"][0]
    at, part = 0, {}
    for name, n in (("qa", SB_W), ("ka", SB_W), ("va", SB_W), ("qb", 384), ("kb", 384), ("vb", 384), ("ob", 384),
                    ("i", ML_H), ("f", ML_H), ("uc", SG_W), ("vc", SG_W)):
        part[name] = w[:, at:at + n]
        at += n

    def pad(*cols):
        c = _np.concatenate(cols, axis=1)
        return _np.concatenate([c, _np.zeros((D, 256 - c.shape[1]), f32)], axis=1)

    ob = part["ob"]
    z = [pad(part[n][:, s:s + 192]) for n in ("qb", "kb") for s in (0, 192)] + [
        pad(ob[:, 0:192]), pad(part["i"], ob[:, 192:288], part["f"], ob[:, 288:384]),
        part["qa"][:, 0:256], pad(part["qa"][:, 256:], part["ka"][:, 0:128]), part["ka"][:, 128:],
        part["va"][:, 0:256], pad(part["va"][:, 256:], part["vb"][:, 0:128]), part["vb"][:, 128:],
        part["uc"], part["vc"]]
    a["w_z"] = _pieces(_np.concatenate(z, axis=1), 256)
    wo = x["w_out_2"][0]
    chunks = [wo[c * P:(c + 1) * P] for c in range(SB_C)]
    chunks += [_np.concatenate([wo[SB_W + h * ML_D:SB_W + (h + 1) * ML_D], _np.zeros((P - ML_D, D), f32)]) for h in range(ML_H)]
    chunks += [wo[768 + c * P:768 + (c + 1) * P] for c in range(2)]
    a["w_out"] = _np.stack(chunks).reshape(9, P, 4, 2, P).transpose(2, 1, 3, 0, 4).reshape(4, P, 2304)
    pj = x["ple_proj_w_2"][0].reshape(2, P, D).transpose(1, 0, 2).reshape(P, 2048)
    pT = x["p_2"][0, 0].T.reshape(2, P, SEQ).transpose(1, 0, 2).reshape(P, 512)
    a["w_proj"] = _np.concatenate([pj, pT], axis=1)[None]
    gu = _np.concatenate([x["w_gate_2"][0], x["w_up_2"][0]], axis=2)
    gu = gu.reshape(NE, KD, P, 512).transpose(0, 2, 1, 3).reshape(NE, P, 4096)
    dn = x["w_down_2"][0].reshape(NE, 2, P, D).transpose(0, 2, 1, 3).reshape(NE, P, 2048)
    a["w_eg"], a["w_ed"] = gu, dn

    nc = _bacc.Bacc("TRN2", target_bir_lowering=False, num_devices=1)
    arrays, args = {}, {}
    for name, v in a.items():
        v = _np.ascontiguousarray(v)
        arrays[f"in_{name}"] = v
        args[name] = nc.dram_tensor(f"in_{name}", v.shape, _mybir.dt.from_np(v.dtype), kind="ExternalInput").ap()
    out = nc.dram_tensor("out_y", (P, KD, SEQ), _mybir.dt.float32, kind="ExternalOutput").ap()
    bass_two_blocks(nc, args, out)
    got = _run(nc, [arrays], core_ids=[0]).results[0]["out_y"]
    return got.transpose(2, 1, 0).reshape(1, SEQ, D)
```

```python
import numpy as np
import concourse.bass as bass
from concourse import mybir
from contextlib import ExitStack

F32 = mybir.dt.float32
F32R = mybir.dt.float32r
I32 = mybir.dt.int32
ACT = mybir.ActivationFunctionType
ALU = mybir.AluOpType
AX = mybir.AxisListType

P = 128
D = 1024
KD = D // P
N_META = 16
SEQ = 256
T = N_META + SEQ
NB = SEQ // P
FF = 2816
NF = FF // P
WINDOWS = (2, 4, 8, 16)
PADT = max(WINDOWS)
NH = 16
HD = 64
HEADS_PER_GROUP = 4
EPS = 1e-6
NEG = -1e30
SB_H = 6
SB_W = SB_H * HD
SB_C = SB_W // P
ML_H = 4
ML_D = 96
SG = 4
SG_D = 64
SG_W = SG * SG_D
NE = 32
NGRP = 4
EPG = NE // NGRP
ROWS = 2 * SEQ
HALF = P
FEW = 32
XS = ROWS + FEW
XS_ALL = (KD - 1) * XS + ROWS + SEQ
WIDE = SEQ
EPIECE = 1024
EPIECES = 6
EBUFS = 3
FE = 256

SLOTS = 3
SLOT = 6144
PIECE = 2048
STREAM = [("w_pool", 1, 2048), ("w_gu0", NF // 2, 4096), ("w_dn0", KD, FF), ("w_kv", 1, 3072),
          ("w_q", 2, 4096), ("w_o", 2, 4096), ("w_gu1", NF // 2, 4096), ("w_dn1", KD, FF),
          ("w_z", 7, 4096), ("w_out", 4, 2304), ("w_proj", 1, 2560), ("w_exp", NE, SLOT),
          ("w_ple", 2, 4096)]
UNSPLIT = ("w_pool", "w_kv", "w_proj", "w_exp")
FIRST, FIRST_PIECE = {}, {}


def tile_of(name, i):
    return FIRST[name] + i


_t = _p = 0
for _name, _n, _ in STREAM:
    FIRST[_name], FIRST_PIECE[_name] = _t, _p
    _t += _n
    _p += 0 if _name in UNSPLIT else 2 * _n

NORMS = [("mixpre0", 8), ("mixpost0", 8), ("ffnpre0", 8), ("ffnpost0", 8), ("pre1", 8),
         ("mixpost1", 8), ("ffnpre1", 8), ("ffnpost1", 8), ("norm1", 8), ("sb_out", SB_C),
         ("norm2", 8), ("ple", 8), ("final", 8)]
NORM, SQ0 = {}, {}
_s = 0
for _i, (_name, _n) in enumerate(NORMS):
    NORM[_name], SQ0[_name] = _i, _s
    _s += _n

PAIRED = ["mixpost0", "ffnpre0", "ffnpost0", "mixpost1", "ffnpre1", "ffnpost1", "ple"]
PAIRS = KD // 2 - 1

VECS = [("mixpre0", 8), ("mixpost0", 8), ("ffnpre0", 8), ("ffnpost0", 8), ("mixpre1", 8),
        ("mixpost1", 8), ("ffnpre1", 8), ("ffnpost1", 8), ("kv_norm", 8), ("pool_scale", 8),
        ("norm1", 8), ("norm2", 8), ("ple", 8), ("final", 8), ("b_q", 8), ("b_o", 8), ("b_k", 2),
        ("sb_out", SB_C), ("conv_w", 32), ("conv_b", 8), ("mnorm", ML_H), ("igate_b", 1),
        ("fgate_b", 1), ("sgu_b", SG)]
VCOL, NV = {}, 0
for _name, _n in VECS:
    VCOL[_name] = NV
    NV += _n
ROWV = [("sinks", NH), ("b_v", 128), ("ln_g", SG_W), ("ln_b", SG_W), ("sgu_out", SG_W),
        ("router_b", NGRP + NE), ("desc", NGRP)]
RCOL, NR = {}, 0
for _name, _n in ROWV:
    RCOL[_name] = NR
    NR += _n
CONST = [("ident", P), ("strict", P), ("negtri", P), ("sgumask", P),
         ("invcnt", len(WINDOWS) * PADT), ("buckets", P)]
CCOL, NC = {}, 0
for _name, _n in CONST:
    CCOL[_name] = NC
    NC += _n

Z_OUT = [[("uc", 0), ("uc", 1)], [("vc", 0), ("vc", 1)], [("qa", 0), ("qa", 1)], [("qa", 2), ("ka", 0)],
         [("ka", 1), ("ka", 2)], [("va", 0), ("va", 1)], [("vab", 0), ("vab", 1)],
         [("gate", 0), ("ob", 2), ("gate", 1), ("ob", 3)],
         [("conv", 0), ("conv", 1)], [("conv", 2), ("conv", 3)], [("conv", 4), ("conv", 5)],
         [("conv", 6), ("conv", 7)], [("vb", 0), ("vb", 1)], [("ob", 0), ("ob", 1)]]
Z_BANKS = 3
SB_FIRST = 6
Z_TOKENS = ("va", "vab", "vb", "uc", "vc")
Z_COUNT = sum(len(x) for x in Z_OUT)
GATE_AT = [(0, ML_H + ML_D), (ML_H, ML_D), (ML_H + ML_D, ML_H + ML_D), (2 * ML_H + ML_D, ML_D)]


def bass_two_blocks(nc, a, out):
    y_rows = nc.dram_tensor("y_rows", (ROWS + WIDE, D), F32, kind="Internal").ap()
    bias_rows = nc.dram_tensor("bias_rows", (NH, 3 * P), F32, kind="Internal").ap()

    ctx = ExitStack()
    with ctx:
        def sb(name, shape, dt=F32, within=None):
            return (within or ctx).enter_context(nc.sbuf_tensor(name, shape, dt))

        sems = {}

        def sem(name):
            if name not in sems:
                sems[name] = ctx.enter_context(nc.semaphore(name))
            return sems[name]

        ring = sb("ring", [P, SLOTS, SLOT])
        hs = sb("hs", [P, KD, T])
        mix = sb("mix", [P, KD, T])
        rstd = sb("rstd", [P, 2, T])
        sq = sb("sq", [P, 4, T])
        vec = sb("vec", [P, NV])
        row = sb("row", [P, NR])
        cst = sb("cst", [P, NC])
        rw = sb("rw", [P, KD, NGRP + NE])
        sgw = sb("sgw", [P, SG, P])
        relb = sb("relb", [32, NH])
        ones = sb("ones", [P, P])
        nones = sb("nones", [P, P])
        iota = sb("iota", [P, ROWS])
        small = sb("small", [P, 420])
        route_i = sb("route_i", [P, 2, NE], I32)

        with ExitStack() as turn:
            wh = sb("wh", [P, 2, PIECE], F32R, turn)
            wl = sb("wl", [P, 2, PIECE], F32R, turn)
        with ExitStack() as turn:
            ewh = sb("ewh", [P, EBUFS, EPIECE], F32R, turn)
            ewl = sb("ewl", [P, EBUFS, EPIECE], F32R, turn)
            sgate = sb("sgate", [P, 2, FE], F32, turn)
            he = sb("he", [P, 2, FE], F32, turn)
            heTh = sb("heTh", [P, 2, FE // P, P], F32R, turn)
            heTl = sb("heTl", [P, 2, FE // P, P], F32R, turn)
        with ExitStack() as turn:
            rscr = sb("rscr", [P, 2 * PIECE], F32, turn)
            psel = sb("psel", [P, NB, ROWS], F32R, turn)
            combt = sb("combt", [P, NB, ROWS], F32, turn)
        ctx.enter_context(nc.sbuf_tensor("split_room", [P, 4 * PIECE], F32))
        with ExitStack() as turn:
            xh = sb("xh", [P, 9, SEQ], F32R, turn)
            xl = sb("xl", [P, 9, SEQ], F32R, turn)
        with ExitStack() as turn:
            xhT = sb("xhT", [P, KD, T], F32R, turn)
            sb("xgap", [P, 9 * SEQ - KD * T], F32, turn)
            xlT = sb("xlT", [P, KD, T], F32R, turn)
        with ExitStack() as turn:
            xtra = sb("xtra", [P, 2, 9 * SEQ], F32, turn)
        with ExitStack() as turn:
            h2h = sb("h2h", [P, NB, D], F32R, turn)
            h2l = sb("h2l", [P, NB, D], F32R, turn)
        ctx.enter_context(nc.sbuf_tensor("x_room", [P, 18 * SEQ], F32))
        with ExitStack() as turn:
            acth = sb("acth", [P, NF, T], F32R, turn)
            actl = sb("actl", [P, NF, T], F32R, turn)
        with ExitStack() as turn:
            xs = sb("xs", [P, XS_ALL], F32, turn)
            xeh = sb("xeh", [P, KD, WIDE], F32R, turn)
            xel = sb("xel", [P, KD, WIDE], F32R, turn)
        with ExitStack() as turn:
            sb("xs_and_xeh", [P, XS_ALL + KD * WIDE], F32, turn)
            xew = sb("xew", [P, KD, WIDE], F32, turn)
            combr = sb("combr", [P, 4, SEQ], F32, turn)
            ppT = sb("ppT", [P, KD, SEQ], F32, turn)
        work = sb("work", [P, 2 * NF * T])

        ps = ctx.enter_context(nc.psum_tensor("ps", [P, 8, 512], F32))

        def carve():
            at = [0]

            def take(*shape):
                n = 1
                for s in shape:
                    n *= s
                v = work[:, at[0]:at[0] + n]
                at[0] += n
                assert at[0] <= 2 * NF * T
                if len(shape) == 2:
                    v = v.rearrange("p (a b) -> p a b", b=shape[1])
                if len(shape) == 3:
                    v = v.rearrange("p (a b c) -> p a b c", b=shape[1], c=shape[2])
                return v
            return take

        take = carve()
        hp = take(KD, PADT + T)
        win = take(2 * len(WINDOWS), 2, PADT + T)
        pooled = take(KD, T)
        brow = take(3 * P)
        take = carve()
        lg = [take(2 * HEADS_PER_GROUP, SEQ) for _ in range(2)]
        h1 = lg[0]
        qT = take(KD, SEQ)
        kT = take(2, T)
        vtok = take(NB + 1, P)
        brev = take(NH, SEQ)
        pT = [mix[:, 2 * i:2 * i + 2, :].rearrange("p a b -> p (a b)")[:, 0:4 * P] for i in range(2)]
        take = carve()
        qaT = take(SB_C, SEQ)
        kaT = take(SB_C, SEQ)
        va = take(NB, SB_W)
        vb = take(NB, ML_H * ML_D)
        ob = take(ML_H, SEQ)
        uc = take(NB, SG_W)
        vc = take(NB, SG_W)
        cv = take(2 * ML_H, SEQ)
        e1 = take(2, 3 * P)
        sp = take(2, 3 * P)
        aw = take(2, 3 * P)
        yaT = take(SB_C, SEQ)
        yb = take(ML_H, SEQ)
        ycT = take(NB, SEQ)
        zpre = [ring[:, s, 4096:4096 + 4 * (SEQ + 3)].rearrange("p (a b) -> p a b", b=SEQ + 3)
                for s in range(2)]
        gt = ring[:, 2, 4096:4096 + 7 * SEQ].rearrange("p (a b) -> p a b", b=SEQ)
        ysr = ring[:, tile_of("w_exp", NE - 1) % SLOTS, 0:4 * D].rearrange("p (a b) -> p a b", b=D)
        ye = [v[:, 0:2 * D].rearrange("p (a b) -> p a b", b=D)
              for v in (mix[:, :, :].rearrange("p a b -> p (a b)"), xtra[:, 0, :], xtra[:, 1, :])]

        def V(name, i=0, rows=P):
            return vec[0:rows, VCOL[name] + i:VCOL[name] + i + 1]

        def R(name, n, at=0):
            return row[:, RCOL[name] + at:RCOL[name] + at + n]

        def C(name, n=P, rows=P, at=0):
            return cst[0:rows, CCOL[name] + at:CCOL[name] + at + n]

        ident = C("ident")

        def tile_at(t):
            return t % SLOTS, t // SLOTS

        def ring_steps(eng, name, body, first=0, last=None):
            n = dict((x, y) for x, y, _ in STREAM)[name] if last is None else last
            turns = (n - first) // SLOTS
            if turns >= 2:
                with eng.Fori(0, turns) as k:
                    for j in range(SLOTS):
                        slot, rnd = tile_at(FIRST[name] + first + j)
                        body(slot, k + rnd, k * SLOTS + (first + j))
            else:
                turns = 0
            for i in range(first + turns * SLOTS, n):
                slot, rnd = tile_at(FIRST[name] + i)
                body(slot, rnd, i)

        def owner(t):
            return next((name, t - FIRST[name]) for name, n, _ in STREAM if t - FIRST[name] < n)

        def tile_done(name, i):
            by_product = {"w_pool": ("mix_psum", KD), "w_kv": ("kv_psum", 3), "w_proj": ("pp_psum", KD),
                          "w_exp": ("elo_done", i * EPIECES + 2)}
            return by_product.get(name) or ("lo_done", i * 2 + (FIRST_PIECE[name] + 2))

        def piece_done(name, q):
            if name == "w_z":
                return "z_psum", sum(len(x) for x in Z_OUT[:q + 1])
            return {"w_gu0": ("gu_psum", q + 1), "w_dn0": ("dn_psum", q + 1), "w_q": ("q_psum", q * 2 + 2),
                    "w_o": ("wo_psum", q * 2 + 2), "w_gu1": ("gu_psum", q + (NF + 1)),
                    "w_dn1": ("dn_psum", q + (2 * KD + 1)), "w_out": ("wout_psum", q + 1),
                    "w_ple": ("ple_psum", q * 2 + 2)}[name]

        def gu_piece_of(e):
            return 0 if type(e) is int and e == 0 else e * EPIECES - 2

        def dn_piece_of(e):
            return NE * EPIECES - 2 if type(e) is int and e == NE - 1 else e * EPIECES + 8

        def expert_buffer(j, down, e):
            first = gu_piece_of(e if type(e) is int else 1) if not down else dn_piece_of(e if type(e) is int else 0)
            return (first + j) % EBUFS

        def expert_tile(slot, rnd, e):
            return rnd - tile_at(next(t for t in range(FIRST["w_exp"], FIRST["w_exp"] + SLOTS) if t % SLOTS == slot))[1]

        def value(eng, which, e):
            return eng.value_load(route_i[0:1, which, bass.ds(e, 1)], min_val=0, max_val=WIDE if which else ROWS)

        def for_halves(eng, count, body):
            with eng.If(count > HALF):
                body(2)
            with eng.Else():
                body(1)

        def hs_add(c):
            return sem("hs_odd" if c % 2 else "hs_even")

        def wait_hs(eng, k, c):
            eng.wait_ge(hs_add(c), k * (KD // 2) + c // 2 + 1)

        def z_done(kind, i):
            return [x for outs in Z_OUT for x in outs].index((kind, i)) + 1

        SPLIT = [(name, 2 * n) for name, n, _ in STREAM if name not in UNSPLIT]

        class Chain:

            def __init__(self, eng, name):
                self.eng, self.sem, self.n = eng, sem(name), 0

            def __call__(self, ins):
                self.n += 1
                ins.then_inc(self.sem, 1)
                self.eng.wait_ge(self.sem, self.n)

        block = ctx.enter_context(nc.Block())

        @block.sync
        def _(sp_):
            sp_.dma_start(hs[:, :, :], a["hT"]).then_inc(sem("hs_loaded"), 16)
            sp_.dma_start(vec[:, :], a["vec"]).then_inc(sem("consts_loaded"), 16)
            sp_.dma_start(cst[:, :], a["cst"]).then_inc(sem("consts_loaded"), 16)

            def load(name, size):
                def body(slot, rnd, i):
                    if type(i) is not int or i >= SLOTS:
                        done, count = tile_done(name, i - SLOTS)
                        sp_.wait_ge(sem(done), count)
                    elif FIRST[name] + i >= SLOTS:
                        done, count = tile_done(*owner(FIRST[name] + i - SLOTS))
                        sp_.wait_ge(sem(done), count)
                    src = a[name][bass.ds(i, 1), :, :] if type(i) is not int else a[name][i:i + 1, :, :]
                    sp_.dma_start(ring[:, slot, 0:size], src.rearrange("a p n -> p (a n)"))\
                       .then_inc(sem(f"tile_ready{slot}"), 16)
                return body

            def stream(name, before_third=None):
                size = dict((x, z) for x, _, z in STREAM)[name]
                body = load(name, size)
                n = dict((x, y) for x, y, _ in STREAM)[name]
                for i in range(min(SLOTS, n)):
                    if i == 2 and before_third:
                        before_third()
                    body(*tile_at(FIRST[name] + i), i)
                ring_steps(sp_, name, body, first=min(SLOTS, n))

            stream("w_pool")
            sp_.dma_start(row[:, :], a["row"]).then_inc(sem("tables_loaded"), 16)
            sp_.dma_start(relb[:, :], a["rel_bias"]).then_inc(sem("tables_loaded"), 16)
            sp_.dma_start(rw[:, :, :], a["rw"]).then_inc(sem("tables_loaded"), 16)
            sp_.dma_start(sgw[:, :, :], a["sgw"]).then_inc(sem("tables_loaded"), 16)

            def store_bias():
                sp_.wait_ge(sem("brow_ready"), 2)
                sp_.dma_start(bias_rows, brow[0:NH, :]).then_inc(sem("bias_out"), 16)

            stream("w_gu0", store_bias)
            stream("w_dn0")
            stream("w_kv")
            sp_.wait_ge(sem("bias_out"), 16)
            sp_.wait_ge(sem("dn_psum"), 2 * KD)
            skew = bass.AP(bias_rows.tensor, 0, [[1, P], [3 * P, NH], [1, SEQ]])
            sp_.dma_start(brev, skew).then_inc(sem("bias_ready"), 16)
            for name in ("w_q", "w_o", "w_gu1", "w_dn1", "w_z", "w_out", "w_proj"):
                if name == "w_proj":
                    sp_.wait_ge(sem("y_split"), 9)
                stream(name)

            def gate_up(slot, rnd, e):
                if type(e) is not int or e >= SLOTS:
                    sp_.wait_ge(sem("elo_done"), gu_piece_of(e - SLOTS) + 4)
                else:
                    done, count = tile_done(*owner(FIRST["w_exp"] + e - SLOTS))
                    sp_.wait_ge(sem(done), count)
                sp_.dma_start(ring[:, slot, 0:4096], a["w_eg"][bass.ds(e, 1), :, :].rearrange("a p n -> p (a n)"))\
                   .then_inc(sem(f"tile_ready{slot}"), 16)

            def down(slot, rnd, e):
                if type(e) is not int or e >= SLOTS:
                    sp_.wait_ge(sem("elo_done"), dn_piece_of(e - SLOTS) + 2)
                sp_.dma_start(ring[:, slot, 4096:SLOT], a["w_ed"][bass.ds(e, 1), :, :].rearrange("a p n -> p (a n)"))\
                   .then_inc(sem(f"down_ready{slot}"), 16)

            def both(slot, rnd, e):
                gate_up((slot + 1) % SLOTS, None, e + 1)
                down(slot, None, e)

            gate_up(*tile_at(FIRST["w_exp"]), 0)
            for e in range(SLOTS + 1):
                both(*tile_at(FIRST["w_exp"] + e), e)
            ring_steps(sp_, "w_exp", both, first=SLOTS + 1, last=NE - 1)
            down(*tile_at(FIRST["w_exp"] + NE - 1), NE - 1)
            stream("w_ple")
            sp_.wait_ge(sem("elo_done"), NE * EPIECES)
            sp_.wait_ge(sem("y_stored"), 16 * NE)
            for r in range(4):
                sp_.dma_start(ysr[:, r, :], y_rows[r * P:(r + 1) * P, :]).then_inc(sem(f"ysr_loaded{r}"), 16)
            for c in range(KD):
                sp_.wait_ge(sem("out_ready"), c + 1)
                sp_.dma_start(out[:, c, :], mix[:, c, 0:SEQ]).then_inc(sem("out_stored"), 16)
            sp_.wait_ge(sem("out_stored"), 16 * KD)

        def pool_groups(eng, chain, groups, done):
            for g in groups:
                eng.wait_ge(sem("h_ready"), 2 * g + 2)
                eng.wait_ge(sem("hp_padded"), 1)
                if g == groups[0]:
                    eng.wait_ge(sem("consts_loaded"), 32)
                cur, lo, w, k = hp[:, 2 * g:2 * g + 2, :], 0, 1, 0
                while w < WINDOWS[g]:
                    new = win[:, 2 * g + k % 2, :, :]
                    chain(eng.tensor_tensor(new[:, :, lo + w:], cur[:, :, lo + w:], cur[:, :, lo:PADT + T - w], ALU.add))
                    cur, lo, w, k = new, lo + w, 2 * w, k + 1
                h = hp[:, 2 * g:2 * g + 2, PADT:]
                p = pooled[:, 2 * g:2 * g + 2, :]
                inv = C("invcnt", PADT, at=g * PADT).unsqueeze(1).to_broadcast([P, 2, PADT])
                fix = win[:, 2 * g + k % 2, :, 0:PADT]
                chain(eng.tensor_scalar(p[:, :, PADT:], cur[:, :, 2 * PADT:], 1.0 / w, None, ALU.mult))
                chain(eng.tensor_tensor(p[:, :, PADT:], p[:, :, PADT:], h[:, :, PADT:], ALU.subtract))
                chain(eng.tensor_tensor(fix, cur[:, :, PADT:2 * PADT], inv, ALU.mult))
                eng.tensor_tensor(p[:, :, 0:PADT], fix, h[:, :, 0:PADT], ALU.subtract).then_inc(sem(done), 1)

        def residual_add(eng, k, cols, c):
            n = cols.stop - cols.start
            eng.wait_ge(sem("delta_ready"), k * KD + c + 1)
            eng.tensor_tensor(hs[:, c, cols], hs[:, c, cols], mix[:, c, 0:n], ALU.add).then_inc(hs_add(c), 1)

        def even_adds(pool, k, cols):
            for c in range(0, KD, 2):
                residual_add(pool, k, cols, c)

        def pair_squares(pool, name, n):
            for q in range(PAIRS):
                even, odd = ((SQ0[name] + 2 * q + i) % 4 for i in range(2))
                pool.wait_ge(sem("sq_ready"), SQ0[name] + 2 * q + 2)
                pool.tensor_tensor(sq[:, even, 0:n], sq[:, even, 0:n], sq[:, odd, 0:n], ALU.add).then_inc(sem("sq_paired"), 1)

        def ffn_pool(pool, l, n):
            with pool.Fori(0, NF // 2) as i:
                for j in range(2):
                    f = i * 2 + j
                    pool.wait_ge(sem("silu_ready"), f + (l * NF + 1))
                    pool.wait_ge(sem("up_ready"), f + (l * NF + 1))
                    pool.tensor_tensor(mix[:, 6 + j, 0:n], mix[:, 2 + j, 0:n], mix[:, 4 + j, 0:n], ALU.mult)\
                        .then_inc(sem("act_ready"), 1)
                    pool.wait_ge(sem("act_ready"), f + (l * NF + 1))
                    pool.tensor_copy(acth[:, bass.ds(f, 1), 0:n], mix[:, 6 + j:7 + j, 0:n])\
                        .then_inc(sem("acth_ready"), 1)
                    pool.wait_ge(sem("acth_ready"), f + (l * NF + 1))
                    pool.tensor_tensor(actl[:, bass.ds(f, 1), 0:n], mix[:, 6 + j:7 + j, 0:n],
                                       acth[:, bass.ds(f, 1), 0:n].bitcast(F32), ALU.subtract)\
                        .then_inc(sem("act_split"), 1)

        def conv(eng, chain, j, done):
            eng.wait_ge(sem("z_evac"), z_done("conv", j))
            eng.wait_ge(sem("zpre_padded"), 2)
            src, dst = zpre[j // ML_H][0:ML_D, j % ML_H, :], cv[0:ML_D, j, :]
            chain(eng.tensor_scalar(dst, src[:, 0:SEQ], V("conv_w", 4 * j, ML_D), V("conv_b", j, ML_D), ALU.mult, ALU.add))
            for k in range(1, 4):
                ins = eng.scalar_tensor_tensor(dst, src[:, k:k + SEQ], V("conv_w", 4 * j + k, ML_D), dst, ALU.mult, ALU.add)
                if k < 3:
                    chain(ins)
            ins.then_inc(sem(done), 1)

        @block.gpsimd
        def _(pool):
            chain = Chain(pool, "pool_chain")
            pool.memset(ones[:, :], 1.0).then_inc(sem("ones_ready"), 1)
            pool.memset(nones[:, :], -1.0).then_inc(sem("ones_ready"), 1)
            pool.memset(hp[:, :, 0:PADT], 0.0).then_inc(sem("hp_padded"), 1)
            pool.memset(brow[0:NH, :], NEG).then_inc(sem("brow_ready"), 1)
            chain(pool.iota(mix[:, 0:2, 0:SEQ].bitcast(I32), pattern=[[SEQ, 2], [1, SEQ]], base=0, channel_multiplier=0))
            pool.tensor_copy(iota[:, :].rearrange("p (a b) -> p a b", a=2), mix[:, 0:2, 0:SEQ].bitcast(I32))\
                .then_inc(sem("iota_ready"), 1)

            pool.wait_ge(sem("consts_loaded"), 32)
            pool.wait_ge(sem("tables_loaded"), 64)
            pool.tensor_tensor(sgw[:, :, :], sgw[:, :, :], C("sgumask").unsqueeze(1).to_broadcast([P, SG, P]), ALU.mult)\
                .then_inc(sem("sgw_masked"), 1)

            pool_groups(pool, chain, (0, 1), "p_pool")
            pair_squares(pool, "mixpost0", T)
            even_adds(pool, 0, slice(0, T))
            pair_squares(pool, "ffnpre0", T)
            pool.wait_ge(sem("bias_out"), 16)
            ffn_pool(pool, 0, T)
            pair_squares(pool, "ffnpost0", T)
            even_adds(pool, 1, slice(0, T))
            pair_squares(pool, "mixpost1", SEQ)
            even_adds(pool, 2, slice(N_META, T))
            pair_squares(pool, "ffnpre1", SEQ)
            ffn_pool(pool, 1, SEQ)
            pair_squares(pool, "ffnpost1", SEQ)
            even_adds(pool, 3, slice(N_META, T))

            for s in range(2):
                pool.memset(zpre[s][0:ML_D, :, 0:3], 0.0).then_inc(sem("zpre_padded"), 1)
            for i in range(SB_H):
                pool.wait_ge(sem("sb_exp"), i + 1)
                v = aw[:, i % 2, :].rearrange("p (a b) -> p a b", a=3)[:, 0:3:2, :]
                pool.affine_select(out=v, in_=v, compare_op=ALU.is_gt, fill=0.0, base=0,
                                   pattern=[[0, 2], [1, P]], channel_multiplier=-1).then_inc(sem("sb_a"), 1)
            for h in range(ML_H):
                pool.wait_ge(sem("ml_exp"), 2 * h + 2)
                v = aw[:, h % 2, :].rearrange("p (a b) -> p a b", a=3)[:, 0:3:2, :]
                pool.affine_select(out=v, in_=v, compare_op=ALU.is_ge, fill=0.0, base=0,
                                   pattern=[[0, 2], [1, P]], channel_multiplier=-1).then_inc(sem("ml_d"), 1)

            wait_hs(pool, 4, KD - 2)
            wait_hs(pool, 4, KD - 1)
            for k in range(KD):
                at = k * XS + ROWS
                n = FEW if k < KD - 1 else WIDE
                pool.tensor_copy(xs[:, at:at + n], iota[:, 0:n]).then_inc(sem("xs_padded"), 1)
            for x in (xeh, xel):
                for k in range(KD):
                    pool.tensor_copy(x[:, k, FEW:HALF], iota[:, FEW:HALF]).then_inc(sem("xs_padded"), 1)
            pool.wait_ge(sem("xs_padded"), 3 * KD)
            pool.wait_ge(sem("route_ready"), 2)
            for ready in ("xs_ready", "xs_ready_d"):
                pool.wait_ge(sem(ready), KD // 2)

            def window(slot, rnd, e):
                start, count = value(pool, 0, e), value(pool, 1, e)

                def rows(n):
                    for j in range(4):
                        if type(e) is not int or e:
                            pool.wait_ge(sem("e_used"), gu_piece_of(e - 1) + (j + 1))
                        pair = slice(2 * j, 2 * j + 2)
                        for k in range(2 * j, 2 * j + 2):
                            src = xs[:, bass.ds(start + k * XS, n)]
                            pool.tensor_copy(xew[:, k, 0:n], src).then_inc(sem("xew_ready"), 1)
                            pool.tensor_copy(xeh[:, k, 0:n], src).then_inc(sem("xew_ready"), 1)
                        pool.wait_ge(sem("xew_ready"), e * (2 * KD) + (4 * j + 4))
                        pool.tensor_tensor(xel[:, pair, 0:n], xew[:, pair, 0:n], xeh[:, pair, 0:n].bitcast(F32), ALU.subtract)\
                            .then_inc(sem("xe_ready"), 1)

                with pool.If(count > FEW):
                    with pool.If(count > HALF):
                        rows(WIDE)
                    with pool.Else():
                        rows(HALF)
                with pool.Else():
                    rows(FEW)

            def store(slot, rnd, e):
                start, count = value(pool, 0, e), value(pool, 1, e)

                def rows(n, halves):
                    pool.wait_ge(sem("y_ready"), e + 1)
                    if type(e) is not int or e:
                        pool.wait_ge(sem("y_stored"), e * 16)
                    dst = y_rows[bass.ds(start, n * halves), :].rearrange("(a p) n -> p a n", p=n)
                    pool.dma_start(dst, ye[slot][0:n, 0:halves, :]).then_inc(sem("y_stored"), 16)

                with pool.If(count > HALF):
                    rows(HALF, 2)
                with pool.Else():
                    with pool.If(count > FEW):
                        rows(HALF, 1)
                    with pool.Else():
                        rows(FEW, 1)

            def window_and_store(slot, rnd, e):
                window(slot, rnd, e)
                store(slot, None, e - SLOTS)

            for e in range(SLOTS):
                window(None, None, e)
            window_and_store(*tile_at(FIRST["w_exp"] + SLOTS), SLOTS)
            ring_steps(pool, "w_exp", window_and_store, first=SLOTS + 1)
            for e in range(NE - SLOTS, NE):
                store(tile_at(FIRST["w_exp"] + e)[0], None, e)
            pair_squares(pool, "ple", SEQ)

        def r_of(name):
            return rstd[:, NORM[name] % 2, :]

        def square(act, name, c, src, n, rows=P, **kw):
            k = SQ0[name] + c
            if k >= 4:
                act.wait_ge(sem("sq_used"), k - 3)
            act.activation(sq[0:rows, k % 4, 0:n], src, ACT.Square, **kw).then_inc(sem("sq_ready"), 1)

        def rsqrt(act, chain, name, width, n):
            r = r_of(name)[:, 0:n]
            act.wait_ge(sem("sq_used"), SQ0[name] + dict(NORMS)[name])
            chain(act.activation(r, ps[:, 6, 0:n], ACT.Ln, scale=1.0 / width, bias=EPS))
            act.activation(r, r, ACT.Exp, scale=-0.5).then_inc(sem("r_ready"), 1)

        def split_hi(act, name, slot, rnd, i, j, size):
            if j == 0:
                act.wait_ge(sem(f"tile_ready{slot}"), rnd * 16 + 16)
            if type(i) is not int or i > 0:
                done, count = piece_done(name, i * 2 + (j - 2))
                act.wait_ge(sem(done), count)
            elif FIRST_PIECE[name]:
                before, n = SPLIT[[x for x, _ in SPLIT].index(name) - 1]
                done, count = piece_done(before, n + j - 2)
                act.wait_ge(sem(done), count)
            act.activation(wh[:, j, 0:size], ring[:, slot, j * size:(j + 1) * size], ACT.Copy)\
               .then_inc(sem("hi_done"), 1)

        def split_lo(dve, name, slot, rnd, i, j, size):
            piece = i * 2 + (FIRST_PIECE[name] + j)
            dve.wait_ge(sem("hi_done"), piece + 1)
            dve.tensor_tensor(wl[:, j, 0:size], ring[:, slot, j * size:(j + 1) * size],
                              wh[:, j, 0:size].bitcast(F32), ALU.subtract).then_inc(sem("lo_done"), 1)

        def halves(name, i, size):
            slot, rnd = tile_at(FIRST[name] + i)
            return [(slot, rnd, i, j, size) for j in range(2)]

        def wo_out(act, c):
            act.wait_ge(sem("wo_psum"), c + 1)
            act.activation(mix[:, c, 0:SEQ], ps[:, c % 4, 0:SEQ], ACT.Identity, bias=V("b_o", c))\
               .then_inc(sem("mix_ready"), 1)
            square(act, "mixpost1", c, ps[:, c % 4, 0:SEQ], SEQ, bias=V("b_o", c))

        def conv_sigmoid(i):
            at = 4 + i % 2 * 2
            return mix[0:ML_D, at:at + 2, 0:SEQ]

        def sb_out_bank(c):
            return ps[:, 5 + c % 2 * 2, 0:SEQ]

        def y_chunks():
            return [(yaT[:, c, :], P) for c in range(SB_C)] + [(ycT[:, c, :], P) for c in range(NB)] \
                + [(yb[0:ML_D, h, :], ML_D) for h in range(ML_H)]

        def z_parts(parts, n):
            bank = ps[:, n % Z_BANKS, :]
            kind, i = parts
            if kind == "conv":
                return [(zpre[i // ML_H][0:ML_D, i % ML_H, 3:], bank[0:ML_D, 0:SEQ], ACT.Copy, {})]
            if kind == "ob":
                return [(ob[0:ML_D, i, :], bank[0:ML_D, 0:SEQ], ACT.Copy, {})]
            if kind == "gate":
                return [(gt[0:ML_H, i, :], bank[0:ML_H, 0:SEQ], ACT.Identity,
                         {"bias": V("fgate_b" if i else "igate_b", 0, ML_H)})]
            if kind == "qa":
                return [(qaT[:, i, :], bank[:, 0:SEQ], ACT.Copy, {"scale": HD ** -0.5})]
            if kind == "ka":
                return [(kaT[:, i, :], bank[:, 0:SEQ], ACT.Copy, {})]
            if kind == "va":
                return [(va[:, i, 0:256], bank[:, 0:256], ACT.Copy, {})]
            if kind == "vab":
                return [(va[:, i, 256:384], bank[:, 0:128], ACT.Copy, {}), (vb[:, i, 0:128], bank[:, 128:256], ACT.Copy, {})]
            if kind == "vb":
                return [(vb[:, i, 128:384], bank[:, 0:256], ACT.Copy, {})]
            if kind == "uc":
                return [(uc[:, i, :], bank[:, 0:SG_W], ACT.Gelu_apprx_tanh, {})]
            return [(vc[:, i, :], bank[:, 0:SG_W], ACT.Gelu_apprx_tanh, {})]

        def ffn_act(act, chain, l, n, cols, unsplit=()):
            gu, dn, pre, post = f"w_gu{l}", f"w_dn{l}", f"ffnpre{l}", f"ffnpost{l}"
            x = xhT if l == 0 else xh
            for c in range(KD):
                wait_hs(act, 2 * l, c)
                act.activation(x[:, c, 0:n], hs[:, c, cols], ACT.Copy, scale=V(pre, c)).then_inc(sem("xh_ready"), 1)
                if c < 4:
                    square(act, pre, c, hs[:, c, cols], n)
            for args in unsplit:
                split_hi(act, gu, *args)
            for c in range(4, KD):
                square(act, pre, c, hs[:, c, cols], n)
            rsqrt(act, chain, pre, D, n)
            act.preload_act_table_set("silu_and_others")

            def silu(f, j):
                act.wait_ge(sem("gr_ready"), f + (l * NF + 1))
                act.activation(mix[:, 2 + j, 0:n], mix[:, j, 0:n], ACT.Silu).then_inc(sem("silu_ready"), 1)

            def body(slot, rnd, i):
                for j in range(2):
                    split_hi(act, gu, slot, rnd, i, j, PIECE)
                    silu(i * 2 + (j - 2), j)

            ring_steps(act, gu, body, first=1)
            for j in range(2):
                split_hi(act, dn, *halves(dn, 0, FF // 2)[j])
                silu(NF - 2 + j, j)
            act.preload_act_table_set("natural_log_exp_and_others")

            def leave(c):
                act.wait_ge(sem("dn_psum"), 2 * (l * KD + c) + 2)
                act.activation(mix[:, c, 0:n], ps[:, 4 + c % 2, 0:n], ACT.Copy).then_inc(sem("mix_ready"), 1)
                square(act, post, c, ps[:, 4 + c % 2, 0:n], n)

            for i in range(KD):
                for args in halves(dn, i, FF // 2) if i else ():
                    split_hi(act, dn, *args)
                if i:
                    leave(i - 1)
            leave(KD - 1)
            rsqrt(act, chain, post, D, n)

        @block.scalar
        def _(act):
            chain = Chain(act, "act_chain")
            act.preload_act_table_set("natural_log_exp_and_others")
            act.wait_ge(sem("hs_loaded"), 16)
            for c in range(KD):
                square(act, "mixpre0", c, hs[:, c, :], T)
            rsqrt(act, chain, "mixpre0", D, T)
            for x in halves("w_gu0", 0, PIECE):
                split_hi(act, "w_gu0", *x)
            act.wait_ge(sem("brow_psum"), 1)
            act.wait_ge(sem("brow_ready"), 1)
            act.activation(brow[0:NH, P:2 * P], ps[0:NH, 7, 0:P], ACT.Copy).then_inc(sem("brow_ready"), 1)
            act.wait_ge(sem("iota_ready"), 1)
            for c in range(KD):
                act.wait_ge(sem("mix_psum"), c + 1)
                act.activation(mix[:, c, :], ps[:, c % 4, 0:T], ACT.Copy, scale=V("pool_scale", c))\
                   .then_inc(sem("mix_ready"), 1)
                square(act, "mixpost0", c, ps[:, c % 4, 0:T], T, scale=V("pool_scale", c))
            rsqrt(act, chain, "mixpost0", D, T)
            ffn_act(act, chain, 0, T, slice(0, T))

            for c in range(KD):
                wait_hs(act, 1, c)
                square(act, "pre1", c, hs[:, c, :], T)
            rsqrt(act, chain, "pre1", D, T)
            for x in halves("w_q", 0, PIECE):
                split_hi(act, "w_q", *x)
            for c in range(KD):
                act.wait_ge(sem("h1_ready"), c + 1)
                act.activation(xh[:, c, :], h1[:, c, :], ACT.Copy).then_inc(sem("xh_ready"), 1)
            for j in range(2):
                act.wait_ge(sem("kv_psum"), j + 1)
                act.activation(kT[:, j, :], ps[:, j, 0:T], ACT.Identity, bias=V("b_k", j))\
                   .then_inc(sem("kT_ready"), 1)
            for x in halves("w_q", 1, PIECE) + halves("w_o", 0, PIECE):
                split_hi(act, "w_q" if x[2] else "w_o", *x)
            for g in range(NH // HEADS_PER_GROUP):
                act.wait_ge(sem("negm_ready"), g + 1)
                for i in range(2 * HEADS_PER_GROUP):
                    n = N_META + P if i % 2 == 0 else 2 * P
                    k = 2 * HEADS_PER_GROUP * g + i
                    v = lg[g % 2][:, i, 0:n]
                    act.activation(v, v, ACT.Exp, bias=small[:, 32 + k:33 + k], accum_out=small[:, 96 + k:97 + k])\
                       .then_inc(sem("exp_ready"), 1)
                k = 2 * HEADS_PER_GROUP * g
                act.activation(small[:, 64 + k:72 + k], small[:, 64 + k:72 + k], ACT.Exp).then_inc(sem("exp_ready"), 1)
                for h in range(HEADS_PER_GROUP * g, HEADS_PER_GROUP * (g + 1)):
                    act.wait_ge(sem("pt_psum"), h + 1)
                    if h >= 2:
                        act.wait_ge(sem("o_done"), h - 1)
                    act.activation(pT[h % 2][:, 0:3 * P], ps[:, 4 + h % 2, 0:3 * P], ACT.Copy).then_inc(sem("pt_ready"), 1)
                    act.activation(pT[h % 2][0:N_META, 3 * P:4 * P], ps[0:N_META, 4 + h % 2, 3 * P:4 * P], ACT.Copy)\
                       .then_inc(sem("pt_ready"), 1)
                    if h % 2 == 1:
                        c = h // 2
                        act.wait_ge(sem("o_done"), h + 1)
                        o = ps[:, 6 + c % 2, 0:SEQ].rearrange("p (b q) -> p b q", q=P)
                        act.activation(xh[:, c, :].rearrange("p (b q) -> p b q", q=P), o[:, :, ::-1], ACT.Copy)\
                           .then_inc(sem("oh_ready"), 1)
            for k in range(NB):
                split_hi(act, "w_o", *halves("w_o", 1, PIECE)[k])
                for c in range(2 * k, 2 * k + 2):
                    wo_out(act, c)
            for c in range(4, KD):
                wo_out(act, c)
                if c == 5:
                    split_hi(act, "w_gu1", *halves("w_gu1", 0, PIECE)[0])
            rsqrt(act, chain, "mixpost1", D, SEQ)
            ffn_act(act, chain, 1, SEQ, slice(N_META, T), halves("w_gu1", 0, PIECE)[1:])

            for x in halves("w_z", 0, PIECE):
                split_hi(act, "w_z", *x)
            for c in range(KD):
                wait_hs(act, 3, c)
                square(act, "norm1", c, hs[:, c, N_META:], SEQ)
            rsqrt(act, chain, "norm1", D, SEQ)
            for c in range(KD):
                act.wait_ge(sem("xn_ready"), c + 1)
                act.activation(xh[:, c, :], mix[:, c, 0:SEQ], ACT.Copy).then_inc(sem("xh_ready"), 1)
            products = iter(enumerate(x for outs in Z_OUT for x in outs))

            def leave(results):
                for parts in results:
                    n, _ = next(products)
                    act.wait_ge(sem("z_psum"), n + 1)
                    for dst, src, func, kw in z_parts(parts, n):
                        ins = act.activation(dst, src, func, **kw)
                    ins.then_inc(sem("z_evac"), 1)

            def sgu_spread():
                act.wait_ge(sem("sgu_centred"), 1)
                act.activation(mix[:, 0:2, 0:SG_W], vc, ACT.Square).then_inc(sem("sgu_sq"), 1)
                act.wait_ge(sem("sgu_var"), 1)
                chain(act.activation(small[:, 8:16], small[:, 8:16], ACT.Ln, scale=1.0 / SG_D, bias=EPS))
                act.activation(small[:, 8:16], small[:, 8:16], ACT.Exp, scale=-0.5).then_inc(sem("sgu_r"), 1)

            def sgu_norm():
                act.wait_ge(sem("sgu_y"), SG)
                for b in range(NB):
                    act.activation(mix[:, 2 + b, 0:SG_W], uc[:, b, :], ACT.Square, accum_out=small[:, 16 + b:17 + b])\
                       .then_inc(sem("sgu_ysq"), 1)
                act.wait_ge(sem("sgu_ysq"), NB)
                chain(act.activation(small[:, 16:18], small[:, 16:18], ACT.Ln, scale=1.0 / SG_W, bias=EPS))
                act.activation(small[:, 16:18], small[:, 16:18], ACT.Exp, scale=-0.5).then_inc(sem("sgu_yr"), 1)

            def sb_step(i):
                if i < SB_H:
                    act.wait_ge(sem("sb_z"), i + 1)
                    if i >= 2:
                        act.wait_ge(sem("sb_sp"), i - 1)
                    e = e1[:, i % 2, :]
                    chain(act.activation(e, ps[:, 3 + i % 2, 0:3 * P], ACT.Abs))
                    chain(act.activation(e, e, ACT.Exp, scale=-1.0))
                    act.activation(e, e, ACT.Ln, bias=1.0).then_inc(sem("sb_ln"), 1)
                if 1 <= i <= SB_H:
                    act.wait_ge(sem("sb_E"), i)
                    if i >= 3:
                        act.wait_ge(sem("sb_o"), i - 2)
                    act.activation(aw[:, (i - 1) % 2, :], ps[:, 3 + (i - 1) % 2, 0:3 * P], ACT.Exp).then_inc(sem("sb_exp"), 1)
                if i >= 3 and i % 2 == 1:
                    c = (i - 2) // 2
                    act.wait_ge(sem("sb_o"), i - 1)
                    act.activation(yaT[:, c, :], sb_out_bank(c), ACT.Copy).then_inc(sem("ya_ready"), 1)
                    square(act, "sb_out", c, sb_out_bank(c), SEQ)

            def sigmoid(v):
                chain(act.activation(v, v, ACT.Exp, scale=-1.0))
                chain(act.activation(v, v, ACT.Ln, bias=1.0))
                return act.activation(v, v, ACT.Exp, scale=-1.0)

            for piece in range(14):
                leave(Z_OUT[piece][:-2])
                if piece < 12:
                    split_hi(act, "w_z", *halves("w_z", piece // 2 + 1, PIECE)[piece % 2])
                leave(Z_OUT[piece][-2:])
                if piece == 1:
                    act.preload_act_table_set("natural_log_exp_and_others")
                if piece == 3:
                    sgu_spread()
                if piece == 6:
                    sgu_norm()
                if piece == 9:
                    act.wait_ge(sem("yc_psum"), 1)
                    act.activation(ycT.rearrange("p a b -> p (a b)"), ps[:, 7, :], ACT.Copy).then_inc(sem("yc_ready"), 1)
                if piece >= SB_FIRST:
                    sb_step(piece - SB_FIRST)
                if piece == 8:
                    chain(act.activation(gt[0:ML_H, 2, :], gt[0:ML_H, 1, :], ACT.Abs))
                    chain(act.activation(gt[0:ML_H, 2, :], gt[0:ML_H, 2, :], ACT.Exp, scale=-1.0))
                    act.activation(gt[0:ML_H, 2, :], gt[0:ML_H, 2, :], ACT.Ln, bias=1.0).then_inc(sem("gate_ln"), 1)
                if piece == 10:
                    act.wait_ge(sem("gate_m"), 1)
                    act.activation(gt[0:ML_H, 6, :], gt[0:ML_H, 6, :], ACT.Exp, scale=-1.0).then_inc(sem("em_ready"), 1)
                if piece >= 10:
                    i = piece - 10
                    act.wait_ge(sem("conv_bounded"), i + 1)
                    sigmoid(conv_sigmoid(i)).then_inc(sem("conv_sig"), 1)
            rsqrt(act, chain, "sb_out", SB_W, SEQ)
            act.wait_ge(sem("ob_bounded"), 1)
            sigmoid(ob[0:ML_D, :, :]).then_inc(sem("ob_ready"), 1)

            r4 = mix[0:ML_D, ML_H:2 * ML_H, 0:SEQ]

            def ml_square(h):
                act.wait_ge(sem("ml_h"), h + 1)
                act.activation(mix[0:ML_D, h, 0:SEQ], yb[0:ML_D, h, :], ACT.Square).then_inc(sem("ml_sq"), 1)

            def ml_rsqrt(h):
                act.wait_ge(sem("ml_ss"), h + 1)
                chain(act.activation(r4[:, h, :], ps[0:ML_D, 2, 0:SEQ], ACT.Ln, scale=1.0 / ML_D, bias=EPS))
                act.activation(r4[:, h, :], r4[:, h, :], ACT.Exp, scale=-0.5).then_inc(sem("ml_r"), 1)

            def ml_decay(h):
                act.wait_ge(sem("ml_max"), 2 * h + 2)
                if h >= 2:
                    act.wait_ge(sem("ml_num"), h - 1)
                for b, cols in ((0, slice(0, SEQ)), (1, slice(SEQ, 3 * P))):
                    act.activation(aw[:, h % 2, cols], sp[:, h % 2, cols], ACT.Exp, scale=-1.0,
                                   bias=small[:, 20 + ML_H * b + h:21 + ML_H * b + h]).then_inc(sem("ml_exp"), 1)

            def ml_floor(h):
                if h >= 2:
                    act.wait_ge(sem("ml_h"), h - 1)
                act.activation(e1[0:ML_D, h % 2, 0:SEQ], ps[0:ML_D, 4 + h % 2, SEQ:2 * SEQ], ACT.Copy).then_inc(sem("ml_em"), 1)

            def y_high(j):
                src, rows = y_chunks()[j]
                if SB_C <= j < SB_C + NB:
                    act.wait_ge(sem("yc_ready"), 1)
                else:
                    act.wait_ge(sem("y_fin"), j + 1 if j < SB_C else j + 1 - NB)
                act.activation(xh[0:rows, j, :], src, ACT.Copy).then_inc(sem("yh_ready"), 1)

            ml_decay(0)
            ml_floor(0)
            ml_decay(1)
            ml_floor(1)
            for x in halves("w_out", 0, 9 * P):
                split_hi(act, "w_out", *x)
            ml_decay(2)
            for j in range(SB_C + NB):
                y_high(j)
            ml_square(0)
            ml_floor(2)
            ml_decay(3)
            ml_rsqrt(0)
            ml_square(1)
            ml_floor(3)
            ml_rsqrt(1)
            for h in (2, 3):
                ml_square(h)
                y_high(SB_C + NB + h - 2)
                ml_rsqrt(h)
            for h in (2, 3):
                y_high(SB_C + NB + h)
            for i in range(1, 4):
                for x in halves("w_out", i, 9 * P):
                    split_hi(act, "w_out", *x)

            for c in range(KD):
                wait_hs(act, 4, c)
                square(act, "norm2", c, hs[:, c, N_META:], SEQ)
            rsqrt(act, chain, "norm2", D, SEQ)
            for q in range(4):
                act.wait_ge(sem("h2_psum"), q + 1)
                act.activation(h2h[:, q // 2, q % 2 * 512:(q % 2 + 1) * 512], ps[:, 1 + q, :], ACT.Copy)\
                   .then_inc(sem("h2_ready"), 1)
            act.wait_ge(sem("route_g"), 1)
            act.activation(small[:, 128:136], small[:, 128:136], ACT.Exp).then_inc(sem("route_gexp"), 1)
            for c in range(KD):
                act.wait_ge(sem("pp_psum"), c + 1)
                act.activation(ppT[:, c, :], ps[:, 6 + c % 2, 0:SEQ], ACT.Copy).then_inc(sem("pp_ready"), 1)
            act.wait_ge(sem("route_d"), 1)
            act.activation(small[:, 180:182], small[:, 180:182], ACT.Exp).then_inc(sem("route_ex"), 1)
            for c in range(1, KD, 2):
                act.wait_ge(sem("xs_psum"), c + 1)
                act.activation(xs[:, c * XS:c * XS + ROWS], ps[:, c % 4, :], ACT.Copy).then_inc(sem("xs_ready"), 1)
            for q in range(2):
                act.wait_ge(sem("comb_psum"), q + 1)
                act.activation(combr[:, 2 * q:2 * q + 2, :].rearrange("p a b -> p (a b)"), ps[:, 6 + q, :], ACT.Copy)\
                   .then_inc(sem("comb_ready"), 1)
            act.preload_act_table_set("silu_and_others")

            def high(e, j, is_down, slot):
                g = (dn_piece_of(e) if is_down else gu_piece_of(e)) + j
                b = expert_buffer(j, is_down, e)
                if type(g) is not int or g >= EBUFS:
                    act.wait_ge(sem("e_used"), g - (EBUFS - 1))
                at = (4096 if is_down else 0) + j * EPIECE
                act.activation(ewh[:, b, :], ring[:, slot, at:at + EPIECE], ACT.Copy).then_inc(sem("ehi_done"), 1)

            def silu(e, count):
                def body(halves):
                    act.wait_ge(sem("e_used"), gu_piece_of(e) + 4)
                    act.activation(sgate[:, 0:halves, :], ps[:, 0:halves, 0:FE], ACT.Silu).then_inc(sem("sg_ready"), 1)
                for_halves(act, count, body)

            def transposed(e, count):
                def body(halves):
                    act.wait_ge(sem("het_psum"), e + 1)
                    act.activation(heTh[:, 0:halves, :, :].rearrange("p a c n -> p a (c n)"),
                                   ps[:, 6:6 + halves, 0:FE], ACT.Copy).then_inc(sem("heth_ready"), 1)
                for_halves(act, count, body)

            def leave(e, slot, count):
                def body(halves):
                    act.wait_ge(sem("e_used"), dn_piece_of(e) + 2)
                    if type(e) is not int or e >= SLOTS:
                        act.wait_ge(sem("y_stored"), e * 16 - 16 * (SLOTS - 1))
                    act.activation(ye[slot][:, 0:halves, :].rearrange("p a n -> p (a n)"),
                                   ps[:, 2:2 + 2 * halves, :].rearrange("p a n -> p (a n)"), ACT.Copy)\
                       .then_inc(sem("y_ready"), 1)
                for_halves(act, count, body)

            def step(slot, rnd, e):
                nxt = (slot + 1) % SLOTS
                act.wait_ge(sem(f"tile_ready{nxt}"), (rnd + (1 if nxt == 0 else 0)) * 16 + 16)
                high(e + 1, 0, False, nxt)
                count = value(act, 1, e)
                silu(e, count)
                high(e + 1, 1, False, nxt)
                high(e + 1, 2, False, nxt)
                transposed(e, count)
                if type(e) is not int or e:
                    leave(e - 1, (slot - 1) % SLOTS, value(act, 1, e - 1))
                high(e + 1, 3, False, nxt)
                act.wait_ge(sem(f"down_ready{slot}"), expert_tile(slot, rnd, e) * 16 + 16)
                for j in range(2):
                    high(e, j, True, slot)

            slot, rnd = tile_at(FIRST["w_exp"])
            act.wait_ge(sem(f"tile_ready{slot}"), rnd * 16 + 16)
            for j in range(4):
                high(0, j, False, slot)
            for e in range(SLOTS + 1):
                step(*tile_at(FIRST["w_exp"] + e), e)
            ring_steps(act, "w_exp", step, first=SLOTS + 1, last=NE - 1)
            last = NE - 1
            slot, rnd = tile_at(FIRST["w_exp"] + last)
            act.wait_ge(sem(f"down_ready{slot}"), expert_tile(slot, rnd, last) * 16 + 16)
            silu(last, value(act, 1, last))
            high(last, 0, True, slot)
            transposed(last, value(act, 1, last))
            leave(last - 1, (slot - 1) % SLOTS, value(act, 1, last - 1))
            high(last, 1, True, slot)
            leave(last, slot, value(act, 1, last))
            act.preload_act_table_set("natural_log_exp_and_others")

            for x in halves("w_ple", 0, PIECE):
                split_hi(act, "w_ple", *x)
            for c in range(KD):
                wait_hs(act, 5, c)
                act.activation(xh[:, c, :], hs[:, c, N_META:], ACT.Copy, scale=V("ple", c)).then_inc(sem("xh_ready"), 1)
                if c < 4:
                    square(act, "ple", c, hs[:, c, N_META:], SEQ)
            for c in range(4, KD):
                square(act, "ple", c, hs[:, c, N_META:], SEQ)
            rsqrt(act, chain, "ple", D, SEQ)
            act.preload_act_table_set("sigmoid_and_others")
            for c in range(KD):
                act.wait_ge(sem("ple_scaled"), c + 1)
                act.activation(mix[:, c, 0:SEQ], mix[:, c, 0:SEQ], ACT.Sigmoid).then_inc(sem("ple_sig"), 1)
                if c in (0, 2):
                    split_hi(act, "w_ple", *halves("w_ple", 1, PIECE)[c // 2])
            act.preload_act_table_set("natural_log_exp_and_others")
            for c in range(KD):
                wait_hs(act, 6, c)
                square(act, "final", c, hs[:, c, N_META:], SEQ)
            rsqrt(act, chain, "final", D, SEQ)

        def z_cols(outs, q):
            kind = outs[q][0]
            if outs[0][0] == "gate":
                return GATE_AT[q]
            if kind in ("conv", "ob"):
                return q * ML_D, ML_D
            return q * P, P

        def onehot(i):
            return small[:, 200 + i * NB * NE:200 + (i + 1) * NB * NE].rearrange("p (b e) -> p b e", b=NB)

        def ffn_pe(pe, mm3, sum_squares, l, n):
            gu, dn, pre, post = f"w_gu{l}", f"w_dn{l}", f"ffnpre{l}", f"ffnpost{l}"
            xa, xb = (xhT, xlT) if l == 0 else (xh, xl)
            base = FIRST_PIECE[gu]

            def piece(i, j, k0=None):
                f = i * 2 + j
                pe.wait_ge(sem("lo_done"), f + (base + 1))
                if not (type(i) is int and i == 0):
                    pe.wait_ge(sem("up_ready"), f + (l * NF - 1))
                for k in range(KD):
                    for g in range(2):
                        at = slice(k * 256 + g * P, k * 256 + g * P + P)
                        ins = mm3(ps[:, 2 * j + g, 0:n], (wh[:, j, at], wl[:, j, at]), (xa[:, k, 0:n], xb[:, k, 0:n]),
                                  k == 0, k == KD - 1)
                ins.then_inc(sem("gu_psum"), 1)

            pe.wait_ge(sem("lo_done"), base + 1)
            for ready, w, x in (("xh_ready", wh, xa), ("xh_ready", wl, xa), ("x_ready", wh, xb)):
                for k in range(KD):
                    pe.wait_ge(sem(ready), 2 * l * KD + k + 1)
                    for g in range(2):
                        ins = pe.matmul(ps[:, g, 0:n], w[:, 0, k * 256 + g * P:k * 256 + g * P + P], x[:, k, 0:n],
                                        start=(w is wh and x is xa and k == 0), stop=(x is xb and k == KD - 1))
            ins.then_inc(sem("gu_psum"), 1)
            for c in range(KD):
                sum_squares(pre, c, n)
            piece(0, 1)
            with pe.Fori(1, NF // 2) as i:
                for j in range(2):
                    piece(i, j)
            base = FIRST_PIECE[dn]
            for c in range(KD):
                if c >= 2:
                    pe.wait_ge(sem("sq_ready"), SQ0[post] + c - 1)
                for j in range(2):
                    pe.wait_ge(sem("lo_done"), base + 2 * c + j + 1)
                    if c == 0:
                        pe.wait_ge(sem("act_split"), l * NF + (j + 1) * (NF // 2))
                    for k in range(NF // 2):
                        at = slice(k * P, (k + 1) * P)
                        f = j * (NF // 2) + k
                        ins = mm3(ps[:, 4 + c % 2, 0:n], (wh[:, j, at], wl[:, j, at]),
                                  (acth[:, f, 0:n], actl[:, f, 0:n]), f == 0, f == NF - 1)
                    ins.then_inc(sem("dn_psum"), 1)
                if c:
                    sum_squares(post, c - 1, n)
            sum_squares(post, KD - 1, n)

        @block.tensor
        def _(pe):
            mm = pe.matmul

            def sum_squares(name, c, n, rows=P):
                k, last = SQ0[name] + c, dict(NORMS)[name] - 1
                chunks = 2 if name in PAIRED and c < 2 * PAIRS else 1
                if chunks == 2 and c % 2 == 0:
                    return
                if c < chunks and NORM[name]:
                    pe.wait_ge(sem("r_ready"), NORM[name])
                if chunks == 2:
                    pe.wait_ge(sem("sq_paired"), PAIRED.index(name) * PAIRS + c // 2 + 1)
                else:
                    pe.wait_ge(sem("sq_ready"), k + 1)
                mm(ps[:, 6, 0:n], ones[0:rows, :], sq[0:rows, (k + 1 - chunks) % 4, 0:n], start=(c < chunks), stop=(c == last))\
                    .then_inc(sem("sq_used"), chunks)

            def mm3(o, w, x, first, last, swap=False):
                (wh_, wl_), (xh_, xl_) = w, x
                for n, (p, q) in enumerate(((wh_, xh_), (wl_, xh_), (wh_, xl_))):
                    if swap:
                        p, q = q, p
                    ins = mm(o, p, q, start=first and n == 0, stop=last and n == 2)
                return ins

            pe.wait_ge(sem("ones_ready"), 2)
            for c in range(KD):
                sum_squares("mixpre0", c, T)
            pe.wait_ge(sem("consts_loaded"), 32)
            pe.wait_ge(sem("tables_loaded"), 64)
            mm(ps[0:NH, 7, 0:P], relb[:, :], C("buckets", rows=32), start=True, stop=True).then_inc(sem("brow_psum"), 1)
            slot, rnd = tile_at(FIRST["w_pool"])
            pe.wait_ge(sem(f"tile_ready{slot}"), 16 * (rnd + 1))
            pw = ring[:, slot, 0:2048].rearrange("p (g k n) -> p g k n", g=4, k=2)
            for c in range(KD):
                g = c // 2
                pe.wait_ge(sem("p_pool" if g < 2 else "p_dve"), g % 2 + 1)
                if c >= 4:
                    pe.wait_ge(sem("sq_ready"), SQ0["mixpost0"] + c - 3)
                for k in range(2):
                    ins = mm(ps[:, c % 4, 0:T], pw[:, g, k, c % 2 * P:c % 2 * P + P], pooled[:, 2 * g + k, :],
                             start=(k == 0), stop=(k == 1))
                ins.then_inc(sem("mix_psum"), 1)
                if c:
                    sum_squares("mixpost0", c - 1, T)
            sum_squares("mixpost0", KD - 1, T)
            ffn_pe(pe, mm3, sum_squares, 0, T)

            for c in range(KD):
                sum_squares("pre1", c, T)
            slot, rnd = tile_at(FIRST["w_kv"])
            pe.wait_ge(sem(f"tile_ready{slot}"), 16 * (rnd + 1))
            wkv = ring[:, slot, 0:3072].rearrange("p (k n) -> p k n", k=KD)
            for j in range(2):
                for k in range(KD):
                    pe.wait_ge(sem("kvin_ready"), k + 1)
                    ins = mm(ps[:, j, 0:T], wkv[:, k, j * P:(j + 1) * P], mix[:, k, :], start=(k == 0), stop=(k == KD - 1))
                ins.then_inc(sem("kv_psum"), 1)
            for j in range(NB + 1):
                cols = slice(0, N_META) if j == 0 else slice(N_META + (j - 1) * P, N_META + j * P)
                for k in range(KD):
                    ins = mm(ps[0:cols.stop - cols.start, 2, j * P:(j + 1) * P], mix[:, k, cols], wkv[:, k, 2 * P:3 * P],
                             start=(k == 0), stop=(k == KD - 1))
            ins.then_inc(sem("kv_psum"), 1)
            x = (xh, xl)
            pe.wait_ge(sem("kT_ready"), 2)
            pe.wait_ge(sem("v_ready"), 2)
            for c in range(KD):
                piece = FIRST_PIECE["w_q"] + c // 2
                pe.wait_ge(sem("lo_done"), piece + 1)
                if c >= 4:
                    pe.wait_ge(sem("q_ready"), c - 3)
                for k in range(KD):
                    pe.wait_ge(sem("x_ready"), KD + k + 1)
                    at = slice(k * 256 + c % 2 * P, k * 256 + c % 2 * P + P)
                    ins = mm3(ps[:, c % 4, 0:SEQ], (wh[:, piece % 2, at], wl[:, piece % 2, at]),
                              (xh[:, k, 0:SEQ], xl[:, k, 0:SEQ]), k == 0, k == KD - 1)
                ins.then_inc(sem("q_psum"), 1)

            def scores(g):
                for h in range(HEADS_PER_GROUP * g, HEADS_PER_GROUP * (g + 1)):
                    rows = slice(h % 2 * HD, h % 2 * HD + HD)
                    for b in range(NB):
                        i = NB * h + b
                        keys = slice(0, N_META + P) if b == 0 else slice(N_META, T)
                        if i >= 4:
                            pe.wait_ge(sem("lg_ready"), i - 3)
                        mm(ps[:, i % 4, 0:keys.stop - keys.start], qT[rows, h // 2, b * P:(b + 1) * P],
                           kT[rows, h // 8, keys], start=True, stop=True).then_inc(sem("s_psum"), 1)

            def values(h):
                i = 2 * (h % HEADS_PER_GROUP)
                p = lg[h // HEADS_PER_GROUP % 2]
                pe.wait_ge(sem("p_ready"), 2 * h + 2)
                if h >= 2:
                    pe.wait_ge(sem("pt_ready"), 2 * h - 2)
                t = ps[:, 4 + h % 2, :]
                pe.transpose(t[:, 0:P], p[:, i, N_META:N_META + P], ident)
                pe.transpose(t[:, P:2 * P], p[:, i + 1, 0:P], ident)
                pe.transpose(t[:, 2 * P:3 * P], p[:, i + 1, P:2 * P], ident)
                pe.transpose(t[0:N_META, 3 * P:4 * P], p[:, i, 0:N_META], ident).then_inc(sem("pt_psum"), 1)

            def outputs(h):
                pe.wait_ge(sem("pt_ready"), 2 * h + 2)
                if h % 2 == 0 and h >= 4:
                    pe.wait_ge(sem("o_ready"), h // 2 - 1)
                c = h // 2
                v = slice(h // 8 * HD, h // 8 * HD + HD)
                o = ps[h % 2 * HD:h % 2 * HD + HD, 6 + c % 2, 0:SEQ]
                t = pT[h % 2]
                mm(o[:, 0:P], vtok[0:N_META, 0, v], t[0:N_META, 3 * P:4 * P], start=True, stop=False)
                mm(o[:, 0:P], vtok[:, 1, v], t[:, 0:P], start=False, stop=True)
                mm(o[:, P:2 * P], vtok[:, 1, v], t[:, P:2 * P], start=True, stop=False)
                mm(o[:, P:2 * P], vtok[:, 2, v], t[:, 2 * P:3 * P], start=False, stop=True).then_inc(sem("o_done"), 1)

            pe.wait_ge(sem("q_ready"), KD)
            scores(0)
            for g in range(NH // HEADS_PER_GROUP):
                if g + 1 < NH // HEADS_PER_GROUP:
                    scores(g + 1)
                heads = range(HEADS_PER_GROUP * g, HEADS_PER_GROUP * (g + 1))
                for h in heads:
                    values(h)
                    if h > heads[0]:
                        outputs(h - 1)
                outputs(heads[-1])
            for c in range(KD):
                piece = FIRST_PIECE["w_o"] + c // 2
                pe.wait_ge(sem("lo_done"), piece + 1)
                if c >= 4:
                    pe.wait_ge(sem("sq_ready"), SQ0["mixpost1"] + c - 3)
                for k in range(KD):
                    pe.wait_ge(sem("o_ready"), k + 1)
                    at = slice(k * 256 + c % 2 * P, k * 256 + c % 2 * P + P)
                    ins = mm3(ps[:, c % 4, 0:SEQ], (wh[:, piece % 2, at], wl[:, piece % 2, at]),
                              (xh[:, k, 0:SEQ], xl[:, k, 0:SEQ]), k == 0, k == KD - 1)
                ins.then_inc(sem("wo_psum"), 1)
                if c:
                    sum_squares("mixpost1", c - 1, SEQ)
            sum_squares("mixpost1", KD - 1, SEQ)
            ffn_pe(pe, mm3, sum_squares, 1, SEQ)

            for c in range(KD):
                sum_squares("norm1", c, SEQ)
            def sgu_mix():
                pe.wait_ge(sem("sgu_v"), 1)
                pe.wait_ge(sem("sgw_masked"), 1)
                for g in range(SG):
                    ins = mm(ps[:, 7, g * P:(g + 1) * P].rearrange("p (b c) -> p b c", b=NB), sgw[:, g, :],
                             vc[:, :, g * SG_D:(g + 1) * SG_D], start=True, stop=True)
                ins.then_inc(sem("sgu_psum"), 1)

            def sgu_transposes():
                pe.wait_ge(sem("sgu_out"), NB)
                for c in range(SG_W // P):
                    for b in range(NB):
                        ins = pe.transpose(ps[:, 7, c * SEQ + b * P:c * SEQ + b * P + P], uc[:, b, c * P:(c + 1) * P], ident)
                ins.then_inc(sem("yc_psum"), 1)

            def sb_scores(h):
                rows = slice(h % 2 * HD, h % 2 * HD + HD)
                pe.wait_ge(sem("z_evac"), z_done("ka", SB_C - 1))
                if h >= 2:
                    pe.wait_ge(sem("sb_exp"), h - 1)
                q, k, z = qaT[rows, h // 2, :], kaT[rows, h // 2, :], ps[:, 3 + h % 2, :]
                mm(z[:, 0:SEQ], k[:, 0:P], q, start=True, stop=False, skip_group_check=True)
                mm(z[:, SEQ:3 * P], k[:, P:SEQ], q[:, P:SEQ], start=False, stop=False, skip_group_check=True)\
                    .then_inc(sem("sb_z"), 1)

            def sb_after(h):
                pe.wait_ge(sem("sb_sp"), h + 1)
                z, s = ps[:, 3 + h % 2, :], sp[:, h % 2, :]
                mm(z[:, 0:SEQ], C("negtri"), s[:, 0:SEQ], start=False, stop=False, skip_group_check=True)
                mm(z[:, P:SEQ], nones[:, :], s[:, SEQ:3 * P], start=False, stop=False, skip_group_check=True)
                mm(z[:, SEQ:3 * P], C("negtri"), s[:, SEQ:3 * P], start=False, stop=True, skip_group_check=True)\
                    .then_inc(sem("sb_E"), 1)

            def sb_values(h):
                pe.wait_ge(sem("sb_a"), h + 1)
                pe.wait_ge(sem("z_evac"), z_done("vab", 1))
                if h == 2:
                    pe.wait_ge(sem("yc_ready"), 1)
                if h == 4:
                    pe.wait_ge(sem("sq_ready"), SQ0["sb_out"] + 1)
                o, w = sb_out_bank(h // 2)[h % 2 * HD:h % 2 * HD + HD, :], aw[:, h % 2, :]
                v = slice(h * HD, (h + 1) * HD)
                mm(o[:, 0:P], va[:, 0, v], w[:, 0:P], start=True, stop=True)
                mm(o[:, P:SEQ], va[:, 0, v], w[:, P:SEQ], start=True, stop=False)
                mm(o[:, P:SEQ], va[:, 1, v], w[:, SEQ:3 * P], start=False, stop=True).then_inc(sem("sb_o"), 1)

            n = 0
            for i, outs in enumerate(Z_OUT):
                piece = FIRST_PIECE["w_z"] + i
                pe.wait_ge(sem("lo_done"), piece + 1)
                for q, (kind, b) in enumerate(outs):
                    if n >= Z_BANKS:
                        pe.wait_ge(sem("z_evac"), n - Z_BANKS + 1)
                    bank = ps[:, n % Z_BANKS, :]
                    for k in range(KD):
                        pe.wait_ge(sem("x_ready"), 3 * KD + k + 1)
                        if kind in Z_TOKENS:
                            at = slice(k * 256, k * 256 + 256)
                            t = slice(b * P, b * P + P)
                            ins = mm3(bank[:, 0:256], (wh[:, i % 2, at], wl[:, i % 2, at]),
                                      (xh[:, k, t], xl[:, k, t]), k == 0, k == KD - 1, swap=True)
                        else:
                            first, m = z_cols(outs, q)
                            at = slice(k * 256 + first, k * 256 + first + m)
                            ins = mm3(bank[0:m, 0:SEQ], (wh[:, i % 2, at], wl[:, i % 2, at]),
                                      (xh[:, k, 0:SEQ], xl[:, k, 0:SEQ]), k == 0, k == KD - 1)
                    ins.then_inc(sem("z_psum"), 1)
                    n += 1
                if i == 5:
                    sgu_mix()
                if i == 8:
                    sgu_transposes()
                h = i - SB_FIRST
                if 0 <= h < SB_H:
                    sb_scores(h)
                if 1 <= h <= SB_H:
                    sb_after(h - 1)
                if h >= 2:
                    sb_values(h - 2)
            for c in range(SB_C):
                sum_squares("sb_out", c, SEQ)

            pe.wait_ge(sem("gate_g"), 1)
            pe.wait_ge(sem("sb_exp"), SB_H)
            for b in range(NB):
                ins = pe.transpose(ps[:, 3, b * ML_H:(b + 1) * ML_H], gt[0:ML_H, 3, b * P:(b + 1) * P], C("ident", ML_H, ML_H))
            ins.then_inc(sem("gcol_psum"), 1)
            pe.wait_ge(sem("em_ready"), 1)

            def ml_scores(h):
                if h >= 2:
                    pe.wait_ge(sem("ml_max"), 2 * h - 2)
                    pe.wait_ge(sem("ml_em"), h - 1)
                mm(ps[:, 4 + h % 2, :], ident[0:ML_H, h:h + 1].to_broadcast([ML_H, P]),
                   gt[0:ML_H, 5:7, :].rearrange("p a t -> p (a t)"), start=True, stop=True).then_inc(sem("ml_bc"), 1)
                if h == 0:
                    pe.wait_ge(sem("z_evac"), Z_COUNT)
                    pe.wait_ge(sem("cv_ready"), ML_H)
                if h >= 2:
                    pe.wait_ge(sem("ml_w"), h - 1)
                q, k, s = cv[0:ML_D, h, :], cv[0:ML_D, ML_H + h, :], ps[:, h % 2, :]
                mm(s[:, 0:SEQ], k[:, 0:P], q, start=True, stop=True)
                mm(s[:, SEQ:3 * P], k[:, P:SEQ], q[:, P:SEQ], start=True, stop=True).then_inc(sem("ml_s"), 1)

            def ml_values(h):
                pe.wait_ge(sem("ml_w"), h + 1)
                if h == 0:
                    pe.wait_ge(sem("gcol_ready"), 1)
                if h >= 2:
                    pe.wait_ge(sem("ml_h"), h - 1)
                w, o = aw[:, h % 2, :], ps[0:ML_D, 3 + 4 * (h % 2), :]
                v = slice(h * ML_D, (h + 1) * ML_D)
                for lhs0, lhs1, at in ((vb[:, 0, v], vb[:, 1, v], 0), (ones[:, 0:ML_D], ones[:, 0:ML_D], SEQ)):
                    mm(o[:, at:at + P], lhs0, w[:, 0:P], start=True, stop=True)
                    mm(o[:, at + P:at + SEQ], lhs0, w[:, P:SEQ], start=True, stop=False)
                    ins = mm(o[:, at + P:at + SEQ], lhs1, w[:, SEQ:3 * P], start=False, stop=True)
                ins.then_inc(sem("ml_num"), 1)

            def ml_squares(h):
                pe.wait_ge(sem("ml_sq"), h + 1)
                if h:
                    pe.wait_ge(sem("ml_r"), h)
                mm(ps[0:ML_D, 2, 0:SEQ], ones[0:ML_D, 0:ML_D], mix[0:ML_D, h, 0:SEQ], start=True, stop=True)\
                    .then_inc(sem("ml_ss"), 1)

            ml_scores(0)
            ml_scores(1)
            ml_values(0)
            ml_scores(2)
            ml_values(1)
            ml_scores(3)
            for h in range(2, ML_H):
                ml_squares(h - 2)
                ml_values(h)
            for h in range(2, ML_H):
                ml_squares(h)
            for c in range(KD):
                piece = FIRST_PIECE["w_out"] + c
                pe.wait_ge(sem("lo_done"), piece + 1)
                if c >= 4:
                    wait_hs(pe, 4, c - 4)
                for k, (_, rows) in enumerate(y_chunks()):
                    pe.wait_ge(sem("y_split"), k + 1)
                    at = slice(k * P, (k + 1) * P)
                    ins = mm3(ps[:, c % 4, 0:SEQ], (wh[0:rows, c % 2, at], wl[0:rows, c % 2, at]),
                              (xh[0:rows, k, :], xl[0:rows, k, :]), k == 0, k == 8)
                ins.then_inc(sem("wout_psum"), 1)

            for c in range(KD):
                sum_squares("norm2", c, SEQ)
            for b in range(NB):
                for k in range(KD):
                    pe.wait_ge(sem("xn_ready"), KD + k + 1)
                    ins = mm(ps[:, 0, b * 36:(b + 1) * 36], mix[:, k, b * P:(b + 1) * P], rw[:, k, :],
                             start=(k == 0), stop=(k == KD - 1))
            ins.then_inc(sem("router_psum"), 1)
            for b in range(NB):
                for c in range(KD):
                    q = b * 2 + c // 4
                    ins = pe.transpose(ps[:, 1 + q, c % 4 * P:c % 4 * P + P], mix[:, c, b * P:(b + 1) * P], ident)
                    if c % 4 == 3:
                        ins.then_inc(sem("h2_psum"), 1)
            slot, rnd = tile_at(FIRST["w_proj"])
            pe.wait_ge(sem(f"tile_ready{slot}"), 16 * (rnd + 1))
            wp = ring[:, slot, 0:2048].rearrange("p (k n) -> p k n", k=2)
            pt = ring[:, slot, 2048:2560].rearrange("p (k t) -> p k t", k=2)
            for c in range(KD):
                if c >= 2:
                    pe.wait_ge(sem("pp_ready"), c - 1)
                for k in range(2):
                    ins = mm(ps[:, 6 + c % 2, 0:SEQ], wp[:, k, c * P:(c + 1) * P], pt[:, k, :], start=(k == 0), stop=(k == 1))
                ins.then_inc(sem("pp_psum"), 1)
            pe.wait_ge(sem("onehot_ready"), 1)
            oh = onehot
            mm(ps[:, 5, 0:NE], C("strict"), oh(2)[:, 0, :], start=True, stop=True)
            mm(ps[:, 5, NE:2 * NE], ones[:, :], oh(2)[:, 0, :], start=True, stop=False)
            mm(ps[:, 5, NE:2 * NE], C("strict"), oh(2)[:, 1, :], start=False, stop=True)
            mm(ps[:, 5, 2 * NE:3 * NE], ones[:, :], oh(2)[:, 0, :], start=True, stop=False)
            mm(ps[:, 5, 2 * NE:3 * NE], ones[:, :], oh(2)[:, 1, :], start=False, stop=True).then_inc(sem("rank_psum"), 1)
            pe.wait_ge(sem("psel_ready"), 1)
            pe.wait_ge(sem("h2l_ready"), 4)
            for c in range(KD):
                if c >= 4:
                    pe.wait_ge(sem("xs_ready" if c % 2 else "xs_ready_d"), c // 2 - 1)
                for b in range(NB):
                    for src in (h2h, h2l):
                        ins = mm(ps[:, c % 4, :], src[:, b, c * P:(c + 1) * P], psel[:, b, :],
                                 start=(b == 0 and src is h2h), stop=(b == NB - 1 and src is h2l))
                ins.then_inc(sem("xs_psum"), 1)
            pe.wait_ge(sem("combt_ready"), 1)
            pe.wait_ge(sem("pp_ready"), KD)
            for r in range(4):
                for b in range(NB):
                    ins = pe.transpose(ps[:, 6 + r // 2, r % 2 * SEQ + b * P:r % 2 * SEQ + b * P + P],
                                       combt[:, b, r * P:(r + 1) * P], ident)
                if r % 2:
                    ins.then_inc(sem("comb_psum"), 1)
            pe.wait_ge(sem("xs_ready"), KD // 2)
            pe.wait_ge(sem("xs_ready_d"), KD // 2)
            pe.wait_ge(sem("route_ready"), 2)

            def gate_up(e, count):
                def body(halves):
                    for j in range(4):
                        pe.wait_ge(sem("elo_done"), gu_piece_of(e) + (j + 1))
                        pe.wait_ge(sem("xe_ready"), e * 4 + (j + 1))
                        if j == 0 and (type(e) is not int or e):
                            pe.wait_ge(sem("he_ready"), e)
                        b = expert_buffer(j, False, e)
                        for i in range(2):
                            k = 2 * j + i
                            w = slice(i * 512, (i + 1) * 512)
                            for half in range(halves):
                                x = [v[:, k, half * HALF:(half + 1) * HALF] for v in (xeh, xel)]
                                ins = mm3(ps[:, half, :], x, (ewh[:, b, w], ewl[:, b, w]), k == 0, k == KD - 1)
                        ins.then_inc(sem("e_used"), 1)
                for_halves(pe, count, body)

            def transposes(e, count):
                def body(halves):
                    pe.wait_ge(sem("he_ready"), e + 1)
                    for half in range(halves):
                        for c in range(FE // P):
                            ins = pe.transpose(ps[:, 6 + half, c * P:(c + 1) * P], he[:, half, c * P:(c + 1) * P], ident)
                    ins.then_inc(sem("het_psum"), 1)
                for_halves(pe, count, body)

            def down(e, count):
                def body(halves):
                    for k in range(2):
                        pe.wait_ge(sem("elo_done"), dn_piece_of(e) + (k + 1))
                        if k == 0:
                            pe.wait_ge(sem("het_ready"), e + 1)
                            if type(e) is not int or e:
                                pe.wait_ge(sem("y_ready"), e)
                        b = expert_buffer(k, True, e)
                        for i in range(2):
                            w = slice(i * 512, (i + 1) * 512)
                            for half in range(halves):
                                ins = mm3(ps[:, 2 + 2 * half + i, :], (heTh[:, half, k, :], heTl[:, half, k, :]),
                                          (ewh[:, b, w], ewl[:, b, w]), k == 0, k == 1)
                        ins.then_inc(sem("e_used"), 1)
                for_halves(pe, count, body)

            def step(slot, rnd, e):
                transposes(e, value(pe, 1, e))
                gate_up(e + 1, value(pe, 1, e + 1))
                down(e, value(pe, 1, e))

            gate_up(0, value(pe, 1, 0))
            step(*tile_at(FIRST["w_exp"]), 0)
            ring_steps(pe, "w_exp", step, first=1, last=NE - 1)
            transposes(NE - 1, value(pe, 1, NE - 1))
            down(NE - 1, value(pe, 1, NE - 1))
            pe.wait_ge(sem("y_ready"), NE)
            for r in range(4):
                pe.wait_ge(sem(f"ysr_loaded{r}"), 16)
                for c in range(KD):
                    ins = mm(ps[:, c, 0:SEQ], ysr[:, r, c * P:(c + 1) * P], combr[:, r, :], start=(r == 0), stop=(r == 3))
                    if r == 3:
                        ins.then_inc(sem("moe_psum"), 1)

            for c in range(KD):
                piece = FIRST_PIECE["w_ple"] + c // 2
                pe.wait_ge(sem("lo_done"), piece + 1)
                if c >= 4:
                    pe.wait_ge(sem("ple_scaled"), c - 3)
                for k in range(KD):
                    pe.wait_ge(sem("x_ready"), 4 * KD + k + 1)
                    at = slice(k * 256 + c % 2 * P, k * 256 + c % 2 * P + P)
                    ins = mm3(ps[:, c % 4, 0:SEQ], (wh[:, piece % 2, at], wl[:, piece % 2, at]),
                              (xh[:, k, 0:SEQ], xl[:, k, 0:SEQ]), k == 0, k == KD - 1)
                ins.then_inc(sem("ple_psum"), 1)
                if c == 0:
                    for q in range(KD):
                        sum_squares("ple", q, SEQ)
            for c in range(KD):
                sum_squares("final", c, SEQ)

        def normed(dve, dst, src, name, c, r):
            return dve.scalar_tensor_tensor(dst, src, V(name, c), r, ALU.mult, ALU.mult)

        def post_apply(dve, k, norm, cols):
            n = cols.stop - cols.start
            dve.wait_ge(sem("r_ready"), NORM[norm] + 1)
            for c in range(KD):
                dve.wait_ge(sem("mix_ready"), k * KD + c + 1)
                normed(dve, mix[:, c, 0:n], mix[:, c, 0:n], norm, c, r_of(norm)[:, 0:n]).then_inc(sem("delta_ready"), 1)
                if c and c % 2 == 0:
                    residual_add(dve, k, cols, c - 1)
            residual_add(dve, k, cols, KD - 1)

        def x_low(dve, u, c, full, high, low):
            dve.wait_ge(sem("xh_ready"), u * KD + c + 1)
            dve.tensor_tensor(low, full, high.bitcast(F32), ALU.subtract).then_inc(sem("x_ready"), 1)

        def ffn_dve(dve, l, n, cols, unsplit=()):
            gu, dn, pre, post = f"w_gu{l}", f"w_dn{l}", f"ffnpre{l}", f"ffnpost{l}"
            xa, xb = (xhT, xlT) if l == 0 else (xh, xl)
            r = r_of(pre)[:, 0:n]
            for c in range(KD):
                dve.wait_ge(sem("xh_ready"), 2 * l * KD + c + 1)
                dve.scalar_tensor_tensor(xb[:, c, 0:n], hs[:, c, cols], V(pre, c), xa[:, c, 0:n].bitcast(F32),
                                         ALU.mult, ALU.subtract).then_inc(sem("x_ready"), 1)
            for args in unsplit:
                split_lo(dve, gu, *args)
            dve.wait_ge(sem("r_ready"), NORM[pre] + 1)

            def gate(f, j):
                dve.wait_ge(sem("gu_psum"), f + (l * NF + 1))
                dve.tensor_tensor(mix[:, j, 0:n], ps[:, 2 * j, 0:n], r, ALU.mult).then_inc(sem("gr_ready"), 1)

            def up(j):
                dve.tensor_tensor(mix[:, 4 + j, 0:n], ps[:, 2 * j + 1, 0:n], r, ALU.mult).then_inc(sem("up_ready"), 1)

            def body(slot, rnd, i):
                for j in range(2):
                    f = i * 2 + (j - 2)
                    if not (type(i) is int and i == 1):
                        dve.wait_ge(sem("act_ready"), f + (l * NF - 1))
                    gate(f, j)
                    split_lo(dve, gu, slot, rnd, i, j, PIECE)
                    up(j)

            body(*tile_at(FIRST[gu] + 1), 1)
            ring_steps(dve, gu, body, first=2)
            for j in range(2):
                dve.wait_ge(sem("act_ready"), NF - 2 + j + l * NF - 1)
                gate(NF - 2 + j, j)
                split_lo(dve, dn, *halves(dn, 0, FF // 2)[j])
                up(j)
            for i in range(1, KD):
                for args in halves(dn, i, FF // 2):
                    split_lo(dve, dn, *args)
            post_apply(dve, 2 * l + 1, post, cols)

        def first_of_ties(dve, chain, values, top, order, key, oh):
            n = values.shape[-1]
            chain(dve.tensor_tensor(key, values, top.unsqueeze(2).to_broadcast([P, NB, n]), ALU.is_equal))
            chain(dve.tensor_tensor(key, key, order.unsqueeze(1).to_broadcast([P, NB, n]), ALU.mult))
            chain(dve.tensor_reduce(small[:, 410:412], key, AX.X, ALU.max))
            chain(dve.tensor_tensor(oh, key, small[:, 410:412].unsqueeze(2).to_broadcast([P, NB, n]), ALU.is_equal))

        def routing(dve, chain):
            scr = rscr
            width = NGRP + NE
            rl = scr[:, 0:NB * width].rearrange("p (b n) -> p b n", b=NB)
            at = NB * width

            def room(n):
                nonlocal at
                at += NB * n
                return scr[:, at - NB * n:at].rearrange("p (b n) -> p b n", b=NB)

            key4, oh4, el, key, pos, desc = room(NGRP), room(NGRP), room(NE), room(NE), room(NE), scr[:, 1024:1024 + NE]
            gl = small[:, 128:136].rearrange("p (b n) -> p b n", b=NB)
            gmax, gsum, v1, v2, rec = (small[:, 140 + 2 * i:142 + 2 * i] for i in range(5))
            pos1, pos2, w1, w2 = (small[:, 160 + 2 * i:162 + 2 * i] for i in range(4))
            ex = small[:, 180:182]
            dve.wait_ge(sem("router_psum"), 1)
            chain(dve.tensor_tensor(rl, ps[:, 0, 0:NB * width].rearrange("p (b n) -> p b n", b=NB),
                                    R("router_b", width).unsqueeze(1).to_broadcast([P, NB, width]), ALU.add))
            chain(dve.tensor_reduce(gmax, rl[:, :, 0:NGRP], AX.X, ALU.max))
            dve.tensor_tensor(gl, rl[:, :, 0:NGRP], gmax.unsqueeze(2).to_broadcast([P, NB, NGRP]), ALU.subtract)\
               .then_inc(sem("route_g"), 1)
            first_of_ties(dve, chain, rl[:, :, 0:NGRP], gmax, R("desc", NGRP), key4, oh4)
            oh4x = oh4.unsqueeze(3).to_broadcast([P, NB, NGRP, EPG])
            el4 = el.rearrange("p b (g e) -> p b g e", e=EPG)
            key44 = key.rearrange("p b (g e) -> p b g e", e=EPG)
            chain(dve.tensor_scalar(key44, oh4x, 3e38, -3e38, ALU.mult, ALU.add))
            chain(dve.tensor_tensor(el4, rl[:, :, NGRP:].rearrange("p b (g e) -> p b g e", e=EPG), oh4x, ALU.mult))
            chain(dve.tensor_tensor(el, el, key, ALU.add))
            dve.wait_ge(sem("iota_ready"), 1)
            chain(dve.tensor_scalar(desc, iota[:, 0:NE], -1.0, float(NE), ALU.mult, ALU.add))
            chain(dve.tensor_reduce(v1, el, AX.X, ALU.max))
            first_of_ties(dve, chain, el, v1, desc, key, onehot(0))
            chain(dve.scalar_tensor_tensor(el, onehot(0), -3e38, el, ALU.mult, ALU.add))
            chain(dve.tensor_reduce(v2, el, AX.X, ALU.max))
            first_of_ties(dve, chain, el, v2, desc, key, onehot(1))
            dve.tensor_tensor(onehot(2), onehot(0), onehot(1), ALU.add).then_inc(sem("onehot_ready"), 1)
            dve.tensor_tensor(ex, v2, v1, ALU.subtract).then_inc(sem("route_d"), 1)
            dve.wait_ge(sem("rank_psum"), 1)
            count, incl = scr[:, 1100:1100 + NE], scr[:, 1200:1200 + NE]
            chain(dve.tensor_copy(count, ps[:, 5, 2 * NE:3 * NE]))
            chain(dve.tensor_tensor_scan(incl, count, count, 0.0, ALU.add, ALU.max))
            chain(dve.tensor_tensor(incl, incl, count, ALU.subtract))
            dve.tensor_copy(route_i[:, 0, :], incl).then_inc(sem("route_ready"), 1)
            dve.tensor_copy(route_i[:, 1, :], count).then_inc(sem("route_ready"), 1)
            chain(dve.tensor_tensor(pos, ps[:, 5, 0:NB * NE].rearrange("p (b e) -> p b e", b=NB),
                                    incl.unsqueeze(1).to_broadcast([P, NB, NE]), ALU.add))
            for oh, p in ((onehot(0), pos1), (onehot(1), pos2)):
                chain(dve.tensor_tensor(key, oh, pos, ALU.mult))
                chain(dve.tensor_reduce(p, key, AX.X, ALU.add))
            for b in range(NB):
                first = scr[:, 2048 + b * ROWS:2048 + (b + 1) * ROWS]
                chain(dve.tensor_scalar(first, iota[:, :], pos1[:, b:b + 1], None, ALU.is_equal))
                ins = dve.scalar_tensor_tensor(psel[:, b, :], iota[:, :], pos2[:, b:b + 1], first, ALU.is_equal, ALU.add)
            ins.then_inc(sem("psel_ready"), 1)
            dve.wait_ge(sem("route_gexp"), 1)
            dve.wait_ge(sem("route_ex"), 1)
            chain(dve.tensor_reduce(gsum, gl, AX.X, ALU.add))
            chain(dve.tensor_scalar(rec, ex, 1.0, None, ALU.add))
            chain(dve.tensor_tensor(rec, rec, gsum, ALU.mult))
            chain(dve.reciprocal(w1, rec))
            chain(dve.tensor_tensor(w2, ex, w1, ALU.mult))
            second = scr[:, 1536:1536 + ROWS]
            for b in range(NB):
                chain(dve.tensor_scalar(combt[:, b, :], iota[:, :], pos1[:, b:b + 1], w1[:, b:b + 1], ALU.is_equal, ALU.mult))
                chain(dve.tensor_scalar(second, iota[:, :], pos2[:, b:b + 1], w2[:, b:b + 1], ALU.is_equal, ALU.mult))
                ins = dve.tensor_tensor(combt[:, b, :], combt[:, b, :], second, ALU.add)
                if b == 0:
                    chain(ins)
            ins.then_inc(sem("combt_ready"), 1)

        @block.vector
        def _(dve):
            chain = Chain(dve, "dve_chain")
            dve.wait_ge(sem("consts_loaded"), 32)
            dve.wait_ge(sem("hs_loaded"), 16)
            dve.wait_ge(sem("r_ready"), 1)
            for c in range(KD):
                normed(dve, hp[:, c, PADT:], hs[:, c, :], "mixpre0", c, r_of("mixpre0")).then_inc(sem("h_ready"), 1)
            pool_groups(dve, chain, (2, 3), "p_dve")
            for x in halves("w_gu0", 0, PIECE):
                split_lo(dve, "w_gu0", *x)
            post_apply(dve, 0, "mixpost0", slice(0, T))
            ffn_dve(dve, 0, T, slice(0, T))

            dve.wait_ge(sem("r_ready"), NORM["pre1"] + 1)
            dve.wait_ge(sem("dn_psum"), 2 * KD)
            r = r_of("pre1")
            for c in range(KD):
                normed(dve, mix[:, c, :], hs[:, c, :], "kv_norm", c, r).then_inc(sem("kvin_ready"), 1)
            for c in range(KD):
                normed(dve, h1[:, c, :], hs[:, c, N_META:], "mixpre1", c, r[:, N_META:]).then_inc(sem("h1_ready"), 1)
            for x in halves("w_q", 0, PIECE):
                split_lo(dve, "w_q", *x)
            for c in range(KD):
                x_low(dve, 1, c, h1[:, c, :], xh[:, c, :], xl[:, c, :])
            dve.wait_ge(sem("tables_loaded"), 64)
            dve.wait_ge(sem("kv_psum"), 3)
            b_v = R("b_v", P)
            dve.tensor_tensor(vtok[0:N_META, 0, :], ps[0:N_META, 2, 0:P], b_v[0:N_META, :], ALU.add).then_inc(sem("v_ready"), 1)
            dve.tensor_tensor(vtok[:, 1:3, :], ps[:, 2, P:3 * P].rearrange("p (b n) -> p b n", b=NB),
                              b_v.unsqueeze(1).to_broadcast([P, NB, P]), ALU.add).then_inc(sem("v_ready"), 1)
            low = {1: ("w_q", halves("w_q", 1, PIECE)[0]), 3: ("w_q", halves("w_q", 1, PIECE)[1]),
                   5: ("w_o", halves("w_o", 0, PIECE)[0]), 7: ("w_o", halves("w_o", 0, PIECE)[1])}
            for c in range(KD):
                dve.wait_ge(sem("q_psum"), c + 1)
                dve.tensor_scalar(qT[:, c, :].rearrange("p (b q) -> p b q", q=P)[:, :, ::-1],
                                  ps[:, c % 4, 0:SEQ].rearrange("p (b q) -> p b q", q=P), V("b_q", c), HD ** -0.5,
                                  ALU.add, ALU.mult).then_inc(sem("q_ready"), 1)
                if c in low:
                    split_lo(dve, low[c][0], *low[c][1])

            PER = NB * HEADS_PER_GROUP

            def logits(g):
                if g == 0:
                    dve.wait_ge(sem("bias_ready"), 16)
                for i in range(PER * g, PER * (g + 1)):
                    n, first = (N_META + P, P - N_META) if i % 2 == 0 else (2 * P, 0)
                    dve.wait_ge(sem("s_psum"), i + 1)
                    dve.tensor_tensor_reduce(out=lg[g % 2][:, i % PER, 0:n], in0=ps[:, i % 4, 0:n],
                                             in1=brev[:, i // 2, first:SEQ], scale=1.0, scalar=-3e38,
                                             op0=ALU.add, op1=ALU.max, accum_out=small[:, i:i + 1])\
                       .then_inc(sem("lg_ready"), 1)
                k = PER * g
                dve.wait_ge(sem("lg_ready"), PER * (g + 1))
                m = small[:, k:k + PER].rearrange("p (h b) -> p h b", b=NB)
                sink = R("sinks", HEADS_PER_GROUP, HEADS_PER_GROUP * g).unsqueeze(2).to_broadcast([P, HEADS_PER_GROUP, NB])
                chain(dve.tensor_tensor(m, m, sink, ALU.max))
                chain(dve.tensor_tensor(small[:, 64 + k:64 + k + PER].rearrange("p (h b) -> p h b", b=NB), sink, m, ALU.subtract))
                dve.tensor_scalar(small[:, 32 + k:32 + k + PER], small[:, k:k + PER], -1.0, None, ALU.mult)\
                   .then_inc(sem("negm_ready"), 1)

            GROUPS = NH // HEADS_PER_GROUP
            logits(0)
            for g in range(GROUPS):
                if g + 1 < GROUPS:
                    if g:
                        dve.wait_ge(sem("pt_psum"), HEADS_PER_GROUP * g)
                    logits(g + 1)
                k = PER * g
                dve.wait_ge(sem("exp_ready"), (PER + 1) * (g + 1))
                den = small[:, 96 + k:96 + k + PER]
                chain(dve.tensor_tensor(den, den, small[:, 64 + k:64 + k + PER], ALU.add))
                chain(dve.reciprocal(den, den))
                for i in range(PER):
                    n = N_META + P if i % 2 == 0 else 2 * P
                    v = lg[g % 2][:, i, 0:n]
                    dve.tensor_scalar(v, v, den[:, i:i + 1], None, ALU.mult).then_inc(sem("p_ready"), 1)
                for h in range(HEADS_PER_GROUP * g, HEADS_PER_GROUP * (g + 1)):
                    if h % 2 == 1:
                        c = h // 2
                        dve.wait_ge(sem("oh_ready"), c + 1)
                        o = ps[:, 6 + c % 2, 0:SEQ].rearrange("p (b q) -> p b q", q=P)[:, :, ::-1]
                        dve.tensor_tensor(xl[:, c, :].rearrange("p (b q) -> p b q", q=P), o,
                                          xh[:, c, :].bitcast(F32).rearrange("p (b q) -> p b q", q=P), ALU.subtract)\
                           .then_inc(sem("o_ready"), 1)
            for x in halves("w_o", 1, PIECE):
                split_lo(dve, "w_o", *x)
            split_lo(dve, "w_gu1", *halves("w_gu1", 0, PIECE)[0])
            post_apply(dve, 2, "mixpost1", slice(N_META, T))
            ffn_dve(dve, 1, SEQ, slice(N_META, T), halves("w_gu1", 0, PIECE)[1:])

            for x in halves("w_z", 0, PIECE):
                split_lo(dve, "w_z", *x)

            def norm_input(name):
                dve.wait_ge(sem("r_ready"), NORM[name] + 1)
                for c in range(KD):
                    normed(dve, mix[:, c, 0:SEQ], hs[:, c, N_META:], name, c, r_of(name)[:, 0:SEQ])\
                        .then_inc(sem("xn_ready"), 1)

            norm_input("norm1")
            for c in range(KD):
                x_low(dve, 3, c, mix[:, c, 0:SEQ], xh[:, c, :], xl[:, c, :])
            groups = vc.rearrange("p b (g c) -> p (b g) c", c=SG_D)
            NG = NB * SG
            g4 = [gt[0:ML_H, i, :] for i in range(7)]

            def sgu_gates():
                dve.wait_ge(sem("z_evac"), z_done("vc", 1))
                chain(dve.tensor_reduce(small[:, 0:NG], groups, AX.X, ALU.add))
                dve.scalar_tensor_tensor(groups, small[:, 0:NG].unsqueeze(2).to_broadcast([P, NG, SG_D]), -1.0 / SG_D, groups,
                                         ALU.mult, ALU.add).then_inc(sem("sgu_centred"), 1)

            def sgu_variance():
                dve.wait_ge(sem("sgu_sq"), 1)
                dve.tensor_reduce(small[:, 8:8 + NG].rearrange("p (b g) -> p b g", g=SG),
                                  mix[:, 0:2, 0:SG_W].rearrange("p b (g c) -> p b g c", c=SG_D), AX.X, ALU.add)\
                   .then_inc(sem("sgu_var"), 1)

            def sgu_normed():
                dve.wait_ge(sem("tables_loaded"), 64)
                dve.wait_ge(sem("sgu_r"), 1)
                chain(dve.tensor_tensor(groups, groups, small[:, 8:8 + NG].unsqueeze(2).to_broadcast([P, NG, SG_D]), ALU.mult))
                chain(dve.tensor_tensor(vc, vc, R("ln_g", SG_W).unsqueeze(1).to_broadcast([P, NB, SG_W]), ALU.mult))
                dve.tensor_tensor(vc, vc, R("ln_b", SG_W).unsqueeze(1).to_broadcast([P, NB, SG_W]), ALU.add)\
                   .then_inc(sem("sgu_v"), 1)

            def sgu_gated():
                dve.wait_ge(sem("sgu_psum"), 1)
                for g in range(SG):
                    u = uc[:, :, g * SG_D:(g + 1) * SG_D]
                    dve.scalar_tensor_tensor(u, ps[:, 7, g * P:(g + 1) * P].rearrange("p (b c) -> p b c", b=NB), V("sgu_b", g), u,
                                             ALU.add, ALU.mult).then_inc(sem("sgu_y"), 1)

            def sgu_scaled():
                dve.wait_ge(sem("sgu_yr"), 1)
                for b in range(NB):
                    dve.scalar_tensor_tensor(uc[:, b, :], uc[:, b, :], small[:, 16 + b:17 + b], R("sgu_out", SG_W),
                                             ALU.mult, ALU.mult).then_inc(sem("sgu_out"), 1)

            def ml_gates():
                dve.wait_ge(sem("gate_ln"), 1)
                chain(dve.tensor_scalar(g4[1], g4[1], 0.0, None, ALU.min))
                chain(dve.tensor_tensor_scan(g4[4], g4[1], g4[2], 0.0, ALU.add, ALU.subtract))
                dve.tensor_tensor(g4[3], g4[0], g4[4], ALU.subtract).then_inc(sem("gate_g"), 1)
                dve.wait_ge(sem("gate_g"), 1)
                chain(dve.tensor_tensor_scan(g4[5], g4[3], g4[3], 0.0, ALU.max, ALU.max))
                dve.tensor_tensor(g4[6], g4[4], g4[5], ALU.add).then_inc(sem("gate_m"), 1)

            def sb_softplus(i):
                dve.wait_ge(sem("sb_ln"), i + 1)
                if i >= 2:
                    dve.wait_ge(sem("sb_E"), i - 1)
                s = sp[:, i % 2, :]
                chain(dve.scalar_tensor_tensor(s, ps[:, 3 + i % 2, 0:3 * P], 0.0, e1[:, i % 2, :], ALU.max, ALU.add))
                diag = s.rearrange("p (a b) -> p a b", a=3)[:, 0:3:2, :]
                dve.tensor_tensor(diag, diag, C("strict").unsqueeze(1).to_broadcast([P, 2, P]), ALU.mult)\
                   .then_inc(sem("sb_sp"), 1)

            def conv_silu(i):
                j = 2 * i
                dve.wait_ge(sem("conv_sig"), i + 1)
                dve.tensor_tensor(cv[0:ML_D, j:j + 2, :], cv[0:ML_D, j:j + 2, :], conv_sigmoid(i), ALU.mult)\
                   .then_inc(sem("cv_ready"), 1)

            behind = {4: [sgu_gates], 5: [sgu_variance], 6: [sgu_normed], 7: [sgu_gated], 8: [sgu_scaled],
                      10: [ml_gates]}
            for piece in range(2, 18):
                if piece < 14:
                    split_lo(dve, "w_z", *halves("w_z", piece // 2, PIECE)[piece % 2])
                for work_ in behind.get(piece, []):
                    work_()
                if 0 <= piece - 2 - SB_FIRST < SB_H:
                    sb_softplus(piece - 2 - SB_FIRST)
                if 13 <= piece < 13 + ML_H:
                    conv_silu(piece - 13)
                if 11 <= piece < 11 + ML_H:
                    for j in range(2 * (piece - 11), 2 * (piece - 11) + 2):
                        conv(dve, chain, j, "conv_done")
                    i = piece - 11
                    dve.wait_ge(sem("conv_done"), 2 * i + 2)
                    if i >= 2:
                        dve.wait_ge(sem("cv_ready"), i - 1)
                    dve.tensor_scalar(conv_sigmoid(i), cv[0:ML_D, 2 * i:2 * i + 2, :], -80.0, None, ALU.max)\
                       .then_inc(sem("conv_bounded"), 1)

            dve.wait_ge(sem("z_evac"), Z_COUNT)
            dve.tensor_scalar(ob[0:ML_D, :, :], ob[0:ML_D, :, :], -80.0, None, ALU.max).then_inc(sem("ob_bounded"), 1)

            dve.wait_ge(sem("gcol_psum"), 1)
            dve.tensor_copy(small[:, 20:20 + NB * ML_H], ps[:, 3, 0:NB * ML_H]).then_inc(sem("gcol_ready"), 1)
            dve.wait_ge(sem("gcol_ready"), 1)

            def ml_maxima(h):
                dve.wait_ge(sem("ml_bc"), h + 1)
                if h >= 2:
                    dve.wait_ge(sem("ml_exp"), 2 * h - 2)
                for b, cols in ((0, slice(0, SEQ)), (1, slice(SEQ, 3 * P))):
                    at = 20 + ML_H * b + h
                    dve.tensor_scalar(sp[:, h % 2, cols], ps[:, 4 + h % 2, b * P:SEQ], small[:, at:at + 1], None, ALU.max)\
                       .then_inc(sem("ml_max"), 1)

            def ml_weights(h):
                dve.wait_ge(sem("ml_s"), h + 1)
                dve.wait_ge(sem("ml_d"), h + 1)
                w = aw[:, h % 2, :]
                dve.scalar_tensor_tensor(w, ps[:, h % 2, 0:3 * P], ML_D ** -0.5, w, ALU.mult, ALU.mult)\
                   .then_inc(sem("ml_w"), 1)

            def ml_quotient(h):
                dve.wait_ge(sem("ml_num"), h + 1)
                dve.wait_ge(sem("ml_em"), h + 1)
                den = e1[0:ML_D, h % 2, 0:SEQ]
                o = ps[0:ML_D, 3 + 4 * (h % 2), :]
                chain(dve.tensor_tensor(den, o[:, SEQ:2 * SEQ], den, ALU.max))
                chain(dve.scalar_tensor_tensor(den, o[:, SEQ:2 * SEQ], -1.0, den, ALU.mult, ALU.max))
                chain(dve.reciprocal(den, den))
                dve.tensor_tensor(yb[0:ML_D, h, :], o[:, 0:SEQ], den, ALU.mult).then_inc(sem("ml_h"), 1)

            def ml_output(h):
                dve.wait_ge(sem("ml_r"), h + 1)
                dve.wait_ge(sem("ob_ready"), 1)
                y = yb[0:ML_D, h, :]
                chain(dve.scalar_tensor_tensor(y, y, V("mnorm", h, ML_D), mix[0:ML_D, ML_H + h, 0:SEQ], ALU.mult, ALU.mult))
                dve.tensor_tensor(y, y, ob[0:ML_D, h, :], ALU.mult).then_inc(sem("y_fin"), 1)

            ml_maxima(0)
            dve.wait_ge(sem("r_ready"), NORM["sb_out"] + 1)
            dve.wait_ge(sem("ya_ready"), SB_C)
            for c in range(SB_C):
                normed(dve, yaT[:, c, :], yaT[:, c, :], "sb_out", c, r_of("sb_out")[:, 0:SEQ]).then_inc(sem("y_fin"), 1)
            def y_low(j):
                src, rows = y_chunks()[j]
                dve.wait_ge(sem("yh_ready"), j + 1)
                dve.tensor_tensor(xl[0:rows, j, :], src, xh[0:rows, j, :].bitcast(F32), ALU.subtract)\
                   .then_inc(sem("y_split"), 1)

            ml_maxima(1)
            ml_weights(0)
            ml_weights(1)
            ml_maxima(2)
            ml_quotient(0)
            ml_maxima(3)
            ml_weights(2)
            ml_quotient(1)
            ml_output(0)
            ml_weights(3)
            for x in halves("w_out", 0, 9 * P):
                split_lo(dve, "w_out", *x)
            ml_quotient(2)
            ml_output(1)
            ml_quotient(3)
            for j in range(SB_C + NB):
                y_low(j)
            for h in (2, 3):
                y_low(SB_C + NB + h - 2)
                ml_output(h)
            for h in (2, 3):
                y_low(SB_C + NB + h)
            for c in range(KD):
                if c + 2 < KD:
                    split_lo(dve, "w_out", *halves("w_out", (c + 2) // 2, 9 * P)[c % 2])
                dve.wait_ge(sem("wout_psum"), c + 1)
                dve.tensor_tensor(hs[:, c, N_META:], hs[:, c, N_META:], ps[:, c % 4, 0:SEQ], ALU.add)\
                   .then_inc(hs_add(c), 1)

            norm_input("norm2")
            for q in range(4):
                dve.wait_ge(sem("h2_ready"), q + 1)
                at = slice(q % 2 * 512, (q % 2 + 1) * 512)
                dve.tensor_tensor(h2l[:, q // 2, at], ps[:, 1 + q, :], h2h[:, q // 2, at].bitcast(F32), ALU.subtract)\
                   .then_inc(sem("h2l_ready"), 1)
            routing(dve, chain)
            for c in range(0, KD, 2):
                dve.wait_ge(sem("xs_psum"), c + 1)
                dve.tensor_copy(xs[:, c * XS:c * XS + ROWS], ps[:, c % 4, :]).then_inc(sem("xs_ready_d"), 1)

            def low(e, j, is_down, slot):
                g = (dn_piece_of(e) if is_down else gu_piece_of(e)) + j
                b = expert_buffer(j, is_down, e)
                dve.wait_ge(sem("ehi_done"), g + 1)
                at = (4096 if is_down else 0) + j * EPIECE
                dve.tensor_tensor(ewl[:, b, :], ring[:, slot, at:at + EPIECE], ewh[:, b, :].bitcast(F32), ALU.subtract)\
                   .then_inc(sem("elo_done"), 1)

            def gated(e, count):
                def body(halves):
                    dve.wait_ge(sem("sg_ready"), e + 1)
                    dve.tensor_tensor(he[:, 0:halves, :], sgate[:, 0:halves, :], ps[:, 0:halves, FE:2 * FE], ALU.mult)\
                       .then_inc(sem("he_ready"), 1)
                for_halves(dve, count, body)

            def transposed(e, count):
                def body(halves):
                    dve.wait_ge(sem("heth_ready"), e + 1)
                    dve.tensor_tensor(heTl[:, 0:halves, :, :].rearrange("p a c n -> p a (c n)"), ps[:, 6:6 + halves, 0:FE],
                                      heTh[:, 0:halves, :, :].bitcast(F32).rearrange("p a c n -> p a (c n)"), ALU.subtract)\
                       .then_inc(sem("het_ready"), 1)
                for_halves(dve, count, body)

            def step(slot, rnd, e):
                nxt = (slot + 1) % SLOTS
                low(e + 1, 0, False, nxt)
                count = value(dve, 1, e)
                gated(e, count)
                low(e + 1, 1, False, nxt)
                low(e + 1, 2, False, nxt)
                transposed(e, count)
                low(e + 1, 3, False, nxt)
                for j in range(2):
                    low(e, j, True, slot)

            slot, rnd = tile_at(FIRST["w_exp"])
            for j in range(4):
                low(0, j, False, slot)
            step(slot, rnd, 0)
            ring_steps(dve, "w_exp", step, first=1, last=NE - 1)
            last = NE - 1
            slot, rnd = tile_at(FIRST["w_exp"] + last)
            gated(last, value(dve, 1, last))
            low(last, 0, True, slot)
            transposed(last, value(dve, 1, last))
            low(last, 1, True, slot)
            for x in halves("w_ple", 0, PIECE):
                split_lo(dve, "w_ple", *x)
            for c in range(KD):
                dve.wait_ge(sem("moe_psum"), c + 1)
                dve.tensor_tensor(hs[:, c, N_META:], hs[:, c, N_META:], ps[:, c, 0:SEQ], ALU.add).then_inc(hs_add(c), 1)
            for c in range(KD):
                dve.wait_ge(sem("xh_ready"), 4 * KD + c + 1)
                dve.scalar_tensor_tensor(xl[:, c, :], hs[:, c, N_META:], V("ple", c), xh[:, c, :].bitcast(F32),
                                         ALU.mult, ALU.subtract).then_inc(sem("x_ready"), 1)
            dve.wait_ge(sem("r_ready"), NORM["ple"] + 1)
            dve.wait_ge(sem("pp_ready"), KD)

            def gate_add(c):
                dve.wait_ge(sem("ple_sig"), c + 1)
                chain(dve.tensor_tensor(mix[:, c, 0:SEQ], mix[:, c, 0:SEQ], ppT[:, c, :], ALU.mult))
                dve.tensor_tensor(hs[:, c, N_META:], hs[:, c, N_META:], mix[:, c, 0:SEQ], ALU.add).then_inc(hs_add(c), 1)

            for c in range(KD):
                dve.wait_ge(sem("ple_psum"), c + 1)
                dve.tensor_tensor(mix[:, c, 0:SEQ], ps[:, c % 4, 0:SEQ], r_of("ple")[:, 0:SEQ], ALU.mult)\
                   .then_inc(sem("ple_scaled"), 1)
                if c:
                    gate_add(c - 1)
                if c in (1, 3):
                    split_lo(dve, "w_ple", *halves("w_ple", 1, PIECE)[c // 2])
            gate_add(KD - 1)
            dve.wait_ge(sem("r_ready"), NORM["final"] + 1)
            for c in range(KD):
                normed(dve, mix[:, c, 0:SEQ], hs[:, c, N_META:], "final", c, r_of("final")[:, 0:SEQ])\
                    .then_inc(sem("out_ready"), 1)


def _pieces(w, cols):
    import numpy as _np
    n = w.shape[1] // cols
    x = w.reshape(w.shape[0] // P, P, n // 2, 2, cols)
    return _np.ascontiguousarray(x.transpose(2, 1, 3, 0, 4)).reshape(n // 2, P, -1)


def _t5_buckets():
    import math
    import numpy as _np
    n, far = 32, 128
    half = n // 2
    d = _np.arange(P)
    df = _np.maximum(d, 1).astype(_np.float32)
    large = half + (_np.log(df / _np.float32(half)) / _np.float32(math.log(far / half))
                    * _np.float32(n - half)).astype(_np.int32)
    return _np.where(d < half, d, _np.minimum(large, n - 1))


def kernel(**inputs):
    import numpy as _np
    import concourse.bacc as _bacc
    from concourse import mybir as _mybir
    from concourse.bass_utils import run_bass_kernel_spmd as _run

    x = {k: _np.asarray(v) for k, v in inputs.items()}
    f32 = _np.float32
    a = {}
    seq = _np.concatenate([x["meta_tokens"], x["x"][0]], axis=0)
    a["hT"] = seq.T.reshape(KD, P, T).transpose(1, 0, 2)

    vec = _np.zeros((P, NV), f32)

    def put(name, v, rows=P):
        v = v.reshape(-1, rows).T
        vec[0:rows, VCOL[name]:VCOL[name] + v.shape[1]] = v

    for l in range(2):
        put(f"mixpre{l}", x["norm_mix_pre"][l])
        put(f"mixpost{l}", x["norm_mix_post"][l])
        put(f"ffnpre{l}", x["norm_ffn_pre"][l])
        put(f"ffnpost{l}", x["norm_ffn_post"][l])
    put("kv_norm", x["kv_norm"])
    put("pool_scale", x["pool_scale"][0])
    put("norm1", x["norm1_g_2"][0])
    put("norm2", x["norm2_g_2"][0])
    put("ple", x["ple_norm_g_2"][0])
    put("final", x["final_g_2"])
    put("b_q", x["b_q"][0])
    put("b_o", x["b_o"][0])
    put("b_k", _np.concatenate([x["b_k"][0:HD], x["b_k"][0:HD], x["b_k"][HD:], x["b_k"][HD:]]))
    put("sb_out", x["sb_out_g_2"][0])
    put("conv_w", x["conv_w_2"][0].reshape(4, 2 * ML_H, ML_D).transpose(1, 0, 2), ML_D)
    put("conv_b", x["conv_b_2"][0], ML_D)
    put("mnorm", x["mnorm_g_2"][0], ML_D)
    put("igate_b", x["igate_b_2"][0], ML_H)
    put("fgate_b", x["fgate_b_2"][0], ML_H)
    put("sgu_b", x["sgu_b_2"][0])
    a["vec"] = vec

    row = _np.concatenate([x["sinks"][0], x["b_v"], x["sgu_ln_g_2"][0], x["sgu_ln_b_2"][0], x["sgu_out_g_2"][0],
                           x["router_gb_2"][0], x["router_eb_2"][0], _np.arange(NGRP, 0, -1).astype(f32)])
    a["row"] = _np.broadcast_to(row[None], (P, NR))

    cst = _np.zeros((P, NC), f32)
    i, j = _np.arange(P)[:, None], _np.arange(P)[None, :]
    cst[:, CCOL["ident"]:CCOL["ident"] + P] = i == j
    cst[:, CCOL["strict"]:CCOL["strict"] + P] = i < j
    cst[:, CCOL["negtri"]:CCOL["negtri"] + P] = -(i >= j).astype(f32)
    cst[:, CCOL["sgumask"]:CCOL["sgumask"] + P] = i // 64 <= j // 64
    for g, w in enumerate(WINDOWS):
        at = CCOL["invcnt"] + g * PADT
        cst[:, at:at + PADT] = f32(1) / _np.minimum(_np.arange(1, PADT + 1), w).astype(f32)
    cst[0:32, CCOL["buckets"]:CCOL["buckets"] + P] = _np.arange(32)[:, None] == _t5_buckets()[::-1][None, :]
    a["cst"] = cst
    a["rel_bias"] = x["rel_bias"]
    rw = _np.concatenate([x["router_gw_2"][0], x["router_ew_2"][0]], axis=1)
    a["rw"] = rw.reshape(KD, P, -1).transpose(1, 0, 2)
    a["sgw"] = x["sgu_w_2"][0].transpose(2, 0, 1)

    a["w_pool"] = x["pool_w"][0].reshape(4, 2, P, 256).transpose(2, 0, 1, 3).reshape(1, P, 2048)
    for l in range(2):
        gu = x["w_gate_up"][l].reshape(KD, P, 2, NF // 2, 2, P)
        a[f"w_gu{l}"] = gu.transpose(3, 1, 4, 0, 2, 5).reshape(NF // 2, P, 4096)
        dn = x["w_down"][l].reshape(NF, P, KD, P)
        a[f"w_dn{l}"] = dn.transpose(2, 1, 0, 3).reshape(KD, P, FF)
    wk = x["w_k"]
    kv = _np.concatenate([wk[:, 0:HD], wk[:, 0:HD], wk[:, HD:], wk[:, HD:], x["w_v"]], axis=1)
    a["w_kv"] = kv.reshape(KD, P, 384).transpose(1, 0, 2).reshape(1, P, 3072)
    a["w_q"] = _pieces(x["w_q"][0], 256)
    a["w_o"] = _pieces(x["w_o"][0], 256)
    a["w_ple"] = _pieces(x["ple_gate_w_2"][0], 256)
    w = x["w_in_2"][0]
    at, part = 0, {}
    for name, n in (("qa", SB_W), ("ka", SB_W), ("va", SB_W), ("qb", 384), ("kb", 384), ("vb", 384), ("ob", 384),
                    ("i", ML_H), ("f", ML_H), ("uc", SG_W), ("vc", SG_W)):
        part[name] = w[:, at:at + n]
        at += n

    def pad(*cols):
        c = _np.concatenate(cols, axis=1)
        return _np.concatenate([c, _np.zeros((D, 256 - c.shape[1]), f32)], axis=1)

    ob = part["ob"]
    z = [part["uc"], part["vc"], part["qa"][:, 0:256], pad(part["qa"][:, 256:], part["ka"][:, 0:128]), part["ka"][:, 128:],
         part["va"][:, 0:256], pad(part["va"][:, 256:], part["vb"][:, 0:128]),
         pad(part["i"], ob[:, 192:288], part["f"], ob[:, 288:384])]
    z += [pad(part[n][:, s:s + 192]) for n in ("qb", "kb") for s in (0, 192)]
    z += [part["vb"][:, 128:], pad(ob[:, 0:192])]
    a["w_z"] = _pieces(_np.concatenate(z, axis=1), 256)
    wo = x["w_out_2"][0]
    chunks = [wo[c * P:(c + 1) * P] for c in range(SB_C)]
    chunks += [wo[768 + c * P:768 + (c + 1) * P] for c in range(2)]
    chunks += [_np.concatenate([wo[SB_W + h * ML_D:SB_W + (h + 1) * ML_D], _np.zeros((P - ML_D, D), f32)]) for h in range(ML_H)]
    a["w_out"] = _np.stack(chunks).reshape(9, P, 4, 2, P).transpose(2, 1, 3, 0, 4).reshape(4, P, 2304)
    pj = x["ple_proj_w_2"][0].reshape(2, P, D).transpose(1, 0, 2).reshape(P, 2048)
    pT = x["p_2"][0, 0].T.reshape(2, P, SEQ).transpose(1, 0, 2).reshape(P, 512)
    a["w_proj"] = _np.concatenate([pj, pT], axis=1)[None]
    gu = _np.concatenate([x["w_gate_2"][0], x["w_up_2"][0]], axis=2)
    gu = gu.reshape(NE, KD, P, 512).transpose(0, 2, 1, 3).reshape(NE, P, 4096)
    dn = x["w_down_2"][0].reshape(NE, 2, P, D).transpose(0, 2, 1, 3).reshape(NE, P, 2048)
    a["w_eg"], a["w_ed"] = gu, dn

    nc = _bacc.Bacc("TRN2", target_bir_lowering=False, num_devices=1)
    arrays, args = {}, {}
    for name, v in a.items():
        v = _np.ascontiguousarray(v)
        arrays[f"in_{name}"] = v
        args[name] = nc.dram_tensor(f"in_{name}", v.shape, _mybir.dt.from_np(v.dtype), kind="ExternalInput").ap()
    out = nc.dram_tensor("out_y", (P, KD, SEQ), _mybir.dt.float32, kind="ExternalOutput").ap()
    bass_two_blocks(nc, args, out)
    got = _run(nc, [arrays], core_ids=[0]).results[0]["out_y"]
    return got.transpose(2, 1, 0).reshape(1, SEQ, D)
```
